# Optimizing a Trainium2 kernel written in Bass

```python
import jax, jax.numpy as jnp
from jax import lax
import numpy as np

D_MODEL = 1024
BATCH = 1
SEQ = 512
DEPTH = 2

N_A = DEPTH // 2
N_B = DEPTH - N_A
D_FF = 2816
NORM_EPS = 1e-6

RW_HEAD_DIM = 64
RW_HEADS = D_MODEL // RW_HEAD_DIM
LORA_DECAY = 64
LORA_ICLR = 64
LORA_GATE = 160
RW_GN_EPS = 64e-5

NSA_HEADS = 16
NSA_GROUPS = 4
HEADS_PER_GROUP = NSA_HEADS // NSA_GROUPS
HEAD_DIM = D_MODEL // NSA_HEADS
L_CMP = 32
D_CMP = 16
L_SEL = 64
N_SEL = 16
WINDOW = 512
CMP_HIDDEN = 256
Q_BLK = 32
ROPE_THETA = 10000.0
FORCE_SCORE = 1e6
NEG_INF = -1e30

kernel_name = 'rwkv7_nsa_yoco_macaron'

def rmsnorm(x, g):
    x32 = x.astype(jnp.float32)
    y = x32 * lax.rsqrt(jnp.mean(x32 * x32, axis=-1, keepdims=True) + NORM_EPS)
    return y.astype(x.dtype) * g

def swiglu(x, w_gate, w_up, w_down):
    return (jax.nn.silu(x @ w_gate) * (x @ w_up)) @ w_down

def rope(x, pos):
    half = x.shape[-1] // 2
    inv = ROPE_THETA ** (-jnp.arange(half, dtype=jnp.float32) / half)
    ang = pos.astype(jnp.float32)[:, None] * inv[None, :]
    cos = jnp.cos(ang)[None, :, None, :].astype(x.dtype)
    sin = jnp.sin(ang)[None, :, None, :].astype(x.dtype)
    x1, x2 = x[..., :half], x[..., half:]
    return jnp.concatenate([x1 * cos - x2 * sin, x2 * cos + x1 * sin], axis=-1)

def masked_softmax(logits, mask):
    p = jax.nn.softmax(jnp.where(mask, logits.astype(jnp.float32), NEG_INF), axis=-1)
    return jnp.where(mask, p, 0.0)

def rwkv7_time_mix(x, mu, w_rkv, w0, w_lora_a, w_lora_b, a0, a_lora_a, a_lora_b,
                   g_lora_a, g_lora_b, k_k, k_a, r_k, gn_w, gn_b, w_o):
    B, S, D = x.shape
    H, N = RW_HEADS, RW_HEAD_DIM
    xx = jnp.pad(x, ((0, 0), (1, 0), (0, 0)))[:, :-1] - x
    x_r, x_w, x_k, x_v, x_a, x_g = [x + xx * mu[i] for i in range(6)]
    rkv = jnp.einsum('cbsd,cde->cbse', jnp.stack([x_r, x_k, x_v]), w_rkv)
    r, k, v = rkv[0], rkv[1], rkv[2]
    w = -jax.nn.softplus(-(w0 + jnp.tanh(x_w @ w_lora_a) @ w_lora_b)) - 0.5
    decay = jnp.exp(-jnp.exp(w.astype(jnp.float32)))
    a = jax.nn.sigmoid(a0 + (x_a @ a_lora_a) @ a_lora_b)
    g = jax.nn.sigmoid(x_g @ g_lora_a) @ g_lora_b
    kk = (k * k_k).reshape(B, S, H, N).astype(jnp.float32)
    kk = kk / jnp.maximum(jnp.sqrt(jnp.sum(kk * kk, axis=-1, keepdims=True)), 1e-12)
    k = k * (1.0 + (a - 1.0) * k_a)
    heads = lambda t: t.reshape(B, S, H, N)
    r, k, v, a, decay = heads(r), heads(k), heads(v), heads(a), heads(decay)

    def step(state, inp):
        r_t, w_t, k_t, v_t, kk_t, a_t = inp
        sa = jnp.einsum('bhij,bhj->bhi', state, -kk_t)
        state = (state * w_t[:, :, None, :]
                 + sa[..., None] * (kk_t * a_t)[:, :, None, :]
                 + v_t[..., :, None] * k_t[..., None, :])
        return state, jnp.einsum('bhij,bhj->bhi', state, r_t)

    seq_first = lambda t: jnp.moveaxis(t.astype(jnp.float32), 1, 0)
    state0 = jnp.zeros((B, H, N, N), jnp.float32)
    _, y = lax.scan(step, state0, (seq_first(r), seq_first(decay), seq_first(k),
                                    seq_first(v), seq_first(kk), seq_first(a)))
    y = jnp.moveaxis(y, 0, 1)
    mean = jnp.mean(y, axis=-1, keepdims=True)
    var = jnp.mean((y - mean) ** 2, axis=-1, keepdims=True)
    y = ((y - mean) * lax.rsqrt(var + RW_GN_EPS)).reshape(B, S, D).astype(x.dtype) * gn_w + gn_b
    bonus = jnp.sum(r * k * r_k, axis=-1, keepdims=True) * v
    y = y + bonus.reshape(B, S, D)
    return (y * g) @ w_o

def nsa_shared_kv(x, kv_norm, kv_w, kv_k_norm, cmp_pos_k, cmp_k_w1, cmp_k_w2,
                  cmp_pos_v, cmp_v_w1, cmp_v_w2):
    B, S, _ = x.shape
    G, dh = NSA_GROUPS, HEAD_DIM
    h = rmsnorm(x, kv_norm)
    kv = (h @ kv_w).reshape(B, S, 6, G, dh)
    k_cmp_tok, v_cmp_tok, k_sel, v_sel, k_win, v_win = [kv[:, :, i] for i in range(6)]
    pos = jnp.arange(S)
    k_sel = rope(rmsnorm(k_sel, kv_k_norm[1]), pos)
    k_win = rope(rmsnorm(k_win, kv_k_norm[2]), pos)
    n_cmp = (S - L_CMP) // D_CMP + 1
    idx = jnp.arange(n_cmp)[:, None] * D_CMP + jnp.arange(L_CMP)[None, :]

    def compress(tok, pos_emb, w1, w2):
        blocks = tok[:, idx] + pos_emb[:, None, :]
        blocks = jnp.moveaxis(blocks, 3, 2).reshape(B, n_cmp, G, L_CMP * dh)
        return jax.nn.gelu(blocks @ w1) @ w2

    k_cmp = rmsnorm(compress(k_cmp_tok, cmp_pos_k, cmp_k_w1, cmp_k_w2), kv_k_norm[0])
    v_cmp = compress(v_cmp_tok, cmp_pos_v, cmp_v_w1, cmp_v_w2)
    return k_cmp, v_cmp, k_sel, v_sel, k_win, v_win

def nsa_attention(h, shared, w_q, q_norm, w_o):
    k_cmp, v_cmp, k_sel, v_sel, k_win, v_win = shared
    B, S, _ = h.shape
    H, G, HPG, dh = NSA_HEADS, NSA_GROUPS, HEADS_PER_GROUP, HEAD_DIM
    qg = h @ w_q
    q = rmsnorm(qg[..., :H * dh].reshape(B, S, H, dh), q_norm)
    q_rot = rope(q, jnp.arange(S))
    gates = jax.nn.sigmoid(qg[..., H * dh:].reshape(B, S, H, 3))
    n_blk = S // Q_BLK
    nsel = S // L_SEL
    n_top = min(N_SEL, nsel)
    n_cmp = k_cmp.shape[1]
    scale = dh ** -0.5
    lpad = L_CMP // D_CMP - 1
    stride = L_SEL // D_CMP
    span = stride + lpad
    lim = stride * (nsel - 1) + 1
    rpad = stride * (nsel - 1) + span - lpad - n_cmp
    kb_sel = jnp.transpose(k_sel.reshape(B, nsel, L_SEL, G, dh), (0, 3, 1, 2, 4))
    vb_sel = jnp.transpose(v_sel.reshape(B, nsel, L_SEL, G, dh), (0, 3, 1, 2, 4))
    k_win_pad = jnp.pad(k_win, ((0, 0), (WINDOW, 0), (0, 0), (0, 0)))
    v_win_pad = jnp.pad(v_win, ((0, 0), (WINDOW, 0), (0, 0), (0, 0)))
    cmp_end = jnp.arange(n_cmp) * D_CMP + L_CMP - 1
    blk = jnp.arange(nsel)
    bi = jnp.arange(B)[:, None, None, None]
    gi = jnp.arange(G)[None, None, :, None]

    def to_blocks(t):
        return jnp.moveaxis(t.reshape(B, n_blk, Q_BLK, G, HPG, t.shape[-1]), 1, 0)

    def attend(args):
        qc, qrc, gc, ci = args
        s0 = ci * Q_BLK
        t = s0 + jnp.arange(Q_BLK)
        lc = jnp.einsum('bqghd,bngd->bqghn', qc, k_cmp) * scale
        p_cmp = masked_softmax(lc, (cmp_end[None, :] <= t[:, None])[None, :, None, None, :])
        o_cmp = jnp.einsum('bqghn,bngd->bqghd', p_cmp.astype(v_cmp.dtype), v_cmp)
        imp = jnp.pad(jnp.sum(p_cmp, axis=3), ((0, 0), (0, 0), (0, 0), (lpad, rpad)))
        p_slc = imp[..., 0:lim:stride]
        for o in range(1, span):
            p_slc = p_slc + imp[..., o:o + lim:stride]
        cur = t // L_SEL
        forced = (blk[None, :] == 0) | (blk[None, :] == cur[:, None]) | (blk[None, :] == cur[:, None] - 1)
        future = blk[None, :] * L_SEL > t[:, None]
        score = jnp.where(forced[None, :, None, :], FORCE_SCORE, p_slc)
        score = jnp.where(future[None, :, None, :], -1.0, score)
        _, sel = lax.top_k(score, n_top)
        kg = kb_sel[bi, gi, sel].reshape(B, Q_BLK, G, n_top * L_SEL, dh)
        vg = vb_sel[bi, gi, sel].reshape(B, Q_BLK, G, n_top * L_SEL, dh)
        tok = (sel[..., None] * L_SEL + jnp.arange(L_SEL)).reshape(B, Q_BLK, G, n_top * L_SEL)
        ls = jnp.einsum('bqghd,bqgkd->bqghk', qrc, kg) * scale
        p_sel = masked_softmax(ls, (tok <= t[None, :, None, None])[:, :, :, None, :])
        o_sel = jnp.einsum('bqghk,bqgkd->bqghd', p_sel.astype(vg.dtype), vg)
        kw = lax.dynamic_slice_in_dim(k_win_pad, s0, WINDOW + Q_BLK, axis=1)
        vw = lax.dynamic_slice_in_dim(v_win_pad, s0, WINDOW + Q_BLK, axis=1)
        kpos = s0 - WINDOW + jnp.arange(WINDOW + Q_BLK)
        mw = (kpos[None, :] <= t[:, None]) & (kpos[None, :] > t[:, None] - WINDOW) & (kpos[None, :] >= 0)
        lw = jnp.einsum('bqghd,bkgd->bqghk', qrc, kw) * scale
        p_win = masked_softmax(lw, mw[None, :, None, None, :])
        o_win = jnp.einsum('bqghk,bkgd->bqghd', p_win.astype(vw.dtype), vw)
        return gc[..., 0:1] * o_cmp + gc[..., 1:2] * o_sel + gc[..., 2:3] * o_win

    o = lax.map(attend, (to_blocks(q), to_blocks(q_rot), to_blocks(gates), jnp.arange(n_blk)))
    o = jnp.moveaxis(o, 0, 1).reshape(B, S, H * dh)
    return o @ w_o

def setup_inputs(seed: int = 0) -> dict:
    key = jax.random.key(seed)
    ks = iter(jax.random.split(key, 64))
    nrm = lambda shape, s: jax.random.normal(next(ks), shape, jnp.float32) * s
    uni = lambda shape, lo, hi: jax.random.uniform(next(ks), shape, jnp.float32, lo, hi)
    D, H, dh, G = D_MODEL, NSA_HEADS, HEAD_DIM, NSA_GROUPS
    return {
        'x': nrm((BATCH, SEQ, D), 1.0),
        'norm_ffn1': 1.0 + nrm((DEPTH, D), 0.02),
        'ffn1_w_gate': nrm((DEPTH, D, D_FF), D ** -0.5),
        'ffn1_w_up': nrm((DEPTH, D, D_FF), D ** -0.5),
        'ffn1_w_down': nrm((DEPTH, D_FF, D), D_FF ** -0.5),
        'norm_mix': 1.0 + nrm((DEPTH, D), 0.02),
        'norm_ffn2': 1.0 + nrm((DEPTH, D), 0.02),
        'ffn2_w_gate': nrm((DEPTH, D, D_FF), D ** -0.5),
        'ffn2_w_up': nrm((DEPTH, D, D_FF), D ** -0.5),
        'ffn2_w_down': nrm((DEPTH, D_FF, D), D_FF ** -0.5),
        'rw_mu': uni((N_A, 6, D), 0.0, 1.0),
        'rw_w_rkv': nrm((N_A, 3, D, D), D ** -0.5),
        'rw_w0': uni((N_A, D), -5.0, 1.0),
        'rw_w_lora_a': nrm((N_A, D, LORA_DECAY), D ** -0.5),
        'rw_w_lora_b': nrm((N_A, LORA_DECAY, D), 0.1 * LORA_DECAY ** -0.5),
        'rw_a0': nrm((N_A, D), 0.1),
        'rw_a_lora_a': nrm((N_A, D, LORA_ICLR), D ** -0.5),
        'rw_a_lora_b': nrm((N_A, LORA_ICLR, D), 0.5 * LORA_ICLR ** -0.5),
        'rw_g_lora_a': nrm((N_A, D, LORA_GATE), D ** -0.5),
        'rw_g_lora_b': nrm((N_A, LORA_GATE, D), LORA_GATE ** -0.5),
        'rw_k_k': 0.85 + nrm((N_A, D), 0.05),
        'rw_k_a': 1.0 + nrm((N_A, D), 0.05),
        'rw_r_k': nrm((N_A, RW_HEADS, RW_HEAD_DIM), 0.1),
        'rw_gn_w': 1.0 + nrm((N_A, D), 0.02),
        'rw_gn_b': nrm((N_A, D), 0.02),
        'rw_w_o': nrm((N_A, D, D), D ** -0.5),
        'kv_norm': 1.0 + nrm((D,), 0.02),
        'kv_w': nrm((D, 6 * G * dh), D ** -0.5),
        'kv_k_norm': 1.0 + nrm((3, dh), 0.02),
        'cmp_pos_k': nrm((L_CMP, dh), 0.5),
        'cmp_k_w1': nrm((L_CMP * dh, CMP_HIDDEN), (L_CMP * dh) ** -0.5),
        'cmp_k_w2': nrm((CMP_HIDDEN, dh), CMP_HIDDEN ** -0.5),
        'cmp_pos_v': nrm((L_CMP, dh), 0.5),
        'cmp_v_w1': nrm((L_CMP * dh, CMP_HIDDEN), (L_CMP * dh) ** -0.5),
        'cmp_v_w2': nrm((CMP_HIDDEN, dh), CMP_HIDDEN ** -0.5),
        'nsa_w_q': nrm((N_B, D, H * dh + 3 * H), D ** -0.5),
        'nsa_q_norm': 1.0 + nrm((N_B, dh), 0.02),
        'nsa_w_o': nrm((N_B, H * dh, D), (H * dh) ** -0.5),
    }

def reference(x, norm_ffn1, ffn1_w_gate, ffn1_w_up, ffn1_w_down, norm_mix, norm_ffn2,
              ffn2_w_gate, ffn2_w_up, ffn2_w_down, rw_mu, rw_w_rkv, rw_w0, rw_w_lora_a,
              rw_w_lora_b, rw_a0, rw_a_lora_a, rw_a_lora_b, rw_g_lora_a, rw_g_lora_b,
              rw_k_k, rw_k_a, rw_r_k, rw_gn_w, rw_gn_b, rw_w_o, kv_norm, kv_w, kv_k_norm,
              cmp_pos_k, cmp_k_w1, cmp_k_w2, cmp_pos_v, cmp_v_w1, cmp_v_w2,
              nsa_w_q, nsa_q_norm, nsa_w_o):
    shared = None
    for l in range(DEPTH):
        x = x + 0.5 * swiglu(rmsnorm(x, norm_ffn1[l]), ffn1_w_gate[l], ffn1_w_up[l], ffn1_w_down[l])
        h = rmsnorm(x, norm_mix[l])
        if l < N_A:
            i = l
            x = x + rwkv7_time_mix(h, rw_mu[i], rw_w_rkv[i], rw_w0[i], rw_w_lora_a[i], rw_w_lora_b[i],
                                   rw_a0[i], rw_a_lora_a[i], rw_a_lora_b[i], rw_g_lora_a[i],
                                   rw_g_lora_b[i], rw_k_k[i], rw_k_a[i], rw_r_k[i], rw_gn_w[i],
                                   rw_gn_b[i], rw_w_o[i])
        else:
            i = l - N_A
            x = x + nsa_attention(h, shared, nsa_w_q[i], nsa_q_norm[i], nsa_w_o[i])
        x = x + 0.5 * swiglu(rmsnorm(x, norm_ffn2[l]), ffn2_w_gate[l], ffn2_w_up[l], ffn2_w_down[l])
        if l == N_A - 1:
            shared = nsa_shared_kv(x, kv_norm, kv_w, kv_k_norm, cmp_pos_k, cmp_k_w1, cmp_k_w2,
                                   cmp_pos_v, cmp_v_w1, cmp_v_w2)
    return x


_drawn_inputs = setup_inputs


def setup_inputs(seed=0):
    import zlib

    import numpy as np

    out = dict(_drawn_inputs(seed))
    spreads = {}
    factors = {'norm_ffn1': 4.227,
     'norm_mix': 2.701,
     'norm_ffn2': 5.664,
     'rw_w_lora_a': 8.0,
     'rw_w_lora_b': 8.0,
     'rw_k_k': 3.475,
     'rw_gn_w': 5.846,
     'rw_gn_b': 5.019,
     'kv_norm': 8.0,
     'kv_k_norm': 8.0,
     'nsa_q_norm': 8.0,
     'cmp_pos_v': 4.232}
    for name, (base, spread) in spreads.items():
        noise = np.random.default_rng([zlib.crc32(name.encode()), seed]).standard_normal(out[name].shape)
        drawn = base * np.exp(spread * noise) if base else spread * noise
        out[name] = __import__('jax').numpy.asarray(drawn.astype(out[name].dtype))
    for name, factor in factors.items():
        out[name] = (out[name] * factor).astype(out[name].dtype)
    return out
```

```python
from contextlib import ExitStack

import numpy as np

import concourse.bass as bass
from concourse import mybir

ALU = mybir.AluOpType
ACT = mybir.ActivationFunctionType
AX = mybir.AxisListType
F32 = mybir.dt.float32
F32R = mybir.dt.float32r

P = 128
T = 512
D = 1024
ND = D // P
F = 2816
NF = F // P
KMAX = 8
SLOTS = 4
EPS = 1e-6
GN_EPS = 64e-5


def fp(view):
    return view.bitcast(F32)


VECTORS = ["norm_ffn1", "norm_mix", "norm_ffn2", "kv_norm", "rw_mu", "rw_w0", "rw_a0", "rw_k_k", "rw_k_a",
           "rw_r_k", "rw_gn_w", "rw_gn_b"]


class Core:

    def __init__(self, nc, ctx, ins, consts):
        self.nc, self.ins, self.consts = nc, ins, consts
        sb = lambda name, shape, dt=F32: ctx.enter_context(nc.sbuf_tensor(name, shape, dt))
        self.x = sb("x_res", [P, ND, T])
        self.ones = sb("ones", [P, P])
        self.head_ones = sb("head_ones", [P, P])
        self.ident = sb("ident", [P, P])
        self.eps = sb("eps", [P, 2])
        self.row, n = {}, 0
        for name in VECTORS:
            self.row[name] = n
            n += int(np.prod(ins[name].shape)) // P
        self.rows = n
        self.vecs = sb("vecs", [P, n])
        self.zero = sb("zero", [P, 1])

    def vec(self, name, index=0):
        r = self.row[name] + ND * index
        return self.vecs[:, r:r + ND]


def open_ring(core, sb):
    core.raw = sb("w_raw", [P, SLOTS, KMAX, P])
    core.whi = sb("w_hi", [P, SLOTS, KMAX, P], F32R)
    core.wlo = sb("w_lo", [P, SLOTS, KMAX, P], F32R)


def open_stage(core, ctx, tag, names):
    nc = core.nc
    s = {n: nc.alloc_semaphore(f"{n}_{tag}") for n in names}
    sb = lambda name, shape, dt=F32: ctx.enter_context(nc.sbuf_tensor(f"{name}_{tag}", shape, dt))
    ps = lambda name, shape: ctx.enter_context(nc.psum_tensor(f"{name}_{tag}", shape, F32))
    return s, sb, ps


def close_stage(core, s):
    nc = core.nc
    with nc.Block() as block:
        @block.sync
        def _(sp):
            for sem in s.values():
                sp.sem_clear(sem)
    for sem in s.values():
        nc.release_semaphore(sem)


def one(i):
    return bass.ds(i, 1)


def flat(view):
    return view.rearrange("p a t -> p (a t)")


def done(unit):
    return unit + (SLOTS + 1)


def load_unit(sp, s, core, slot, count, source):
    sp.wait_ge(s["w_ready"], count + 1)
    k = source.shape[1]
    sp.dma_start(core.raw[:, slot, 0:k, 0:source.shape[2]], source).then_inc(s[f"raw{slot}"], 16)


def split_unit(dve, s, core, slot, rounds, count, k, m=P):
    nc = core.nc
    dve.wait_ge(s[f"raw{slot}"], 16 * rounds + 16)
    dve.wait_ge(s["w_free"], count + 1)
    raw, hi, lo = (t[:, slot, 0:k, 0:m] for t in (core.raw, core.whi, core.wlo))
    nc.vector.tensor_copy(hi, raw).then_inc(s["w_hi"], 1)
    dve.wait_ge(s["w_hi"], count + 1)
    nc.vector.tensor_tensor(lo, raw, fp(hi), ALU.subtract).then_inc(s["w_ready"], 1)


def three_passes(core, out, slot, k, hi, lo, first, last):
    nc = core.nc
    whi, wlo = core.whi[:, slot, k], core.wlo[:, slot, k]
    nc.tensor.matmul(out, whi, hi, start=first, stop=False)
    nc.tensor.matmul(out, whi, lo, start=False, stop=False)
    return nc.tensor.matmul(out, wlo, hi, start=False, stop=last)


FFN_SEMS = ["raw0", "raw1", "raw2", "raw3", "w_free", "w_hi", "w_ready", "rstd", "h_lo", "h_hi", "h32", "sq",
            "sq_used", "ms", "gu_free", "down_free", "a_lo", "a_hi", "act32", "silu", "half_free", "ready"]


def ffn(core, tag, x_gain, w_gate, w_up, w_down):
    nc = core.nc
    groups = [(f0, min(KMAX, NF - f0)) for f0 in range(0, NF, KMAX)]
    gate = w_gate.rearrange("(k p) f -> p k f", p=P)
    up = w_up.rearrange("(k p) f -> p k f", p=P)
    down = w_down.rearrange("(k p) d -> p k d", p=P)
    with ExitStack() as ctx:
        s, sb, ps = open_stage(core, ctx, tag, FFN_SEMS)
        open_ring(core, sb)
        sq = sb("sq", [P, 2, T])
        ms = sb("ms", [P, T])
        rstd = sb("rstd", [P, T])
        h32 = sb("h32", [P, 2, T])
        hhi = sb("hhi", [P, ND, T], F32R)
        hlo = sb("hlo", [P, ND, T], F32R)
        gated = sb("gated", [P, T])
        upc = sb("upc", [P, T])
        act32 = sb("act32", [P, T])
        ahi = sb("ahi", [P, KMAX, T], F32R)
        alo = sb("alo", [P, KMAX, T], F32R)
        half = sb("half", [P, 2, T])
        p_gate = ps("p_gate", [P, 2, T])
        p_up = ps("p_up", [P, 2, T])
        p_down = ps("p_down", [P, 2, T])
        p_ms = ps("p_ms", [P, T])
        block = ctx.enter_context(nc.Block())

        @block.sync
        def _(sp):
            unit = 0
            for f0, nf in groups:
                with sp.Fori(0, nf // 2) as i:
                    for j in range(4):
                        w = gate if j % 2 == 0 else up
                        src = w[:, :, bass.ds(2 * P * i + (f0 + j // 2) * P, P)]
                        load_unit(sp, s, core, j, 4 * i + (unit + j), src)
                unit += 2 * nf
                with sp.Fori(0, ND // 4) as i:
                    for j in range(4):
                        src = down[:, f0:f0 + nf, bass.ds(4 * P * i + j * P, P)]
                        load_unit(sp, s, core, j, 4 * i + (unit + j), src)
                unit += ND

        @block.vector
        def _(dve):
            dve.sem_inc(s["w_ready"], SLOTS)
            norm_vector(core, dve, s, x_gain, ms, rstd, h32, hhi, hlo)
            unit = 0
            for f0, nf in groups:
                with dve.Fori(0, nf // 2) as i:
                    for j in range(4):
                        split_unit(dve, s, core, j, i + unit // 4, 4 * i + (unit + j), ND)
                unit += 2 * nf
                with dve.Fori(0, ND // 4) as i:
                    for j in range(4):
                        split_unit(dve, s, core, j, i + unit // 4, 4 * i + (unit + j), nf)
                unit += ND

        @block.tensor
        def _(pe):
            pe.sem_inc(s["w_free"], SLOTS)
            norm_tensor(core, pe, s, sq, p_ms)
            pe.wait_ge(s["h_lo"], ND)
            unit, ftile, dtile = 0, 0, 0
            for f0, nf in groups:
                with pe.Fori(0, nf // 2) as i:
                    for j in range(4):
                        out = (p_gate if j % 2 == 0 else p_up)[:, j // 2]
                        pe.wait_ge(s["w_ready"], done(4 * i + (unit + j)))
                        if j % 2 == 0:
                            pe.wait_ge(s["gu_free"], 2 * i + (ftile + j // 2 + 1))
                        for k in range(ND):
                            mm = three_passes(core, out, j, k, hhi[:, k], hlo[:, k], k == 0, k == ND - 1)
                        mm.then_inc(s["w_free"], 1)
                unit += 2 * nf
                ftile += nf
                with pe.Fori(0, ND // 4) as i:
                    for j in range(4):
                        out = p_down[:, j % 2]
                        pe.wait_ge(s["w_ready"], done(4 * i + (unit + j)))
                        pe.wait_ge(s["down_free"], 4 * i + (dtile + j + 1))
                        for k in range(nf):
                            if j == 0:
                                pe.wait_ge(s["a_lo"], f0 + k + 2)
                            mm = three_passes(core, out, j, k, ahi[:, k], alo[:, k], k == 0, k == nf - 1)
                        mm.then_inc(s["w_free"], 1)
                unit += ND
                dtile += ND

        @block.scalar
        def _(act):
            norm_scalar(core, act, s, sq, p_ms, ms, h32, hhi)
            act.sem_inc(s["gu_free"], 2)
            act.sem_inc(s["down_free"], 2)
            unit, ftile, dtile = 0, 0, 0
            for f0, nf in groups:
                with act.Fori(0, nf // 2) as i:
                    for j in range(2):
                        f = 2 * i + (ftile + j)
                        act.wait_ge(s["w_free"], done(4 * i + (unit + 2 * j + 1)))
                        act.wait_ge(s["act32"], f + 1)
                        nc.scalar.activation(gated[:], p_gate[:, j], ACT.Silu).then_inc(s["silu"], 1)
                        act.wait_ge(s["silu"], f + 1)
                        nc.scalar.activation(upc[:], p_up[:, j], ACT.Copy).then_inc(s["gu_free"], 1)
                        act.wait_ge(s["act32"], f + 2)
                        act.wait_ge(s["ready"], 1)
                        nc.scalar.activation(ahi[:, bass.ds(2 * i + j, 1)].rearrange("p a t -> p (a t)"), act32[:], ACT.Copy).then_inc(s["a_hi"], 1)
                unit += 2 * nf
                ftile += nf
                with act.Fori(0, ND // 4) as i:
                    for j in range(4):
                        act.wait_ge(s["w_free"], done(4 * i + (unit + j)))
                        act.wait_ge(s["half_free"], 4 * i + (dtile + j + 1))
                        nc.scalar.activation(half[:, j % 2], p_down[:, j % 2], ACT.Copy, scale=0.5).then_inc(s["down_free"], 1)
                unit += ND
                dtile += ND

        @block.gpsimd
        def _(pool):
            pool.sem_inc(s["act32"], 1)
            pool.sem_inc(s["a_lo"], 1)
            pool.sem_inc(s["half_free"], 2)
            pool.sem_inc(s["ready"], 1)
            ftile, dtile = 0, 0
            for f0, nf in groups:
                with pool.Fori(0, nf // 2) as i:
                    for j in range(2):
                        f = 2 * i + (ftile + j)
                        pool.wait_ge(s["gu_free"], f + 3)
                        pool.wait_ge(s["a_lo"], f + 1)
                        nc.gpsimd.tensor_tensor(act32[:], gated[:], upc[:], ALU.mult).then_inc(s["act32"], 1)
                        pool.wait_ge(s["a_hi"], f + 1)
                        pool.wait_ge(s["ready"], 1)
                        sl = bass.ds(2 * i + j, 1)
                        nc.gpsimd.tensor_tensor(alo[:, sl].rearrange("p a t -> p (a t)"), act32[:],
                                                fp(ahi[:, sl]).rearrange("p a t -> p (a t)"), ALU.subtract).then_inc(s["a_lo"], 1)
                ftile += nf
                with pool.Fori(0, ND // 4) as i:
                    for j in range(4):
                        pool.wait_ge(s["down_free"], 4 * i + (dtile + j + 3))
                        pool.wait_ge(s["ready"], 1)
                        xs = core.x[:, bass.ds(4 * i + j, 1)].rearrange("p a t -> p (a t)")
                        nc.gpsimd.tensor_tensor(xs, xs, half[:, j % 2], ALU.add).then_inc(s["half_free"], 1)
                dtile += ND
            pool.wait_ge(s["half_free"], 2 + dtile)
    close_stage(core, s)


PASSES = [("r", 0, ND), ("lw", 1, 1), ("k", 2, ND), ("la", 4, 1), ("v", 3, ND), ("lg", 5, 2)]
MAIN = ("r", "k", "v")

MIX_SEMS = ["raw0", "raw1", "raw2", "raw3", "w_free", "w_hi", "w_ready", "rstd", "h", "sq", "sq_used", "ms",
            "dx", "mix32", "mix_hi", "mix_lo", "out", "st0", "st1", "st2", "st3", "ready", "pad"]


def mix_project(core, tag, rkv, lora):
    nc, ins = core.nc, core.ins
    wide = [ins["rw_w_rkv"][0, c].rearrange("(k p) e -> p k e", p=P) for c in range(3)]
    narrow = {"lw": ins["rw_w_lora_a"][0], "la": ins["rw_a_lora_a"][0], "lg": ins["rw_g_lora_a"][0]}
    widths = {"lw": [narrow["lw"].shape[1]], "la": [narrow["la"].shape[1]], "lg": [P, narrow["lg"].shape[1] - P]}
    first, n = {}, 0
    for name, _, units in PASSES:
        first[name] = n
        n += units
    buf = {"r": 0, "lw": 1, "k": 2, "la": 1, "v": 0, "lg": 1}
    beside = {"r": ["lw", "k"], "k": ["la", "v"], "v": ["lg"]}
    began = {"r": ND, "k": 3 * ND, "v": 5 * ND}
    complete = {"lw": 3 * ND - 1, "k": 3 * ND, "la": 5 * ND - 1, "v": 5 * ND, "lg": 6 * ND}
    mu_row = {name: c for name, c, _ in PASSES}

    with ExitStack() as ctx:
        s, sb, ps = open_stage(core, ctx, tag, MIX_SEMS)
        open_ring(core, sb)
        h = sb("h", [P, ND, T + 1])
        dx = sb("dx", [P, 2, T])
        mix32 = sb("mix32", [P, 4, T])
        sq, ms, rstd = mix32[:, 0:2], dx[:, 0], dx[:, 1]
        mhi = sb("mhi", [P, 3, ND, T], F32R)
        mlo = sb("mlo", [P, 3, ND, T], F32R)
        staged = sb("staged", [P, 2, T])
        p_ms = ps("p_ms", [P, T])
        p_out = ps("p_out", [P, 4, T])
        block = ctx.enter_context(nc.Block())

        def units_of(eng, name, body):
            base, n = first[name], dict((a, c) for a, _, c in PASSES)[name]
            if name in MAIN:
                with eng.Fori(0, n // 4) as i:
                    for j in range(4):
                        body(4 * i + (base + j), (base + j) % 4, i + (base + j) // 4, 4 * i + j, j)
            else:
                for j in range(n):
                    body(base + j, (base + j) % 4, (base + j) // 4, j, j)

        @block.sync
        def _(sp):
            for name, _, n in PASSES:
                def load(unit, slot, rounds, e, j):
                    if name in MAIN:
                        src = wide[MAIN.index(name)][:, :, bass.ds(e * P, P)]
                    else:
                        m = widths[name][j]
                        src = narrow[name].rearrange("(k p) e -> p k e", p=P)[:, :, j * P:j * P + m]
                    load_unit(sp, s, core, slot, unit, src)
                units_of(sp, name, load)

        @block.vector
        def _(dve):
            dve.sem_inc(s["w_ready"], SLOTS)
            dve.sem_inc(s["ready"], 1)
            nc.vector.memset(h[:, :, 0:1], 0.0).then_inc(s["pad"], 1)
            dve.wait_ge(s["ms"], 1)
            nc.vector.reciprocal(rstd[:], ms[:]).then_inc(s["rstd"], 1)
            dve.wait_ge(s["rstd"], 1)
            gain = core.vec("norm_mix", 0)
            for d in range(ND):
                nc.vector.scalar_tensor_tensor(out=h[:, d, 1:T + 1], in0=core.x[:, d], scalar=gain[:, d:d + 1],
                                               in1=rstd[:], op0=ALU.mult, op1=ALU.mult).then_inc(s["h"], 1)
            dve.wait_ge(s["h"], ND)
            dve.wait_ge(s["pad"], 1)

            def mix_tile(name, m, slot, d):
                mu = core.vec("rw_mu", mu_row[name])
                mu = mu[:, d:d + 1] if isinstance(d, int) else mu[:, one(d)]
                hd = h[:, d:d + 1] if isinstance(d, int) else h[:, one(d)]
                dve.wait_ge(s["mix_hi"], m + 1)
                nc.vector.tensor_tensor(dx[:, slot % 2], flat(hd[:, :, 0:T]), flat(hd[:, :, 1:T + 1]),
                                        ALU.subtract).then_inc(s["dx"], 1)
                dve.wait_ge(s["dx"], m + 1)
                dve.wait_ge(s["mix_lo"], m + 1)
                nc.vector.scalar_tensor_tensor(out=mix32[:, slot], in0=dx[:, slot % 2], scalar=mu,
                                               in1=flat(hd[:, :, 1:T + 1]), op0=ALU.mult, op1=ALU.add).then_inc(s["mix32"], 1)

            for d in range(ND):
                mix_tile("r", d, d % 4, d)
            for name, _, n in PASSES:
                def step(unit, slot, rounds, e, j):
                    m = P if name in MAIN else widths[name][j]
                    split_unit(dve, s, core, slot, rounds, unit, ND, m)
                    for b, other in enumerate(beside.get(name, [])):
                        made = len(beside[name])
                        mix_tile(other, e * made + (began[name] + b), (made * j + b) % 4, e)
                units_of(dve, name, step)

        @block.scalar
        def _(act):
            act.sem_inc(s["mix_hi"], 4)
            act.sem_inc(s["out"], 4)
            for d in range(ND):
                if d >= 2:
                    act.wait_ge(s["sq_used"], d - 1)
                nc.scalar.activation(sq[:, d % 2], core.x[:, d], ACT.Square).then_inc(s["sq"], 1)
            act.wait_ge(s["sq_used"], ND)
            nc.scalar.activation(ms[:], p_ms[:], ACT.Sqrt, scale=1.0 / D, bias=core.eps[:, 0:1]).then_inc(s["ms"], 1)

            def round_tile(name, m, slot, d):
                act.wait_ge(s["mix32"], m + 1)
                act.wait_ge(s["ready"], 1)
                dst = mhi[:, buf[name], d] if isinstance(d, int) else flat(mhi[:, buf[name], one(d)])
                nc.scalar.activation(dst, mix32[:, slot], ACT.Copy).then_inc(s["mix_hi"], 1)

            for d in range(ND):
                round_tile("r", d, d % 4, d)
            for name, _, n in PASSES:
                def step(unit, slot, rounds, e, j):
                    for b, other in enumerate(beside.get(name, [])):
                        made = len(beside[name])
                        round_tile(other, e * made + (began[name] + b), (made * j + b) % 4, e)
                    act.wait_ge(s["w_free"], done(unit))
                    if name in MAIN:
                        before = MAIN.index(name) * ND
                        turn = j % 2
                        act.wait_ge(s[f"st{turn}"], 8 * e + (8 * before - 8 * turn + 16))
                        nc.scalar.activation(staged[:, turn], p_out[:, slot], ACT.Copy).then_inc(s["out"], 1)
                        act.wait_ge(s["out"], unit + 5)
                        dst = rkv[MAIN.index(name)].rearrange("(e p) t -> e p t", p=P)[one(e)].rearrange("a p t -> p (a t)")
                        act.dma_start(dst, staged[:, turn]).then_inc(s[f"st{turn}"], 16)
                    else:
                        m = widths[name][j]
                        func = {"lw": ACT.Tanh, "la": ACT.Copy, "lg": ACT.Sigmoid}[name]
                        nc.scalar.activation(lora[name][0:m, j], p_out[0:m, slot], func).then_inc(s["out"], 1)
                units_of(act, name, step)
            for turn in range(2):
                act.wait_ge(s[f"st{turn}"], 16 * (3 * ND // 2 + 1))

        @block.gpsimd
        def _(pool):
            pool.sem_inc(s["mix_lo"], 4)
            pool.sem_inc(s["st0"], 16)
            pool.sem_inc(s["st1"], 16)

            def low_tile(name, m, slot, d):
                pool.wait_ge(s["mix_hi"], m + 5)
                pool.wait_ge(s["ready"], 1)
                if isinstance(d, int):
                    dst, hi = mlo[:, buf[name], d], fp(mhi[:, buf[name], d])
                else:
                    dst, hi = flat(mlo[:, buf[name], one(d)]), flat(fp(mhi[:, buf[name], one(d)]))
                nc.gpsimd.tensor_tensor(dst, mix32[:, slot], hi, ALU.subtract).then_inc(s["mix_lo"], 1)

            for d in range(ND):
                low_tile("r", d, d % 4, d)
            for name in MAIN:
                def step(unit, slot, rounds, e, j):
                    for b, other in enumerate(beside[name]):
                        made = len(beside[name])
                        low_tile(other, e * made + (began[name] + b), (made * j + b) % 4, e)
                units_of(pool, name, step)

        @block.tensor
        def _(pe):
            pe.sem_inc(s["w_free"], SLOTS)
            for d in range(ND):
                pe.wait_ge(s["sq"], d + 1)
                nc.tensor.matmul(p_ms[:], core.ones[:], sq[:, d % 2], start=(d == 0), stop=(d == ND - 1)).then_inc(s["sq_used"], 1)
            for name, _, n in PASSES:
                if name in complete:
                    pe.wait_ge(s["mix_lo"], complete[name] + 4)
                def step(unit, slot, rounds, e, j):
                    pe.wait_ge(s["w_ready"], done(unit))
                    pe.wait_ge(s["out"], unit + 1)
                    for k in range(ND):
                        if name == "r" and j == 0:
                            pe.wait_ge(s["mix_lo"], k + 5)
                        mm = three_passes(core, p_out[:, slot], slot, k, mhi[:, buf[name], k], mlo[:, buf[name], k],
                                          k == 0, k == ND - 1)
                    mm.then_inc(s["w_free"], 1)
                units_of(pe, name, step)
    close_stage(core, s)


PAIR_EVENTS = {
    "loaded": 16 * 3, "lora_w": 16 * 4, "cur": 1, "zp": 1, "ap": 1, "tw": 1, "ta": 1, "sqk": 1, "ssk": 1, "clip": 1, "lnk": 1,
    "inv": 1, "sg": 1, "cum": 1, "ctr": 1, "qsum": 1, "cc": 1, "ce": 1, "eex": 1, "ep": 1, "em": 1, "q": 1, "pk": 6,
    "tilde": 4, "rk": 1, "bsum": 1, "bon": 1, "gp": 1, "gsb": 1, "vturn": 1, "vtok": 1, "turn": 3, "tok": 3,
    "score": 6, "bl": 4, "kl": 4, "nm": 2, "x_init": 6, "lakv": 1, "aw": 1, "g_mm": 10, "g": 10,
    "x_mm": 10, "x": 10, "au_mm": 2, "au": 2, "rp_mm": 1, "rp": 1, "f_mm": 1, "f": 2, "z_mm": 1, "z": 2,
    "chain": 6, "state": 6, "y_mm": 1, "ysb": 1, "mean": 1, "dev": 1, "sqy": 1, "var": 1, "lny": 1, "rs": 1,
    "yn": 3, "yhi": 1, "pair": 1,
}
C = 64
NC_ = T // C
NT = T // P
KAPPA = float(np.exp(-0.5))
LEVELS = (2, 4, 8, 16, 32)
LN_SCALE = 2.0 ** 16
W0H, A0H, KK, HKA, OKA, RK, GNW, GNB = range(8)


def recurrence(core, tag, rkv, lora, yhi, ylo):
    nc, ins = core.nc, core.ins
    with ExitStack() as ctx:
        s, sb, ps = open_stage(core, ctx, tag, list(PAIR_EVENTS) + ["ready", "consts", "pv"])

        def at(eng, p, name, k):
            eng.wait_ge(s[name], p * PAIR_EVENTS[name] + k)

        def plain(eng):
            eng.sem_inc(s["ready"], 1)

        row = lambda name: sb(name, [P, T])
        masks = sb("masks", [P, 2, P])
        merge = sb("merge", [P, 5, P])
        first = sb("first", [P, 2, P])
        i64 = sb("i64", [P, C])
        resets = row("resets")
        half_log = sb("half_log", [P, 1])
        pv = sb("pv", [P, ND, 8])
        cur = sb("cur", [P, 8])
        r, k, v = row("r"), row("k"), row("v")
        wb, ab, gb = sb("wb", [C, P]), sb("ab", [C, P]), sb("gb", [P, 2, P])
        sg, cum, cc, ce = row("sg"), row("cum"), row("cc"), row("ce")
        tw, ta = row("tw"), row("ta")
        ctr, qs, q = sb("ctr", [P, NC_]), sb("qs", [P, NC_]), sb("q", [P, NC_])
        eex, ep, em = row("eex"), row("ep"), row("em")
        sqk, inv, kk0, kk, kf, kp, a1, beta = (row(n) for n in ("sqk", "inv", "kk0", "kk", "kf", "kp", "a1", "beta"))
        rk, bon, gsb = row("rk"), row("bon"), row("gsb")
        ar = sb("ar", [P, NT, 2, P])
        bt, kt = row("bt"), row("kt")
        vtok, btok, ktok = (sb(n, [P, NT, P]) for n in ("vtok", "btok", "ktok"))
        aw = sb("aw", [P, NT, 2, P])
        bl = [sb(f"bl{h}", [P, NT, 2, P]) for h in range(2)]
        kl = [sb(f"kl{h}", [P, NT, 2, P]) for h in range(2)]
        x = [sb(f"x{h}", [P, NT, P]) for h in range(2)]
        xt = [sb(f"xt{h}", [P, NT, P]) for h in range(2)]
        g = [sb(f"g{h}", [P, NT, P]) for h in range(2)]
        au = [sb(f"au{h}", [P, NT, P]) for h in range(2)]
        rp, ft, zq, st = row("rp"), sb("ft", [P, NC_, C]), sb("zq", [P, NC_, C]), sb("st", [P, NC_, C])
        ysb, dev, sqy, rs, yn = cum, cc, ce, eex, ep
        bank = ps("bank", [P, 8, T])
        block = ctx.enter_context(nc.Block())

        def tiles(view):
            return view.rearrange("p (t c) -> p t c", t=NT)

        @block.sync
        def _(sp):
            for dst, name in ((masks, "c_masks"), (merge, "c_merge"), (first, "c_first")):
                sp.dma_start(dst[:], core.consts[name]).then_inc(s["consts"], 16)
            sp.dma_start(i64[:], core.consts["c_i64"]).then_inc(s["consts"], 16)
            sp.sem_inc(s["pair"], 1)
            sp.sem_inc(s["bon"], 1)
            sp.sem_inc(s["gsb"], 1)
            sp.sem_inc(s["tilde"], 4)
            with sp.Fori(0, ND) as p:
                at(sp, p, "bon", 1)
                at(sp, p, "tilde", 4)
                for c, dst in enumerate((r, k, v)):
                    src = rkv[c].rearrange("(e p) t -> e p t", p=P)[one(p)].rearrange("a p t -> p (a t)")
                    sp.dma_start(dst[:], src).then_inc(s["loaded"], 16)
                at(sp, p, "gsb", 1)
                cols = bass.ds(p * P, P)
                for dst, src in ((wb[:], ins["rw_w_lora_b"][0][:, cols]), (ab[:], ins["rw_a_lora_b"][0][:, cols]),
                                 (gb[:, 0], ins["rw_g_lora_b"][0][0:P, cols]),
                                 (gb[0:32, 1], ins["rw_g_lora_b"][0][P:P + 32, cols])):
                    sp.dma_start(dst, src).then_inc(s["lora_w"], 16)

        @block.tensor
        def _(pe):
            pe.wait_ge(s["consts"], 64)
            with pe.Fori(0, ND) as p:
                at(pe, p, "pair", 1)
                at(pe, p, "lora_w", 64)
                nc.tensor.matmul(bank[:, 0], wb[:], lora["lw"][0:C, 0], start=True, stop=True).then_inc(s["zp"], 1)
                nc.tensor.matmul(bank[:, 1], ab[:], lora["la"][0:C, 0], start=True, stop=True).then_inc(s["ap"], 1)
                at(pe, p, "sqk", 1)
                nc.tensor.matmul(bank[:, 2], core.head_ones[:], sqk[:], start=True, stop=True).then_inc(s["ssk"], 1)
                nc.tensor.matmul(bank[:, 4], gb[:, 0], lora["lg"][:, 0], start=True, stop=False)
                nc.tensor.matmul(bank[:, 4], gb[0:32, 1], lora["lg"][0:32, 1], start=False, stop=True).then_inc(s["gp"], 1)
                at(pe, p, "loaded", 48)
                for t in range(NT):
                    mm = nc.tensor.transpose(bank[:, 5, t * P:(t + 1) * P], v[:, t * P:(t + 1) * P], core.ident[:])
                mm.then_inc(s["vturn"], 1)
                at(pe, p, "rk", 1)
                nc.tensor.matmul(bank[:, 3], core.head_ones[:], rk[:], start=True, stop=True).then_inc(s["bsum"], 1)
                at(pe, p, "tilde", 8)
                for n, src in enumerate((ar[:, :, 0], tiles(bt[:]), tiles(kt[:]))):
                    for t in range(NT):
                        mm = nc.tensor.transpose(bank[:, n, t * P:(t + 1) * P], src[:, t], core.ident[:])
                    mm.then_inc(s["turn"], 1)
                for h in range(2):
                    hp = slice(C * h, C * h + C)
                    banks = (3, 5, 7) if h == 0 else (0, 2, 4)
                    if h == 0:
                        at(pe, p, "bon", 2)
                        at(pe, p, "gsb", 2)
                        at(pe, p, "vtok", 1)
                    for n, lhs in enumerate((bt, kt)):
                        if h == 1:
                            at(pe, p, "tok", 3)
                            at(pe, p, "bl", 2)
                        for t in range(NT):
                            out = bank[:, banks[n] + t // 2, (t % 2) * 2 * P:(t % 2 + 1) * 2 * P]
                            mm = nc.tensor.matmul(out, lhs[hp, t * P:(t + 1) * P], ar[hp, t].rearrange("p a c -> p (a c)"),
                                                  start=True, stop=True)
                        mm.then_inc(s["score"], 1)
                    for t in range(NT):
                        mm = nc.tensor.matmul(bank[:, banks[2], t * P:(t + 1) * P], ar[hp, t, 0], bt[hp, t * P:(t + 1) * P],
                                              start=True, stop=True)
                    mm.then_inc(s["score"], 1)
                at(pe, p, "kl", 4)
                for h in range(2):
                    for t in range(NT):
                        mm = nc.tensor.matmul(bank[:, 5, (t * 2 + h) * C:(t * 2 + h + 1) * C], kl[h][:, t, 0],
                                              vtok[:, t, C * h:C * h + C], start=True, stop=True)
                mm.then_inc(s["lakv"], 1)
                for level in range(len(LEVELS)):
                    last = level == len(LEVELS) - 1
                    for h in range(2):
                        if level == 0:
                            at(pe, p, "x_init", 3 * h + 3)
                            at(pe, p, "nm", h + 1)
                            at(pe, p, "bl", 4)
                        else:
                            at(pe, p, "x", 2 * (level - 1) + h + 1)
                        for t in range(NT):
                            mm = nc.tensor.matmul(bank[:, 6 + h, t * P:(t + 1) * P], bl[h][:, t, 0], x[h][:, t], start=True, stop=True)
                        mm.then_inc(s["g_mm"], 1)
                    for h in range(2):
                        at(pe, p, "g", 2 * level + h + 1)
                        for t in range(NT):
                            cs = slice(t * P, (t + 1) * P)
                            mm = nc.tensor.matmul(bank[:, 2 * h + 1, cs], g[h][:, t], xt[h][:, t], start=True, stop=True)
                            if not last:
                                mm = nc.tensor.matmul(bank[:, 2 * h, cs], xt[h][:, t], g[h][:, t], start=True, stop=True)
                        mm.then_inc(s["x_mm"], 1)
                at(pe, p, "aw", 1)
                for h in range(2):
                    at(pe, p, "x", 8 + h + 1)
                    for t in range(NT):
                        mm = nc.tensor.matmul(bank[:, 6 + h, t * P:(t + 1) * P], xt[h][:, t], aw[:, t, h], start=True, stop=True)
                    mm.then_inc(s["au_mm"], 1)
                at(pe, p, "au", 2)
                for h in range(2):
                    for t in range(NT):
                        mm = nc.tensor.matmul(bank[C * h:C * h + C, 0, t * P:(t + 1) * P], au[h][:, t, 0:C], bl[h][:, t, 1],
                                              start=True, stop=True)
                mm.then_inc(s["rp_mm"], 1)
                for h in range(2):
                    for c in range(NC_):
                        cp = slice(C * (c % 2), C * (c % 2) + C)
                        mm = nc.tensor.matmul(bank[C * h:C * h + C, 1 + 2 * (c % 2), c * C:(c + 1) * C], au[h][cp, c // 2, 0:C],
                                              btok[cp, c // 2, C * h:C * h + C], start=True, stop=True)
                mm.then_inc(s["f_mm"], 1)
                for h in range(2):
                    hc = slice(C * h, C * h + C)
                    for c in range(NC_):
                        cp = slice(C * (c % 2), C * (c % 2) + C)
                        out = bank[hc, 2 + 2 * (c % 2), c * C:(c + 1) * C]
                        nc.tensor.matmul(out, btok[cp, c // 2, hc], au[h][cp, c // 2, C:P], start=True, stop=False)
                        mm = nc.tensor.matmul(out, ktok[cp, c // 2, hc], vtok[cp, c // 2, hc], start=False, stop=True)
                mm.then_inc(s["z_mm"], 1)

                def chain(c):
                    at(pe, p, "f", 2)
                    if c == 1:
                        at(pe, p, "z", 2)
                    else:
                        at(pe, p, "state", c - 1)
                    plain(pe)
                    for h in range(2):
                        hp = slice(C * h, C * h + C)
                        state = zq[hp, 0] if c == 1 else st[hp, c]
                        mm = nc.tensor.matmul(bank[hp, 4, c * C:(c + 1) * C], ft[hp, c], state, start=True, stop=True)
                    mm.then_inc(s["chain"], 1)

                def outputs(t):
                    at(pe, p, "rp", 1)
                    if t:
                        at(pe, p, "state", 2 * t)
                    for h in range(2):
                        hp = slice(C * h, C * h + C)
                        out = bank[hp, 5, t * P:(t + 1) * P]
                        nc.tensor.matmul(out, vtok[:, t, hp], kl[h][:, t, 1], start=True, stop=False)
                        nc.tensor.matmul(out, au[h][:, t, C:P], bl[h][:, t, 1], start=False, stop=False)
                        for c in (2 * t, 2 * t + 1):
                            if c:
                                state = zq[hp, 0] if c == 1 else st[hp, c]
                                mm = nc.tensor.matmul(bank[hp, 5, c * C:(c + 1) * C], state, rp[hp, c * C:(c + 1) * C],
                                                      start=False, stop=(c % 2 == 1))
                    return mm

                chain(1)
                outputs(0)
                for c in (2, 3, 4, 5, 6):
                    chain(c)
                    if c in (3, 5):
                        outputs(c // 2)
                outputs(3).then_inc(s["y_mm"], 1)
                at(pe, p, "ysb", 1)
                nc.tensor.matmul(bank[:, 6], core.head_ones[:], ysb[:], start=True, stop=True).then_inc(s["mean"], 1)
                at(pe, p, "sqy", 1)
                nc.tensor.matmul(bank[:, 7], core.head_ones[:], sqy[:], start=True, stop=True).then_inc(s["var"], 1)

        @block.scalar
        def _(act):
            A = nc.scalar.activation
            with act.Fori(0, ND) as p:
                at(act, p, "pair", 1)
                at(act, p, "cur", 1)
                at(act, p, "loaded", 48)
                A(sqk[:], k[:], ACT.Square, scale=cur[:, KK:KK + 1]).then_inc(s["sqk"], 1)
                at(act, p, "zp", 1)
                A(tw[:], bank[:, 0], ACT.Tanh, scale=0.5, bias=cur[:, W0H:W0H + 1]).then_inc(s["tw"], 1)
                at(act, p, "ap", 1)
                A(ta[:], bank[:, 1], ACT.Tanh, scale=0.5, bias=cur[:, A0H:A0H + 1]).then_inc(s["ta"], 1)
                at(act, p, "vturn", 1)
                A(vtok[:].rearrange("p t c -> p (t c)"), bank[:, 5], ACT.Copy).then_inc(s["vtok"], 1)
                at(act, p, "gp", 1)
                A(gsb[:], bank[:, 4], ACT.Copy).then_inc(s["gsb"], 1)
                at(act, p, "clip", 1)
                A(inv[:], sqk[:], ACT.Ln, scale=LN_SCALE).then_inc(s["lnk"], 1)
                at(act, p, "lnk", 1)
                A(inv[:], inv[:], ACT.Exp, scale=-0.5, bias=half_log[:, 0:1]).then_inc(s["inv"], 1)
                at(act, p, "ce", 1)
                A(eex[:], ce[:], ACT.Exp, scale=-KAPPA).then_inc(s["eex"], 1)
                A(ep[:], cc[:], ACT.Exp, scale=-KAPPA).then_inc(s["ep"], 1)
                A(em[:], cc[:], ACT.Exp, scale=KAPPA).then_inc(s["em"], 1)
                at(act, p, "qsum", 1)
                A(q[:], qs[:], ACT.Exp, scale=-KAPPA).then_inc(s["q"], 1)
                at(act, p, "turn", 1)
                A(aw[:, :, :, 0:C], bank[:, 0].rearrange("p (t h c) -> p t h c", t=NT, h=2), ACT.Copy).then_inc(s["tok"], 1)
                for n, dst in ((1, btok), (2, ktok)):
                    at(act, p, "turn", n + 1)
                    A(dst[:].rearrange("p t c -> p (t c)"), bank[:, n], ACT.Copy).then_inc(s["tok"], 1)
                at(act, p, "lakv", 1)
                A(aw[:, :, :, C:P], bank[:, 5].rearrange("p (t h c) -> p t h c", t=NT, h=2), ACT.Copy).then_inc(s["aw"], 1)
                for h in range(2):
                    at(act, p, "au_mm", h + 1)
                    A(au[h][:].rearrange("p t c -> p (t c)"), bank[:, 6 + h], ACT.Copy).then_inc(s["au"], 1)
                at(act, p, "y_mm", 1)
                A(ysb[:], bank[:, 5], ACT.Copy).then_inc(s["ysb"], 1)
                at(act, p, "dev", 1)
                A(sqy[:], dev[:], ACT.Square).then_inc(s["sqy"], 1)
                at(act, p, "var", 1)
                A(rs[:], bank[:, 7], ACT.Ln, scale=1.0 / C, bias=core.eps[:, 1:2]).then_inc(s["lny"], 1)
                at(act, p, "lny", 1)
                A(rs[:], rs[:], ACT.Exp, scale=-0.5).then_inc(s["rs"], 1)
                at(act, p, "yn", 3)
                plain(act)
                A(flat(yhi[:, one(p)]), yn[:], ACT.Copy).then_inc(s["yhi"], 1)

        @block.gpsimd
        def _(pool):
            G = nc.gpsimd
            ic = lambda h: core.ident[:].rearrange("p (a c) -> p a c", a=1).to_broadcast([P, NT, P])
            pool.wait_ge(s["consts"], 64)
            with pool.Fori(0, ND) as p:
                at(pool, p, "pair", 1)
                at(pool, p, "cur", 1)
                at(pool, p, "loaded", 48)
                plain(pool)
                G.tensor_scalar(kk0[:], k[:], cur[:, KK:KK + 1], None, ALU.mult).then_inc(s["pk"], 1)
                at(pool, p, "ta", 1)
                plain(pool)
                G.tensor_scalar(kf[:], ta[:], cur[:, HKA:HKA + 1], cur[:, OKA:OKA + 1], ALU.mult, ALU.add).then_inc(s["pk"], 1)
                G.tensor_scalar(a1[:], ta[:], 0.5, 0.5, ALU.mult, ALU.add).then_inc(s["pk"], 1)
                at(pool, p, "pk", 2)
                G.tensor_tensor(kp[:], k[:], kf[:], ALU.mult).then_inc(s["pk"], 1)
                at(pool, p, "pk", 3)
                at(pool, p, "inv", 1)
                G.tensor_tensor(kk[:], kk0[:], inv[:], ALU.mult).then_inc(s["pk"], 1)
                at(pool, p, "pk", 5)
                G.tensor_tensor(beta[:], kk[:], a1[:], ALU.mult).then_inc(s["pk"], 1)
                for h in range(2):
                    m = first[:, 1:2].to_broadcast([P, NT, P])
                    at(pool, p, "bl", 2 * h + 2)
                    G.tensor_tensor(xt[h][:], bl[h][:, :, 0], m, ALU.mult).then_inc(s["x_init"], 1)
                    at(pool, p, "x_init", 3 * h + 1)
                    G.tensor_tensor(xt[h][:], xt[h][:], ic(h), ALU.add).then_inc(s["x_init"], 1)
                    at(pool, p, "nm", h + 1)
                    G.tensor_tensor(x[h][:], x[h][:], ic(h), ALU.add).then_inc(s["x_init"], 1)
                at(pool, p, "yhi", 1)
                plain(pool)
                G.tensor_tensor(flat(ylo[:, one(p)]), yn[:], flat(fp(yhi[:, one(p)])), ALU.subtract).then_inc(s["pair"], 1)
            pool.wait_ge(s["pair"], ND + 1)

        @block.vector
        def _(dve):
            V = nc.vector
            TT = V.tensor_tensor
            V.memset(half_log[:], 0.5 * float(np.log(LN_SCALE)))
            V.memset(resets[:], 1.0).then_inc(s["pv"], 1)
            dve.wait_ge(s["pv"], 1)
            V.memset(resets[:].rearrange("p (c t) -> p c t", t=C)[:, :, 0:1], 0.0)
            for c, name, a in ((W0H, "rw_w0", 0.5), (A0H, "rw_a0", 0.5), (KK, "rw_k_k", 1.0), (HKA, "rw_k_a", 0.5),
                               (RK, "rw_r_k", 1.0), (GNW, "rw_gn_w", 1.0), (GNB, "rw_gn_b", 1.0)):
                V.tensor_scalar(pv[:, :, c], core.vec(name), a, None, ALU.mult)
            V.tensor_scalar(pv[:, :, OKA], core.vec("rw_k_a"), -0.5, 1.0, ALU.mult, ALU.add).then_inc(s["pv"], 1)
            dve.wait_ge(s["pv"], 2)
            dve.wait_ge(s["consts"], 64)
            by_chunk = lambda view: view.rearrange("p (c t) -> p c t", t=C)
            spread = lambda view: view.rearrange("p (c a) -> p c a", a=1).to_broadcast([P, NC_, C])
            pairs = lambda n: bank[:, n].rearrange("p (t a c) -> p t a c", t=2, a=2)
            with dve.Fori(0, ND) as p:
                at(dve, p, "pair", 1)
                plain(dve)
                V.tensor_copy(cur[:], pv[:, one(p)].rearrange("p a c -> p (a c)")).then_inc(s["cur"], 1)
                at(dve, p, "tw", 1)
                V.tensor_scalar(sg[:], tw[:], 0.5, 0.5, ALU.mult, ALU.add).then_inc(s["sg"], 1)
                at(dve, p, "sg", 1)
                V.tensor_tensor_scan(cum[:], resets[:], sg[:], 0.0, ALU.mult, ALU.add).then_inc(s["cum"], 1)
                at(dve, p, "cum", 1)
                V.tensor_scalar(ctr[:], by_chunk(cum[:])[:, :, C - 1], 0.5, None, ALU.mult).then_inc(s["ctr"], 1)
                at(dve, p, "ctr", 1)
                TT(by_chunk(cc[:]), by_chunk(cum[:]), spread(ctr[:]), ALU.subtract).then_inc(s["cc"], 1)
                at(dve, p, "cc", 1)
                TT(ce[:], cc[:], sg[:], ALU.subtract).then_inc(s["ce"], 1)
                V.memset(qs[:, NC_ - 1:NC_], 0.0)
                TT(qs[:, 0:NC_ - 1], ctr[:, 0:NC_ - 1], ctr[:, 1:NC_], ALU.add).then_inc(s["qsum"], 1)
                at(dve, p, "ssk", 1)
                V.tensor_scalar(sqk[:], bank[:, 2], 1e-24, None, ALU.max).then_inc(s["clip"], 1)
                at(dve, p, "eex", 1)
                at(dve, p, "pk", 5)
                V.scalar_tensor_tensor(out=ar[:, :, 0], in0=tiles(kk[:]), scalar=-1.0, in1=tiles(eex[:]), op0=ALU.mult,
                                       op1=ALU.mult).then_inc(s["tilde"], 1)
                at(dve, p, "ep", 1)
                TT(ar[:, :, 1], tiles(r[:]), tiles(ep[:]), ALU.mult).then_inc(s["tilde"], 1)
                at(dve, p, "em", 1)
                TT(kt[:], kp[:], em[:], ALU.mult).then_inc(s["tilde"], 1)
                V.scalar_tensor_tensor(out=rk[:], in0=r[:], scalar=cur[:, RK:RK + 1], in1=kp[:], op0=ALU.mult,
                                       op1=ALU.mult).then_inc(s["rk"], 1)
                at(dve, p, "pk", 6)
                TT(bt[:], beta[:], em[:], ALU.mult).then_inc(s["tilde"], 1)
                at(dve, p, "bsum", 1)
                TT(bon[:], bank[:, 3], v[:], ALU.mult).then_inc(s["bon"], 1)
                mm2 = masks[:].rearrange("p a c -> p (a c)").rearrange("p (o n) -> p o n", o=1).to_broadcast([P, 2, 2 * P])
                for h in range(2):
                    banks = (3, 5, 7) if h == 0 else (0, 2, 4)
                    for n, dst, name in ((0, bl[h], "bl"), (1, kl[h], "kl")):
                        at(dve, p, "score", 3 * h + n + 1)
                        for half in range(2):
                            TT(dst[:, 2 * half:2 * half + 2].rearrange("p t a c -> p t (a c)"),
                               bank[:, banks[n] + half].rearrange("p (t n) -> p t n", t=2), mm2, ALU.mult).then_inc(s[name], 1)
                    at(dve, p, "score", 3 * h + 3)
                    TT(x[h][:], tiles(bank[:, banks[2]]), first[:, 0:1].to_broadcast([P, NT, P]), ALU.mult).then_inc(s["nm"], 1)
                for level in range(len(LEVELS)):
                    last = level == len(LEVELS) - 1
                    for h in range(2):
                        at(dve, p, "g_mm", 2 * level + h + 1)
                        TT(g[h][:], tiles(bank[:, 6 + h]), merge[:, level:level + 1].to_broadcast([P, NT, P]), ALU.mult).then_inc(s["g"], 1)
                    for h in range(2):
                        at(dve, p, "x_mm", 2 * level + h + 1)
                        if not last:
                            TT(x[h][:], tiles(bank[:, 2 * h]), x[h][:], ALU.add)
                        TT(xt[h][:], tiles(bank[:, 2 * h + 1]), xt[h][:], ALU.add).then_inc(s["x"], 1)
                at(dve, p, "rp_mm", 1)
                TT(tiles(rp[:]), tiles(bank[:, 0]), ar[:, :, 1], ALU.add).then_inc(s["rp"], 1)
                at(dve, p, "f_mm", 1)
                for odd in range(2):
                    TT(ft[:, odd::2], by_chunk(bank[:, 1 + 2 * odd])[:, odd::2],
                       i64[:].rearrange("p (o c) -> p o c", o=1).to_broadcast([P, NC_ // 2, C]), ALU.add).then_inc(s["f"], 1)
                at(dve, p, "z_mm", 1)
                at(dve, p, "q", 1)
                for odd in range(2):
                    TT(zq[:, odd::2], by_chunk(bank[:, 2 + 2 * odd])[:, odd::2], spread(q[:])[:, odd::2], ALU.mult).then_inc(s["z"], 1)
                at(dve, p, "z", 2)
                for c in range(1, NC_ - 1):
                    at(dve, p, "chain", c)
                    V.scalar_tensor_tensor(out=st[:, c + 1], in0=bank[:, 4, c * C:(c + 1) * C], scalar=q[:, c:c + 1],
                                           in1=zq[:, c], op0=ALU.mult, op1=ALU.add).then_inc(s["state"], 1)
                at(dve, p, "mean", 1)
                V.scalar_tensor_tensor(out=dev[:], in0=bank[:, 6], scalar=-1.0 / C, in1=ysb[:], op0=ALU.mult,
                                       op1=ALU.add).then_inc(s["dev"], 1)
                at(dve, p, "rs", 1)
                V.scalar_tensor_tensor(out=yn[:], in0=dev[:], scalar=cur[:, GNW:GNW + 1], in1=rs[:], op0=ALU.mult,
                                       op1=ALU.mult).then_inc(s["yn"], 1)
                at(dve, p, "yn", 1)
                V.scalar_tensor_tensor(out=yn[:], in0=yn[:], scalar=cur[:, GNB:GNB + 1], in1=bon[:], op0=ALU.add,
                                       op1=ALU.add).then_inc(s["yn"], 1)
                at(dve, p, "yn", 2)
                TT(yn[:], yn[:], gsb[:], ALU.mult).then_inc(s["yn"], 1)
    close_stage(core, s)


PROJECT_SEMS = ["raw0", "raw1", "raw2", "raw3", "w_free", "w_hi", "w_ready", "rstd", "h_lo", "h_hi", "h32", "sq",
                "sq_used", "ms", "out", "st0", "st1", "ready"]


def project(core, tag, gain, weights, dst):
    nc = core.nc
    cols = weights.shape[1]
    full, rest = cols // P, cols % P
    assert full % 4 == 0
    w = weights.rearrange("(k p) e -> p k e", p=P)
    with ExitStack() as ctx:
        s, sb, ps = open_stage(core, ctx, tag, PROJECT_SEMS)
        open_ring(core, sb)
        sq = sb("sq", [P, 2, T])
        ms = sb("ms", [P, T])
        rstd = sb("rstd", [P, T])
        h32 = sb("h32", [P, 2, T])
        hhi = sb("hhi", [P, ND, T], F32R)
        hlo = sb("hlo", [P, ND, T], F32R)
        staged = sb("staged", [P, 2, T])
        p_ms = ps("p_ms", [P, T])
        p_out = ps("p_out", [P, 4, T])
        block = ctx.enter_context(nc.Block())

        def units(eng, body):
            with eng.Fori(0, full // 4) as i:
                for j in range(4):
                    body(4 * i + j, j, i, P)
            if rest:
                body(full, 0, full // 4, rest)

        @block.sync
        def _(sp):
            def load(unit, slot, rounds, m):
                src = w[:, :, full * P:] if isinstance(unit, int) else w[:, :, bass.ds(unit * P, P)]
                load_unit(sp, s, core, slot, unit, src)
            units(sp, load)

        @block.vector
        def _(dve):
            dve.sem_inc(s["w_ready"], SLOTS)
            norm_vector(core, dve, s, gain, ms, rstd, h32, hhi, hlo)
            units(dve, lambda unit, slot, rounds, m: split_unit(dve, s, core, slot, rounds, unit, ND, m))

        @block.tensor
        def _(pe):
            pe.sem_inc(s["w_free"], SLOTS)
            norm_tensor(core, pe, s, sq, p_ms)
            pe.wait_ge(s["h_lo"], ND)

            def step(unit, slot, rounds, m):
                pe.wait_ge(s["w_ready"], done(unit))
                pe.wait_ge(s["out"], unit + 1)
                for k in range(ND):
                    mm = three_passes(core, p_out[:, slot], slot, k, hhi[:, k], hlo[:, k], k == 0, k == ND - 1)
                mm.then_inc(s["w_free"], 1)
            units(pe, step)

        @block.scalar
        def _(act):
            act.sem_inc(s["out"], 4)
            act.sem_inc(s["st0"], 16)
            act.sem_inc(s["st1"], 16)
            norm_scalar(core, act, s, sq, p_ms, ms, h32, hhi)
            rows = dst[0:full * P].rearrange("(e p) t -> e p t", p=P)

            def step(unit, slot, rounds, m):
                turn = slot % 2
                act.wait_ge(s["w_free"], done(unit))
                act.wait_ge(s[f"st{turn}"], 32 * rounds + (8 * (slot - turn) + 16))
                nc.scalar.activation(staged[0:m, turn], p_out[0:m, slot], ACT.Copy).then_inc(s["out"], 1)
                act.wait_ge(s["out"], unit + 5)
                to = dst[full * P:cols] if isinstance(unit, int) else rows[one(unit)].rearrange("a p t -> p (a t)")
                act.dma_start(to, staged[0:m, turn]).then_inc(s[f"st{turn}"], 16)
            units(act, step)
            act.wait_ge(s["st0"], 16 * (full // 2 + (1 if rest else 0) + 1))
            act.wait_ge(s["st1"], 16 * (full // 2 + 1))
    close_stage(core, s)


def norm_scalar(core, act, s, sq, p_ms, ms, h32, hhi):
    nc = core.nc
    for d in range(ND):
        if d >= 2:
            act.wait_ge(s["sq_used"], d - 1)
        nc.scalar.activation(sq[:, d % 2], core.x[:, d], ACT.Square).then_inc(s["sq"], 1)
    act.wait_ge(s["sq_used"], ND)
    nc.scalar.activation(ms[:], p_ms[:], ACT.Sqrt, scale=1.0 / D, bias=core.eps[:, 0:1]).then_inc(s["ms"], 1)
    for d in range(ND):
        act.wait_ge(s["h32"], d + 1)
        nc.scalar.activation(hhi[:, d], h32[:, d % 2], ACT.Copy).then_inc(s["h_hi"], 1)


def norm_tensor(core, pe, s, sq, p_ms):
    nc = core.nc
    for d in range(ND):
        pe.wait_ge(s["sq"], d + 1)
        nc.tensor.matmul(p_ms[:], core.ones[:], sq[:, d % 2], start=(d == 0), stop=(d == ND - 1)).then_inc(s["sq_used"], 1)


def norm_vector(core, dve, s, gain, ms, rstd, h32, hhi, hlo):
    nc = core.nc
    dve.wait_ge(s["ms"], 1)
    nc.vector.reciprocal(rstd[:], ms[:]).then_inc(s["rstd"], 1)
    dve.wait_ge(s["rstd"], 1)
    for d in range(ND):
        if d >= 2:
            dve.wait_ge(s["h_lo"], d - 1)
        nc.vector.scalar_tensor_tensor(out=h32[:, d % 2], in0=core.x[:, d], scalar=gain[:, d:d + 1],
                                       in1=rstd[:], op0=ALU.mult, op1=ALU.mult).then_inc(s["h32"], 1)
        dve.wait_ge(s["h_hi"], d + 1)
        nc.vector.tensor_tensor(hlo[:, d], h32[:, d % 2], fp(hhi[:, d]), ALU.subtract).then_inc(s["h_lo"], 1)


ADD_SEMS = ["raw0", "raw1", "raw2", "raw3", "w_free", "w_hi", "w_ready", "out", "added", "ready"]


def project_add(core, tag, yhi, ylo, weights):
    nc = core.nc
    w = weights.rearrange("(k p) e -> p k e", p=P)
    with ExitStack() as ctx:
        s, sb, ps = open_stage(core, ctx, tag, ADD_SEMS)
        open_ring(core, sb)
        part = sb("part", [P, 2, T])
        p_out = ps("p_out", [P, 2, T])
        block = ctx.enter_context(nc.Block())

        @block.sync
        def _(sp):
            with sp.Fori(0, ND // 4) as i:
                for j in range(4):
                    load_unit(sp, s, core, j, 4 * i + j, w[:, :, bass.ds(4 * P * i + j * P, P)])

        @block.vector
        def _(dve):
            dve.sem_inc(s["w_ready"], SLOTS)
            with dve.Fori(0, ND // 4) as i:
                for j in range(4):
                    split_unit(dve, s, core, j, i, 4 * i + j, ND)

        @block.tensor
        def _(pe):
            pe.sem_inc(s["w_free"], SLOTS)
            with pe.Fori(0, ND // 4) as i:
                for j in range(4):
                    pe.wait_ge(s["w_ready"], done(4 * i + j))
                    pe.wait_ge(s["out"], 4 * i + (j + 1))
                    for k in range(ND):
                        mm = three_passes(core, p_out[:, j % 2], j, k, yhi[:, k], ylo[:, k], k == 0, k == ND - 1)
                    mm.then_inc(s["w_free"], 1)

        @block.scalar
        def _(act):
            act.sem_inc(s["out"], 2)
            with act.Fori(0, ND // 4) as i:
                for j in range(4):
                    act.wait_ge(s["w_free"], done(4 * i + j))
                    act.wait_ge(s["added"], 4 * i + (j + 1))
                    nc.scalar.activation(part[:, j % 2], p_out[:, j % 2], ACT.Copy).then_inc(s["out"], 1)

        @block.gpsimd
        def _(pool):
            pool.sem_inc(s["added"], 2)
            with pool.Fori(0, ND // 4) as i:
                for j in range(4):
                    pool.wait_ge(s["out"], 4 * i + (j + 3))
                    pool.sem_inc(s["ready"], 1)
                    xs = flat(core.x[:, one(4 * i + j)])
                    nc.gpsimd.tensor_tensor(xs, xs, part[:, j % 2], ALU.add).then_inc(s["added"], 1)
            pool.wait_ge(s["added"], ND + 2)
    close_stage(core, s)


G = 4
KIND = G * C
N_CMP = (T - 32) // 16 + 1
CMP_LEN, CMP_STRIDE, CMP_HIDDEN = 32, 16, 256
NL = CMP_LEN // 2
NH = CMP_HIDDEN // P

ROTATE_EVENTS = {"sqx": 1, "ss": 1, "ln": 1, "rs": 1, "n": 1, "perm": 1, "t1": 1, "t2": 1, "rot": 1}


def rotate(core, tag, source, tiles, gain_of, plain_out, rot_out, scale=1.0):
    nc = core.nc
    per = tiles // len(gain_of)
    with ExitStack() as ctx:
        s, sb, ps = open_stage(core, ctx, tag, list(ROTATE_EVENTS) + ["loaded", "ready", "consts", "gains", "scaled", "out0", "out1"])

        def at(eng, m, name, k=1):
            eng.wait_ge(s[name], m * ROTATE_EVENTS[name] + k * ROTATE_EVENTS[name])

        def wait_plain(eng):
            eng.sem_inc(s["ready"], 1)

        cos, sin = sb("cos", [P, T]), sb("sin", [P, T])
        swap = sb("swap", [P, P])
        gain = sb("gain", [P, len(gain_of)])
        xt = sb("xt", [P, tiles, T])
        rs = sb("rs", [P, tiles, T])
        sq = sb("sq", [P, 2, T])
        n = sb("n", [P, 2, T])
        t1, t2 = sb("t1", [P, 2, T]), sb("t2", [P, 2, T])
        rot = sb("rot", [P, 2, T])
        p_ss = ps("p_ss", [P, 2, T])
        p_swap = ps("p_swap", [P, 2, T])
        block = ctx.enter_context(nc.Block())
        outs = 2 if plain_out else 1
        loop = lambda eng: eng.Fori(0, tiles // 2)

        @block.sync
        def _(sp):
            for c, g in enumerate(gain_of):
                for h in range(2):
                    sp.dma_start(gain[C * h:C * h + C, c:c + 1], g.rearrange("(d a) -> d a", a=1)).then_inc(s["gains"], 16)
            with loop(sp) as i:
                for j in range(2):
                    sp.dma_start(flat(xt[:, one(2 * i + j)]), source(i, j)).then_inc(s["loaded"], 16)
            for dst, name in ((cos[:], "c_cos"), (sin[:], "c_sin"), (swap[:], "c_swap")):
                sp.dma_start(dst, core.consts[name]).then_inc(s["consts"], 16)
            with loop(sp) as i:
                for j in range(2):
                    m = 2 * i + j
                    at(sp, m, "rot")
                    if plain_out:
                        sp.dma_start(plain_out(i, j), n[:, j]).then_inc(s[f"out{j}"], 16)
                    sp.dma_start(rot_out(i, j), rot[:, j]).then_inc(s[f"out{j}"], 16)
            for j in range(2):
                sp.wait_ge(s[f"out{j}"], 16 * outs * (tiles // 2 + 1))

        @block.scalar
        def _(act):
            act.sem_inc(s["ss"], 2)
            with loop(act) as i:
                for j in range(2):
                    m = 2 * i + j
                    act.wait_ge(s["loaded"], 16 * tiles)
                    at(act, m, "ss")
                    wait_plain(act)
                    nc.scalar.activation(sq[:, j], flat(xt[:, one(m)]), ACT.Square).then_inc(s["sqx"], 1)
                    at(act, m, "ss", 3)
                    wait_plain(act)
                    nc.scalar.activation(flat(rs[:, one(m)]), p_ss[:, j], ACT.Ln, scale=1.0 / C,
                                         bias=core.eps[:, 0:1]).then_inc(s["ln"], 1)
            with loop(act) as i:
                for j in range(2):
                    m = 2 * i + j
                    at(act, m, "ln", 3)
                    wait_plain(act)
                    nc.scalar.activation(flat(rs[:, one(m)]), flat(rs[:, one(m)]), ACT.Exp, scale=-0.5).then_inc(s["rs"], 1)

        @block.tensor
        def _(pe):
            with loop(pe) as i:
                for j in range(2):
                    m = 2 * i + j
                    at(pe, m, "sqx")
                    at(pe, m, "ln")
                    nc.tensor.matmul(p_ss[:, j], core.head_ones[:], sq[:, j], start=True, stop=True).then_inc(s["ss"], 1)
            pe.wait_ge(s["consts"], 48)
            with loop(pe) as i:
                for j in range(2):
                    m = 2 * i + j
                    at(pe, m, "n")
                    nc.tensor.matmul(p_swap[:, j], swap[:], n[:, j], start=True, stop=True).then_inc(s["perm"], 1)

        @block.vector
        def _(dve):
            dve.wait_ge(s["gains"], 32 * len(gain_of))
            nc.vector.tensor_scalar(gain[:], gain[:], scale, None, ALU.mult).then_inc(s["scaled"], 1)
            dve.wait_ge(s["scaled"], 1)
            dve.wait_ge(s["consts"], 48)
            for j in range(2):
                dve.sem_inc(s[f"out{j}"], 16 * outs)
            with loop(dve) as i:
                for j in range(2):
                    m = 2 * i + j
                    at(dve, m, "rs")
                    dve.wait_ge(s[f"out{j}"], 16 * outs * (i + 1))
                    at(dve, m, "t1")
                    g = gain[:, 0:1] if len(gain_of) == 1 else gain[:, one(i)]
                    nc.vector.scalar_tensor_tensor(out=n[:, j], in0=flat(xt[:, one(m)]), scalar=g,
                                                   in1=flat(rs[:, one(m)]), op0=ALU.mult, op1=ALU.mult).then_inc(s["n"], 1)
                    at(dve, m, "perm")
                    nc.vector.tensor_tensor(t2[:, j], p_swap[:, j], sin[:], ALU.mult).then_inc(s["t2"], 1)
                    at(dve, m, "t2")
                    at(dve, m, "t1", 3)
                    nc.vector.tensor_tensor(rot[:, j], t1[:, j], t2[:, j], ALU.add).then_inc(s["rot"], 1)

        @block.gpsimd
        def _(pool):
            pool.wait_ge(s["consts"], 48)
            pool.sem_inc(s["t1"], 2)
            pool.sem_inc(s["ln"], 2)
            with loop(pool) as i:
                for j in range(2):
                    m = 2 * i + j
                    at(pool, m, "n")
                    wait_plain(pool)
                    nc.gpsimd.tensor_tensor(t1[:, j], n[:, j], cos[:], ALU.mult).then_inc(s["t1"], 1)
    close_stage(core, s)


def values(core, tag, kv, v_tok, k_cmp, v_cmp):
    nc, ins = core.nc, core.ins
    with ExitStack() as ctx:
        s, sb, ps = open_stage(core, ctx, tag, ["vt", "turned", "read", "vout", "tok", "pos", "w1", "w2", "blk", "h1",
                                               "gelu", "c2", "sqc", "ss", "pos_turned", "pos_copied", "ln", "rsc", "kc", "vc", "cout", "gain"])
        vt = sb("vt", [P, 4, T])
        vsb = sb("vsb", [P, 4, T])
        tok = sb("tok", [P, 2, G, T])
        pos_rows, pos = sb("pos_rows", [NL, 2, P]), sb("pos", [P, 2, NL])
        w1 = sb("w1", [P, 2, NL, CMP_HIDDEN])
        w2 = sb("w2", [P, 2, NH, C])
        gain = sb("gain", [C, 1])
        NB = G * N_CMP
        blk = sb("blk", [P, 4, NB])
        hid = sb("hid", [P, 2, NH, NB])
        kc, sqc, rsc, vc = sb("kc", [C, NB]), sb("sqc", [C, NB]), sb("rsc", [C, NB]), sb("vc", [NB, C])
        turn = ps("turn", [P, 2, T])
        p_h = ps("p_h", [P, 4, T])
        p_o = ps("p_o", [P, 2, T])
        block = ctx.enter_context(nc.Block())
        v_rows = kv[2 * KIND:6 * KIND].rearrange("(b x e p) t -> x b e p t", b=2, x=2, p=P)[1]
        steps = [(which, lp) for which in range(2) for lp in range(NL)]

        @block.sync
        def _(sp):
            for which in range(2):
                src = kv[which * KIND:(which + 1) * KIND].rearrange("(g d) t -> d g t", d=C)
                sp.dma_start(tok[0:C, which], src).then_inc(s["tok"], 16)
                sp.dma_start(tok[C:P, which, :, 0:T - 1], src[:, :, 1:T]).then_inc(s["tok"], 16)
                p_src = ins["cmp_pos_k" if which == 0 else "cmp_pos_v"].rearrange("(l a) d -> l (a d)", a=2)
                sp.dma_start(pos_rows[:, which], p_src).then_inc(s["pos"], 16)
                w = ins["cmp_k_w1" if which == 0 else "cmp_v_w1"].rearrange("(l p) h -> p l h", p=P)
                sp.dma_start(w1[:, which], w).then_inc(s["w1"], 16)
                sp.dma_start(w2[:, which], ins["cmp_k_w2" if which == 0 else "cmp_v_w2"].rearrange("(l p) h -> p l h", p=P)).then_inc(s["w2"], 16)
            sp.dma_start(gain[:], ins["kv_k_norm"][0].rearrange("(d a) -> d a", a=1)).then_inc(s["gain"], 16)
            sp.wait_ge(s["vc"], 1)
            sp.dma_start(v_cmp, vc[:]).then_inc(s["cout"], 16)
            sp.wait_ge(s["kc"], 1)
            sp.dma_start(k_cmp, kc[:]).then_inc(s["cout"], 16)
            sp.wait_ge(s["cout"], 32)

        @block.scalar
        def _(act):
            for n in range(4):
                act.dma_start(vt[:, n], v_rows[n // 2, n % 2]).then_inc(s["vt"], 16)
            for n in range(4):
                act.wait_ge(s["turned"], n + 1)
                nc.scalar.activation(vsb[:, n], turn[:, n % 2], ACT.Copy).then_inc(s["read"], 1)
                act.wait_ge(s["read"], n + 1)
                act.dma_start(v_tok[n], vsb[:, n]).then_inc(s["vout"], 16)
            for which in range(2):
                for t in range(NH):
                    act.wait_ge(s["h1"], NL * which + NL)
                    nc.scalar.activation(hid[:, which, t], p_h[:, 2 * which + t, 0:NB], ACT.Gelu_apprx_tanh).then_inc(s["gelu"], 1)
            act.wait_ge(s["c2"], 1)
            nc.scalar.activation(sqc[:], p_o[0:C, 0, 0:NB], ACT.Square).then_inc(s["sqc"], 1)
            act.wait_ge(s["c2"], 2)
            nc.scalar.activation(vc[:], p_o[0:NB, 1, 0:C], ACT.Copy).then_inc(s["vc"], 1)
            act.wait_ge(s["ss"], 1)
            nc.scalar.activation(rsc[:], p_h[0:C, 0, 0:NB], ACT.Ln, scale=1.0 / C, bias=core.eps[0:C, 0:1]).then_inc(s["ln"], 1)
            act.wait_ge(s["ln"], 1)
            nc.scalar.activation(rsc[:], rsc[:], ACT.Exp, scale=-0.5).then_inc(s["rsc"], 1)
            act.wait_ge(s["vout"], 64)

        @block.tensor
        def _(pe):
            pe.wait_ge(s["pos"], 32)
            for which in range(2):
                mm = nc.tensor.transpose(p_o[:, 1, which * NL:(which + 1) * NL], pos_rows[:, which], core.ident[0:NL, 0:NL])
            mm.then_inc(s["pos_turned"], 1)
            for n in range(4):
                pe.wait_ge(s["vt"], 64)
                if n >= 2:
                    pe.wait_ge(s["read"], n - 1)
                for t in range(NT):
                    mm = nc.tensor.transpose(turn[:, n % 2, t * P:(t + 1) * P], vt[:, n, t * P:(t + 1) * P], core.ident[:])
                mm.then_inc(s["turned"], 1)
            for n, (which, lp) in enumerate(steps):
                pe.wait_ge(s["blk"], n + 1)
                if lp == 0:
                    pe.wait_ge(s["w1"], 32)
                for t in range(NH):
                    mm = nc.tensor.matmul(p_h[:, 2 * which + t, 0:NB], w1[:, which, lp, t * P:(t + 1) * P],
                                          blk[:, n % 4], start=(lp == 0), stop=(lp == NL - 1))
                mm.then_inc(s["h1"], 1)
            pe.wait_ge(s["w2"], 32)
            pe.wait_ge(s["gelu"], 2)
            for t in range(NH):
                mm = nc.tensor.matmul(p_o[0:C, 0, 0:NB], w2[:, 0, t], hid[:, 0, t], start=(t == 0), stop=(t == NH - 1))
            mm.then_inc(s["c2"], 1)
            pe.wait_ge(s["gelu"], 4)
            for t in range(NH):
                mm = nc.tensor.matmul(p_o[0:NB, 1, 0:C], hid[:, 1, t], w2[:, 1, t], start=(t == 0), stop=(t == NH - 1))
            mm.then_inc(s["c2"], 1)
            pe.wait_ge(s["sqc"], 1)
            nc.tensor.matmul(p_h[0:C, 0, 0:NB], core.ones[0:C, 0:C], sqc[:], start=True, stop=True).then_inc(s["ss"], 1)

        @block.vector
        def _(dve):
            dve.wait_ge(s["tok"], 64)
            dve.wait_ge(s["pos_turned"], 1)
            nc.vector.tensor_copy(pos[:], p_o[:, 1, 0:2 * NL].rearrange("p (a l) -> p a l", a=2)).then_inc(s["pos_copied"], 1)
            dve.wait_ge(s["pos_copied"], 1)
            for n, (which, lp) in enumerate(steps):
                if n >= 4:
                    dve.wait_ge(s["h1"], n - 3)
                src = tok[:, which, :, 2 * lp:2 * lp + CMP_STRIDE * (N_CMP - 1) + 1:CMP_STRIDE]
                nc.vector.tensor_scalar(blk[:, n % 4].rearrange("p (g n) -> p g n", g=G), src,
                                        pos[:, which, lp:lp + 1], None, ALU.add).then_inc(s["blk"], 1)
            dve.wait_ge(s["gain"], 16)
            dve.wait_ge(s["rsc"], 1)
            nc.vector.scalar_tensor_tensor(out=kc[:], in0=p_o[0:C, 0, 0:NB], scalar=gain[:, 0:1], in1=rsc[:],
                                           op0=ALU.mult, op1=ALU.mult).then_inc(s["kc"], 1)
    close_stage(core, s)




def attention_steps():
    steps, turn = [], None
    for group in range(2):
        for pair in range(2):
            for head in range(2):
                steps.append(("cmp", group, pair, head, 0))
                steps += [("main", group, pair, head, t) for t in range(NT)][0:1]
                if turn and head == 0:
                    steps.append(turn)
                steps += [("main", group, pair, head, t) for t in range(1, NT)]
            turn = ("turn", group, pair, 0, 0)
    return steps + [turn]


STEPS = attention_steps()
ATTENTION_EVENTS = {
    "scores": ("cmp", "main"), "masked": ("cmp",), "nmax": ("cmp", "main"), "probs": ("cmp", "main"),
    "turned": ("cmp", "main", "turn"), "copied_v": ("main", "turn"), "copied_a": ("cmp", "main", "turn"),
    "o_mm": ("cmp", "main"), "recip": ("cmp", "main"), "coef": ("cmp", "main"), "o_sel": ("main",), "o": ("cmp", "main"),
}
N_LOADS = 9


def attention(core, tag, q_plain, q_rot, gate_logits, k_rot, v_tok, k_cmp, v_cmp, yhi, ylo):
    nc, ins = core.nc, core.ins
    U = len(STEPS)
    assert U % 4 == 0
    per_body = {e: sum(st[0] in kinds for st in STEPS) for e, kinds in ATTENTION_EVENTS.items()}

    with ExitStack() as ctx:
        s, sb, ps = open_stage(core, ctx, tag, list(ATTENTION_EVENTS) + ["in0", "in1", "gl", "consts", "sig", "gt", "gates", "ready"])

        def at(eng, i, name, u):
            kinds = ATTENTION_EVENTS[name]
            whole, u = divmod(u, U)
            count = sum(st[0] in kinds for st in STEPS[:u + 1]) + whole * per_body[name]
            eng.wait_ge(s[name], i * per_body[name] + (per_body[name] + count))

        def credit(eng, *names):
            for name in names:
                eng.sem_inc(s[name], per_body[name])

        kk = [sb(f"kk{g}", [P, 2, T]) for g in range(2)]
        kc = [sb(f"kc{g}", [P, N_CMP]) for g in range(2)]
        vv = [sb(f"vv{g}", [P, 2, NT, C]) for g in range(2)]
        vc = [sb(f"vc{g}", [N_CMP, C]) for g in range(2)]
        qp = [sb(f"qp{g}", [P, 2, T]) for g in range(2)]
        qr = [sb(f"qr{g}", [P, 2, T]) for g in range(2)]
        glog = sb("glog", [48, T])
        gates = sb("gates", [P, NT, 48])
        causal = sb("causal", [P, P])
        cmp_neg = sb("cmp_neg", [P, NT, N_CMP])
        has_block = sb("has_block", [P, 1])
        ident16, causal16 = sb("ident16", [P, P], mybir.dt.bfloat16), sb("causal16", [P, P], mybir.dt.bfloat16)
        masked = sb("masked", [P, 2, NT, N_CMP])
        nmax, sums = sb("nmax", [P, 2, NT]), sb("sums", [P, 4, NT])
        probs = sb("probs", [P, 2, 2, T])
        pt = sb("pt", [P, 2, 2, T])
        rcp, coef = sb("rcp", [P, NT]), sb("coef", [P, NT])
        osb = sb("osb", [P, 2, NT, P])
        bank = ps("bank", [P, 8, T])
        block = ctx.enter_context(nc.Block())

        @block.sync
        def _(sp):
            sp.dma_start(glog[:], gate_logits).then_inc(s["gl"], 16)
            for dst, name in ((causal, "c_causal"), (cmp_neg, "c_cmp_neg"), (has_block, "c_has_block")):
                sp.dma_start(dst[:], core.consts[name]).then_inc(s["consts"], 16)
            with sp.Fori(0, 2) as i:
                for g in range(2):
                    last = max(u for u, st in enumerate(STEPS) if st[0] != "turn" and st[1] == g)
                    at(sp, i, "o_mm", last - U)
                    it = lambda view: view[one(i)].rearrange
                    keys = k_rot.rearrange("(b e x d) t -> x e d b t", b=2, x=2, d=C)[g][one(i)].rearrange("o d b t -> (o d) b t")
                    keys_c = k_cmp.rearrange("d (e x n) -> x e d n", x=2, n=N_CMP)[g][one(i)].rearrange("o d n -> (o d) n")
                    for h in range(2):
                        sp.dma_start(kk[g][C * h:C * h + C], keys).then_inc(s[f"in{g}"], 16)
                        sp.dma_start(kc[g][C * h:C * h + C], keys_c).then_inc(s[f"in{g}"], 16)
                    for q, dst in ((q_plain, qp[g]), (q_rot, qr[g])):
                        src = q.rearrange("(e x j p) t -> x e p j t", x=2, j=2, p=P)[g][one(i)].rearrange("o p j t -> (o p) j t")
                        sp.dma_start(dst[:], src).then_inc(s[f"in{g}"], 16)
                    for b in range(2):
                        src = v_tok.rearrange("(b e) p (t x d) -> b x e p t d", b=2, x=2, d=C)[b][g][one(i)].rearrange("o p t d -> (o p) t d")
                        sp.dma_start(vv[g][:, b], src).then_inc(s[f"in{g}"], 16)
                    src = v_cmp.rearrange("(e x n) d -> x e n d", x=2, n=N_CMP)[g][one(i)].rearrange("o n d -> (o n) d")
                    sp.dma_start(vc[g][:], src).then_inc(s[f"in{g}"], 16)

        @block.tensor
        def _(pe):
            pe.wait_ge(s["sig"], 1)
            for t in range(NT):
                mm = nc.tensor.transpose(bank[:, 6, t * 48:(t + 1) * 48], glog[:, t * P:(t + 1) * P], core.ident[0:48, 0:48])
            mm.then_inc(s["gt"], 1)
            pe.wait_ge(s["gates"], 2)
            credit(pe, "scores", "turned", "o_mm")

            def scores(i, u):
                kind, g, pair, head, t = STEPS[u]
                if kind == "turn":
                    return
                hp, slot = slice(C * head, C * head + C), u % 2
                if u == 0 or STEPS[u - 1][1] != g and kind == "cmp":
                    pe.wait_ge(s[f"in{g}"], 16 * N_LOADS * (i + 1))
                at(pe, i, "probs", u - 2)
                if kind == "cmp":
                    for t in range(NT):
                        mm = nc.tensor.matmul(bank[:, 2 * slot, t * N_CMP:(t + 1) * N_CMP], qp[g][hp, pair, t * P:(t + 1) * P],
                                              kc[g][hp], start=True, stop=True)
                    mm.then_inc(s["scores"], 1)
                    return
                n = (t + 1) * P
                for b in range(2):
                    nc.tensor.matmul(bank[:, 2 * slot + b, 0:n], qr[g][hp, pair, t * P:n], kk[g][hp, b, 0:n],
                                     start=True, stop=False)
                    mm = nc.tensor.matmul(bank[:, 2 * slot + b, t * P:n], ident16[:], causal16[:], start=False, stop=True)
                mm.then_inc(s["scores"], 1)

            def turn(i, u):
                kind, g, pair, head, t = STEPS[u]
                at(pe, i, "copied_v", u - 1)
                at(pe, i, "copied_a", u - 1)
                if kind == "turn":
                    last = max(w for w in range(U) if STEPS[w] == ("main", g, pair, 1, NT - 1))
                    at(pe, i, "o", last)
                    for t in range(NT):
                        mm = nc.tensor.transpose(bank[:, 4, t * P:(t + 1) * P], osb[:, pair, t], core.ident[:])
                elif kind == "cmp":
                    at(pe, i, "probs", u)
                    for t in range(NT):
                        mm = nc.tensor.transpose(bank[0:N_CMP, 4, t * P:(t + 1) * P], probs[:, u % 2, 0, t * N_CMP:(t + 1) * N_CMP],
                                                 core.ident[:])
                else:
                    at(pe, i, "probs", u)
                    for b in range(2):
                        for j in range(t + 1):
                            mm = nc.tensor.transpose(bank[:, 4 + b, j * P:(j + 1) * P], probs[:, u % 2, b, j * P:(j + 1) * P],
                                                     core.ident[:])
                mm.then_inc(s["turned"], 1)

            def weigh(i, u):
                kind, g, pair, head, t = STEPS[u]
                if kind == "turn":
                    return
                at(pe, i, "copied_a", u)
                at(pe, i, "o", u - 2)
                if kind == "cmp":
                    for t in range(NT):
                        mm = nc.tensor.matmul(bank[:, 6 + u % 2, t * C:(t + 1) * C], pt[0:N_CMP, u % 2, 0, t * P:(t + 1) * P], vc[g][:],
                                              start=True, stop=True)
                else:
                    at(pe, i, "copied_v", u)
                    for b in range(2):
                        out = bank[:, 6 + u % 2, b * C:(b + 1) * C]
                        for j in range(t + 1):
                            mm = nc.tensor.matmul(out, pt[:, u % 2, b, j * P:(j + 1) * P], vv[g][:, b, j], start=(j == 0), stop=(j == t))
                mm.then_inc(s["o_mm"], 1)

            with pe.Fori(0, 2) as i:
                scores(i, 0)
                for u in range(U):
                    if u + 1 < U:
                        scores(i, u + 1)
                    if STEPS[u][0] == "turn":
                        weigh(i, u - 1)
                        turn(i, u)
                    else:
                        turn(i, u)
                        if u:
                            weigh(i, u - 1)

        @block.scalar
        def _(act):
            A = nc.scalar.activation
            credit(act, "probs", "copied_a")
            act.wait_ge(s["gl"], 16)
            A(glog[:], glog[:], ACT.Sigmoid).then_inc(s["sig"], 1)

            def exps(i, u):
                kind, g, pair, head, t = STEPS[u]
                if kind == "turn":
                    return
                slot = u % 2
                at(act, i, "nmax", u)
                at(act, i, "turned", u - 2)
                if kind == "cmp":
                    for t in range(NT):
                        a = A(probs[:, slot, 0, t * N_CMP:(t + 1) * N_CMP], masked[:, slot, t], ACT.Exp,
                              bias=nmax[:, slot, t:t + 1], accum_out=sums[:, u % 4, t:t + 1])
                else:
                    n = (t + 1) * P
                    for b in range(2):
                        a = A(probs[:, slot, b, 0:n], bank[:, 2 * slot + b, 0:n], ACT.Exp, bias=nmax[:, slot, b:b + 1],
                              accum_out=sums[:, u % 4, b:b + 1])
                a.then_inc(s["probs"], 1)

            def copy(i, u):
                kind, g, pair, head, t = STEPS[u]
                at(act, i, "turned", u)
                at(act, i, "o_mm", u - 2)
                if kind == "turn":
                    act.sem_inc(s["ready"], 1)
                    A(flat(yhi[:, one(4 * i + (2 * g + pair))]), bank[:, 4], ACT.Copy).then_inc(s["copied_a"], 1)
                elif kind == "cmp":
                    A(pt[0:N_CMP, u % 2, 0], bank[0:N_CMP, 4], ACT.Copy).then_inc(s["copied_a"], 1)
                else:
                    n = (t + 1) * P
                    A(pt[:, u % 2, 1, 0:n], bank[:, 5, 0:n], ACT.Copy).then_inc(s["copied_a"], 1)

            with act.Fori(0, 2) as i:
                for u in range(U + 1):
                    if u < U:
                        exps(i, u)
                    if u:
                        copy(i, u - 1)

        @block.vector
        def _(dve):
            V = nc.vector
            dve.wait_ge(s["consts"], 48)
            V.tensor_copy(ident16[:], core.ident[:])
            V.tensor_copy(causal16[:], causal[:])
            dve.wait_ge(s["gt"], 1)
            V.tensor_copy(gates[:], bank[:, 6, 0:NT * 48].rearrange("p (t g) -> p t g", t=NT)).then_inc(s["gates"], 1)
            dve.wait_ge(s["gates"], 1)
            V.tensor_scalar(gates[:, 0, 0::3], gates[:, 0, 0::3], has_block[:, 0:1], None, ALU.mult).then_inc(s["gates"], 1)
            dve.wait_ge(s["gates"], 2)
            credit(dve, "masked", "nmax", "copied_v", "recip", "coef", "o_sel", "o")

            def maxima(i, u):
                kind, g, pair, head, t = STEPS[u]
                if kind == "turn":
                    return
                slot = u % 2
                at(dve, i, "scores", u)
                if kind == "cmp":
                    V.tensor_tensor(masked[:, slot], bank[:, 2 * slot, 0:NT * N_CMP].rearrange("p (t n) -> p t n", t=NT),
                                    cmp_neg[:], ALU.add).then_inc(s["masked"], 1)
                    at(dve, i, "masked", u)
                    V.reduce_max(nmax[:, slot], masked[:, slot], axis=AX.X, negate=True).then_inc(s["nmax"], 1)
                else:
                    V.reduce_max(nmax[:, slot, 0:2], bank[:, 2 * slot:2 * slot + 2, 0:(t + 1) * P], axis=AX.X,
                                 negate=True).then_inc(s["nmax"], 1)

            def copy(i, u):
                kind, g, pair, head, t = STEPS[u]
                if kind == "turn":
                    at(dve, i, "copied_a", u)
                    pi = one(4 * i + (2 * g + pair))
                    V.tensor_tensor(flat(ylo[:, pi]), bank[:, 4], flat(fp(yhi[:, pi])), ALU.subtract).then_inc(s["copied_v"], 1)
                elif kind == "main":
                    at(dve, i, "turned", u)
                    at(dve, i, "o_mm", u - 2)
                    n = (t + 1) * P
                    V.tensor_copy(pt[:, u % 2, 0, 0:n], bank[:, 4, 0:n]).then_inc(s["copied_v"], 1)

            def combine(i, u):
                kind, g, pair, head, t = STEPS[u]
                if kind == "turn":
                    return
                m = NT if kind == "cmp" else 2
                h3 = 24 * i + (12 * g + 6 * pair + 3 * head)
                at(dve, i, "o_mm", u)
                at(dve, i, "o", u - 1)
                V.reciprocal(rcp[:, 0:m], sums[:, u % 4, 0:m]).then_inc(s["recip"], 1)
                at(dve, i, "recip", u)
                if kind == "cmp":
                    gate = gates[:, :, one(h3)].rearrange("p t a -> p (t a)")
                else:
                    gate = gates[:, t, bass.ds(h3 + 1, 2)]
                V.tensor_tensor(coef[:, 0:m], rcp[:, 0:m], gate, ALU.mult).then_inc(s["coef"], 1)
                at(dve, i, "coef", u)
                if kind == "cmp":
                    V.tensor_tensor(osb[:, pair, :, C * head:C * head + C], bank[:, 6 + u % 2, 0:NT * C].rearrange("p (t d) -> p t d", t=NT),
                                    coef[:].rearrange("p (t a) -> p t a", a=1).to_broadcast([P, NT, C]), ALU.mult).then_inc(s["o"], 1)
                    return
                o = osb[:, pair, t, C * head:C * head + C]
                V.scalar_tensor_tensor(out=o, in0=bank[:, 6 + u % 2, 0:C], scalar=coef[:, 0:1], in1=o,
                                       op0=ALU.mult, op1=ALU.add).then_inc(s["o_sel"], 1)
                at(dve, i, "o_sel", u)
                V.scalar_tensor_tensor(out=o, in0=bank[:, 6 + u % 2, C:2 * C], scalar=coef[:, 1:2], in1=o,
                                       op0=ALU.mult, op1=ALU.add).then_inc(s["o"], 1)

            with dve.Fori(0, 2) as i:
                for u in range(U + 2):
                    if u < U:
                        maxima(i, u)
                    late = 1 <= u <= U and STEPS[u - 1][0] == "turn"
                    if 1 <= u <= U and not late:
                        copy(i, u - 1)
                    if u >= 2:
                        combine(i, u - 2)
                    if late:
                        copy(i, u - 1)
    close_stage(core, s)


def tile_pairs(view):
    return lambda i, j: view[j][one(i)].rearrange("a p t -> p (a t)")


def setup(core):
    nc, ins = core.nc, core.ins
    with ExitStack() as ctx:
        s, sb, ps = open_stage(core, ctx, "setup", ["const", "rows", "x", "turned", "copied", "filled"])
        nt = T // P
        tok = sb("tok", [P, nt, D])
        rows = sb("rows", [P, 2, P])
        turn = ps("turn", [P, 4, T])
        rest = core.rows - P
        block = ctx.enter_context(nc.Block())

        @block.sync
        def _(sp):
            sp.dma_start(core.ident[:], core.consts["c_ident"]).then_inc(s["const"], 16)
            sp.dma_start(core.head_ones[:], core.consts["c_head_ones"]).then_inc(s["const"], 16)
            for name in VECTORS:
                n = int(np.prod(ins[name].shape)) // P
                r = core.row[name]
                shape = ins[name].shape
                src = ins[name]
                axes = " ".join("abcd"[:len(shape)])
                src = src.rearrange(f"{axes} -> ({axes})") if len(shape) > 1 else src
                src = src.rearrange("(r p) -> r p", p=P)
                for tile in range(2):
                    lo, hi = max(r, tile * P), min(r + n, tile * P + P)
                    if lo < hi:
                        sp.dma_start(rows[lo - tile * P:hi - tile * P, tile], src[lo - r:hi - r]).then_inc(s["rows"], 16)
            core.row_loads = sum(1 + (core.row[v] < P < core.row[v] + int(np.prod(ins[v].shape)) // P) for v in VECTORS)

        @block.scalar
        def _(act):
            for t in range(nt):
                act.dma_start(tok[:, t], ins["x"].rearrange("b (t p) d -> t p (b d)", p=P)[t]).then_inc(s["x"], 16)
            for d in range(ND):
                act.wait_ge(s["turned"], d + 1)
                nc.scalar.activation(core.x[:, d], turn[:, d % 4], ACT.Copy).then_inc(s["copied"], 1)
            for tile, n in enumerate((P, rest)):
                act.wait_ge(s["turned"], ND + tile + 1)
                nc.scalar.activation(core.vecs[:, tile * P:tile * P + n], turn[:, tile, 0:n], ACT.Copy).then_inc(s["copied"], 1)

        @block.vector
        def _(dve):
            nc.vector.memset(core.ones[:], 1.0)
            nc.vector.memset(core.eps[:, 0:1], EPS)
            nc.vector.memset(core.eps[:, 1:2], GN_EPS)
            nc.vector.memset(core.zero[:], 0.0).then_inc(s["filled"], 1)

        @block.tensor
        def _(pe):
            pe.wait_ge(s["const"], 32)
            pe.wait_ge(s["x"], 16 * nt)
            for d in range(ND):
                if d >= 4:
                    pe.wait_ge(s["copied"], d - 3)
                for t in range(nt):
                    mm = nc.tensor.transpose(turn[:, d % 4, t * P:(t + 1) * P], tok[:, t, d * P:(d + 1) * P], core.ident[:])
                mm.then_inc(s["turned"], 1)
            pe.wait_ge(s["rows"], 16 * core.row_loads)
            for tile, n in enumerate((P, rest)):
                pe.wait_ge(s["copied"], ND - 3 + tile)
                nc.tensor.transpose(turn[:, tile, 0:n], rows[0:n, tile], core.ident[0:n, 0:n]).then_inc(s["turned"], 1)
    close_stage(core, s)


def finish(core, out):
    nc = core.nc
    with ExitStack() as ctx:
        s, sb, ps = open_stage(core, ctx, "finish", ["turned", "copied", "out"])
        nt = T // P
        tok = sb("tok", [P, nt, D])
        turn = ps("turn", [P, 4, T])
        block = ctx.enter_context(nc.Block())
        steps = [(t, q) for t in range(nt) for q in range(2)]

        @block.tensor
        def _(pe):
            for n, (t, q) in enumerate(steps):
                if n >= 4:
                    pe.wait_ge(s["copied"], n - 3)
                for j in range(4):
                    mm = nc.tensor.transpose(turn[:, n % 4, j * P:(j + 1) * P],
                                             core.x[:, 4 * q + j, t * P:(t + 1) * P], core.ident[:])
                mm.then_inc(s["turned"], 1)

        @block.scalar
        def _(act):
            for n, (t, q) in enumerate(steps):
                act.wait_ge(s["turned"], n + 1)
                nc.scalar.activation(tok[:, t, q * T:(q + 1) * T], turn[:, n % 4], ACT.Copy).then_inc(s["copied"], 1)

        @block.sync
        def _(sp):
            dst = out.rearrange("b (t p) d -> t p (b d)", p=P)
            for t in range(nt):
                sp.wait_ge(s["copied"], 2 * t + 2)
                sp.dma_start(dst[t], tok[:, t]).then_inc(s["out"], 16)
            sp.wait_ge(s["out"], 16 * nt)


def shared_kv(core, kv, k_rot, v_tok, k_cmp, v_cmp):
    ins = core.ins
    project(core, "kv", core.vec("kv_norm"), ins["kv_w"], kv)
    keys = kv[2 * KIND:].rearrange("(b x e p) t -> x e b p t", b=2, x=2, p=P)[0]
    rows = k_rot.rearrange("(b e p) t -> e b p t", b=2, p=P)
    rotate(core, "krot", tile_pairs(keys), 4, [ins["kv_k_norm"][1], ins["kv_k_norm"][2]], None, tile_pairs(rows))
    values(core, "val", kv, v_tok, k_cmp, v_cmp)


def queries_attend(core, shared, yhi, ylo):
    nc, ins = core.nc, core.ins
    scratch = lambda name, rows: nc.dram_tensor(name, (rows, T), F32).ap()
    qg, q_plain, q_rot = scratch("qg_scratch", D + 48), scratch("q_plain_scratch", D), scratch("q_rot_scratch", D)
    project(core, "q", core.vec("norm_mix", 1), ins["nsa_w_q"][0], qg)
    tiles = lambda view: tile_pairs(view.rearrange("(b e p) t -> e b p t", e=2, p=P))
    rotate(core, "qrot", tiles(qg[0:D]), ND, [ins["nsa_q_norm"][0]], tiles(q_plain), tiles(q_rot), scale=C ** -0.5)
    attention(core, "att", q_plain, q_rot, qg[D:], shared["k_rot"], shared["v_tok"], shared["k_cmp"], shared["v_cmp"], yhi, ylo)


def program(nc, ins, consts, out):
    with ExitStack() as ctx:
        core = Core(nc, ctx, ins, consts)
        scratch = lambda name, *shape: nc.dram_tensor(name, shape, F32).ap()
        half_ffn = lambda n, layer: ffn(core, f"ffn{n}_{layer}", core.vec(f"norm_ffn{n}", layer), ins[f"ffn{n}_w_gate"][layer],
                                        ins[f"ffn{n}_w_up"][layer], ins[f"ffn{n}_w_down"][layer])
        setup(core)
        half_ffn(1, 0)
        rkv = scratch("rkv_scratch", 3, D, T)
        with ExitStack() as mixing:
            hold = lambda name, shape, dt=F32: mixing.enter_context(nc.sbuf_tensor(name, shape, dt))
            lora = {n: hold(f"lora_{n}", [P, c, T]) for n, c in (("lw", 1), ("la", 1), ("lg", 2))}
            mix_project(core, "mix", rkv, lora)
            yhi, ylo = hold("y_hi", [P, ND, T], F32R), hold("y_lo", [P, ND, T], F32R)
            recurrence(core, "rec", rkv, lora, yhi, ylo)
            project_add(core, "rwo", yhi, ylo, ins["rw_w_o"][0])
        half_ffn(2, 0)
        shared = {"kv": scratch("kv_scratch", 6 * KIND, T), "k_rot": scratch("k_rot_scratch", 2 * KIND, T),
                  "v_tok": scratch("v_tok_scratch", 4, P, T), "k_cmp": scratch("k_cmp_scratch", C, G * N_CMP),
                  "v_cmp": scratch("v_cmp_scratch", G * N_CMP, C)}
        shared_kv(core, **shared)
        half_ffn(1, 1)
        with ExitStack() as mixing:
            hold = lambda name, shape, dt=F32: mixing.enter_context(nc.sbuf_tensor(name, shape, dt))
            yhi, ylo = hold("o_hi", [P, ND, T], F32R), hold("o_lo", [P, ND, T], F32R)
            queries_attend(core, shared, yhi, ylo)
            project_add(core, "nwo", yhi, ylo, ins["nsa_w_o"][0])
        half_ffn(2, 1)
        finish(core, out)


def constants():
    head = np.kron(np.eye(2), np.ones((64, 64)))
    a, b = np.arange(P)[:, None], np.arange(P)[None, :]
    same = a // C == b // C
    between = lambda n: (a // (2 * n) == b // (2 * n)) & ((a // n) % 2 == 1) & ((b // n) % 2 == 0)
    tables = {
        "c_ident": np.eye(P), "c_head_ones": head,
        "c_masks": np.stack([same & (a < b), same & (a <= b)], 1),
        "c_merge": np.stack([between(n) for n in LEVELS], 1),
        "c_first": np.stack([between(1), between(1).T], 1),
        "c_i64": a % C == np.arange(C)[None, :],
    }
    half = C // 2
    rate = (10000.0 ** (-np.arange(half) / half)).astype(np.float32)
    angle = (np.arange(T, dtype=np.float32)[None, :] * rate[:, None]).astype(np.float64)
    t, n = np.arange(T).reshape(NT, P).T[:, :, None], np.arange(N_CMP)[None, None, :]
    tables["c_causal"] = np.where(b > a, -1e30, 0.0)
    tables["c_cmp_neg"] = np.where(CMP_STRIDE * n + CMP_LEN - 1 > t, -1e30, 0.0)
    tables["c_has_block"] = (np.arange(P)[:, None] >= CMP_LEN - 1)
    tables["c_cos"] = np.tile(np.cos(angle), (4, 1))
    tables["c_sin"] = np.tile(np.concatenate([-np.sin(angle), np.sin(angle)]), (2, 1))
    tables["c_swap"] = (a // C == b // C) & ((a - b) % C == half)
    return {n: np.ascontiguousarray(t).astype(np.float32) for n, t in tables.items()}


_INS = ['x', 'norm_ffn1', 'ffn1_w_gate', 'ffn1_w_up', 'ffn1_w_down', 'norm_mix', 'norm_ffn2', 'ffn2_w_gate',
        'ffn2_w_up', 'ffn2_w_down', 'rw_mu', 'rw_w_rkv', 'rw_w0', 'rw_w_lora_a', 'rw_w_lora_b', 'rw_a0',
        'rw_a_lora_a', 'rw_a_lora_b', 'rw_g_lora_a', 'rw_g_lora_b', 'rw_k_k', 'rw_k_a', 'rw_r_k', 'rw_gn_w',
        'rw_gn_b', 'rw_w_o', 'kv_norm', 'kv_w', 'kv_k_norm', 'cmp_pos_k', 'cmp_k_w1', 'cmp_k_w2', 'cmp_pos_v',
        'cmp_v_w1', 'cmp_v_w2', 'nsa_w_q', 'nsa_q_norm', 'nsa_w_o']


def kernel(**inputs):
    import concourse.bacc as _bacc
    from concourse.bass_utils import run_bass_kernel_spmd as _run

    nc = _bacc.Bacc("TRN2", target_bir_lowering=False, num_devices=1)
    arrays = {f"in_{n}_dram": np.ascontiguousarray(inputs[n]) for n in _INS}
    arrays.update({f"in_{n}_dram": a for n, a in constants().items()})
    aps = {n[3:-5]: nc.dram_tensor(n, a.shape, mybir.dt.from_np(a.dtype), kind="ExternalInput").ap()
           for n, a in arrays.items()}
    out = nc.dram_tensor("out_0_dram", (1, T, D), F32, kind="ExternalOutput").ap()
    program(nc, {n: aps[n] for n in _INS}, {n: aps[n] for n in constants()}, out)
    r = _run(nc, [arrays], core_ids=[0])
    return r.results[0]["out_0_dram"]
```

```python
from contextlib import ExitStack

import numpy as np

import concourse.bass as bass
from concourse import mybir

ALU = mybir.AluOpType
ACT = mybir.ActivationFunctionType
AX = mybir.AxisListType
F32 = mybir.dt.float32
F32R = mybir.dt.float32r

P = 128
T = 512
D = 1024
ND = D // P
F = 2816
NF = F // P
KMAX = 8
SLOTS = 4
EPS = 1e-6
GN_EPS = 64e-5


def fp(view):
    return view.bitcast(F32)


VECTORS = ["norm_ffn1", "norm_mix", "norm_ffn2", "kv_norm", "rw_mu", "rw_w0", "rw_a0", "rw_k_k", "rw_k_a",
           "rw_r_k", "rw_gn_w", "rw_gn_b"]


class Core:

    def __init__(self, nc, ctx, ins, consts):
        self.nc, self.ins, self.consts = nc, ins, consts
        sb = lambda name, shape, dt=F32: ctx.enter_context(nc.sbuf_tensor(name, shape, dt))
        self.x = sb("x_res", [P, ND, T])
        self.ones = sb("ones", [P, P])
        self.head_ones = sb("head_ones", [P, P])
        self.ident = sb("ident", [P, P])
        self.eps = sb("eps", [P, 2])
        self.row, n = {}, 0
        for name in VECTORS:
            self.row[name] = n
            n += int(np.prod(ins[name].shape)) // P
        self.rows = n
        self.vecs = sb("vecs", [P, n])
        self.zero = sb("zero", [P, 1])

    def vec(self, name, index=0):
        r = self.row[name] + ND * index
        return self.vecs[:, r:r + ND]


def open_ring(core, sb):
    core.raw = sb("w_raw", [P, SLOTS, KMAX, P])
    core.whi = sb("w_hi", [P, SLOTS, KMAX, P], F32R)
    core.wlo = sb("w_lo", [P, SLOTS, KMAX, P], F32R)


def open_stage(core, ctx, tag, names):
    nc = core.nc
    s = {n: nc.alloc_semaphore(f"{n}_{tag}") for n in names}
    sb = lambda name, shape, dt=F32: ctx.enter_context(nc.sbuf_tensor(f"{name}_{tag}", shape, dt))
    ps = lambda name, shape: ctx.enter_context(nc.psum_tensor(f"{name}_{tag}", shape, F32))
    return s, sb, ps


def close_stage(core, s):
    nc = core.nc
    with nc.Block() as block:
        @block.sync
        def _(sp):
            for sem in s.values():
                sp.sem_clear(sem)
    for sem in s.values():
        nc.release_semaphore(sem)


def one(i):
    return bass.ds(i, 1)


def flat(view):
    return view.rearrange("p a t -> p (a t)")


def done(unit):
    return unit + (SLOTS + 1)


def load_unit(sp, s, core, slot, count, source):
    sp.wait_ge(s["w_ready"], count + 1)
    k = source.shape[1]
    sp.dma_start(core.raw[:, slot, 0:k, 0:source.shape[2]], source).then_inc(s[f"raw{slot}"], 16)


def split_unit(dve, s, core, slot, rounds, count, k, m=P):
    nc = core.nc
    dve.wait_ge(s[f"raw{slot}"], 16 * rounds + 16)
    dve.wait_ge(s["w_free"], count + 1)
    raw, hi, lo = (t[:, slot, 0:k, 0:m] for t in (core.raw, core.whi, core.wlo))
    nc.vector.tensor_copy(hi, raw).then_inc(s["w_hi"], 1)
    dve.wait_ge(s["w_hi"], count + 1)
    nc.vector.tensor_tensor(lo, raw, fp(hi), ALU.subtract).then_inc(s["w_ready"], 1)


def three_passes(core, out, slot, k, hi, lo, first, last):
    nc = core.nc
    whi, wlo = core.whi[:, slot, k], core.wlo[:, slot, k]
    nc.tensor.matmul(out, whi, hi, start=first, stop=False)
    nc.tensor.matmul(out, whi, lo, start=False, stop=False)
    return nc.tensor.matmul(out, wlo, hi, start=False, stop=last)


FFN_SEMS = ["raw0", "raw1", "raw2", "raw3", "w_free", "w_hi", "w_ready", "rstd", "h_lo", "h_hi", "h32", "sq",
            "sq_used", "ms", "gu_free", "down_free", "a_lo", "a_hi", "act32", "silu", "half_free", "ready"]


def ffn(core, tag, x_gain, w_gate, w_up, w_down):
    nc = core.nc
    groups = [(f0, min(KMAX, NF - f0)) for f0 in range(0, NF, KMAX)]
    gate = w_gate.rearrange("(k p) f -> p k f", p=P)
    up = w_up.rearrange("(k p) f -> p k f", p=P)
    down = w_down.rearrange("(k p) d -> p k d", p=P)
    with ExitStack() as ctx:
        s, sb, ps = open_stage(core, ctx, tag, FFN_SEMS)
        open_ring(core, sb)
        sq = sb("sq", [P, 2, T])
        ms = sb("ms", [P, T])
        rstd = sb("rstd", [P, T])
        h32 = sb("h32", [P, 2, T])
        hhi = sb("hhi", [P, ND, T], F32R)
        hlo = sb("hlo", [P, ND, T], F32R)
        gated = sb("gated", [P, T])
        upc = sb("upc", [P, T])
        act32 = sb("act32", [P, T])
        ahi = sb("ahi", [P, KMAX, T], F32R)
        alo = sb("alo", [P, KMAX, T], F32R)
        half = sb("half", [P, 2, T])
        p_gate = ps("p_gate", [P, 2, T])
        p_up = ps("p_up", [P, 2, T])
        p_down = ps("p_down", [P, 2, T])
        p_ms = ps("p_ms", [P, T])
        block = ctx.enter_context(nc.Block())

        @block.sync
        def _(sp):
            unit = 0
            for f0, nf in groups:
                with sp.Fori(0, nf // 2) as i:
                    for j in range(4):
                        w = gate if j % 2 == 0 else up
                        src = w[:, :, bass.ds(2 * P * i + (f0 + j // 2) * P, P)]
                        load_unit(sp, s, core, j, 4 * i + (unit + j), src)
                unit += 2 * nf
                with sp.Fori(0, ND // 4) as i:
                    for j in range(4):
                        src = down[:, f0:f0 + nf, bass.ds(4 * P * i + j * P, P)]
                        load_unit(sp, s, core, j, 4 * i + (unit + j), src)
                unit += ND

        @block.vector
        def _(dve):
            dve.sem_inc(s["w_ready"], SLOTS)
            norm_vector(core, dve, s, x_gain, ms, rstd, h32, hhi, hlo)
            unit = 0
            for f0, nf in groups:
                with dve.Fori(0, nf // 2) as i:
                    for j in range(4):
                        split_unit(dve, s, core, j, i + unit // 4, 4 * i + (unit + j), ND)
                unit += 2 * nf
                with dve.Fori(0, ND // 4) as i:
                    for j in range(4):
                        split_unit(dve, s, core, j, i + unit // 4, 4 * i + (unit + j), nf)
                unit += ND

        @block.tensor
        def _(pe):
            pe.sem_inc(s["w_free"], SLOTS)
            norm_tensor(core, pe, s, sq, p_ms)
            pe.wait_ge(s["h_lo"], ND)
            unit, ftile, dtile = 0, 0, 0
            for f0, nf in groups:
                with pe.Fori(0, nf // 2) as i:
                    for j in range(4):
                        out = (p_gate if j % 2 == 0 else p_up)[:, j // 2]
                        pe.wait_ge(s["w_ready"], done(4 * i + (unit + j)))
                        if j % 2 == 0:
                            pe.wait_ge(s["gu_free"], 2 * i + (ftile + j // 2 + 1))
                        for k in range(ND):
                            mm = three_passes(core, out, j, k, hhi[:, k], hlo[:, k], k == 0, k == ND - 1)
                        mm.then_inc(s["w_free"], 1)
                unit += 2 * nf
                ftile += nf
                with pe.Fori(0, ND // 4) as i:
                    for j in range(4):
                        out = p_down[:, j % 2]
                        pe.wait_ge(s["w_ready"], done(4 * i + (unit + j)))
                        pe.wait_ge(s["down_free"], 4 * i + (dtile + j + 1))
                        for k in range(nf):
                            if j == 0:
                                pe.wait_ge(s["a_lo"], f0 + k + 2)
                            mm = three_passes(core, out, j, k, ahi[:, k], alo[:, k], k == 0, k == nf - 1)
                        mm.then_inc(s["w_free"], 1)
                unit += ND
                dtile += ND

        @block.scalar
        def _(act):
            norm_scalar(core, act, s, sq, p_ms, ms, h32, hhi)
            act.sem_inc(s["gu_free"], 2)
            act.sem_inc(s["down_free"], 2)
            unit, ftile, dtile = 0, 0, 0
            for f0, nf in groups:
                with act.Fori(0, nf // 2) as i:
                    for j in range(2):
                        f = 2 * i + (ftile + j)
                        act.wait_ge(s["w_free"], done(4 * i + (unit + 2 * j + 1)))
                        act.wait_ge(s["act32"], f + 1)
                        nc.scalar.activation(gated[:], p_gate[:, j], ACT.Silu).then_inc(s["silu"], 1)
                        act.wait_ge(s["silu"], f + 1)
                        nc.scalar.activation(upc[:], p_up[:, j], ACT.Copy).then_inc(s["gu_free"], 1)
                        act.wait_ge(s["act32"], f + 2)
                        act.wait_ge(s["ready"], 1)
                        nc.scalar.activation(ahi[:, bass.ds(2 * i + j, 1)].rearrange("p a t -> p (a t)"), act32[:], ACT.Copy).then_inc(s["a_hi"], 1)
                unit += 2 * nf
                ftile += nf
                with act.Fori(0, ND // 4) as i:
                    for j in range(4):
                        act.wait_ge(s["w_free"], done(4 * i + (unit + j)))
                        act.wait_ge(s["half_free"], 4 * i + (dtile + j + 1))
                        nc.scalar.activation(half[:, j % 2], p_down[:, j % 2], ACT.Copy, scale=0.5).then_inc(s["down_free"], 1)
                unit += ND
                dtile += ND

        @block.gpsimd
        def _(pool):
            pool.sem_inc(s["act32"], 1)
            pool.sem_inc(s["a_lo"], 1)
            pool.sem_inc(s["half_free"], 2)
            pool.sem_inc(s["ready"], 1)
            ftile, dtile = 0, 0
            for f0, nf in groups:
                with pool.Fori(0, nf // 2) as i:
                    for j in range(2):
                        f = 2 * i + (ftile + j)
                        pool.wait_ge(s["gu_free"], f + 3)
                        pool.wait_ge(s["a_lo"], f + 1)
                        nc.gpsimd.tensor_tensor(act32[:], gated[:], upc[:], ALU.mult).then_inc(s["act32"], 1)
                        pool.wait_ge(s["a_hi"], f + 1)
                        pool.wait_ge(s["ready"], 1)
                        sl = bass.ds(2 * i + j, 1)
                        nc.gpsimd.tensor_tensor(alo[:, sl].rearrange("p a t -> p (a t)"), act32[:],
                                                fp(ahi[:, sl]).rearrange("p a t -> p (a t)"), ALU.subtract).then_inc(s["a_lo"], 1)
                ftile += nf
                with pool.Fori(0, ND // 4) as i:
                    for j in range(4):
                        pool.wait_ge(s["down_free"], 4 * i + (dtile + j + 3))
                        pool.wait_ge(s["ready"], 1)
                        xs = core.x[:, bass.ds(4 * i + j, 1)].rearrange("p a t -> p (a t)")
                        nc.gpsimd.tensor_tensor(xs, xs, half[:, j % 2], ALU.add).then_inc(s["half_free"], 1)
                dtile += ND
            pool.wait_ge(s["half_free"], 2 + dtile)
    close_stage(core, s)


PASSES = [("r", 0, ND), ("lw", 1, 1), ("k", 2, ND), ("la", 4, 1), ("v", 3, ND), ("lg", 5, 2)]
MAIN = ("r", "k", "v")

MIX_SEMS = ["raw0", "raw1", "raw2", "raw3", "w_free", "w_hi", "w_ready", "rstd", "h", "sq", "sq_used", "ms",
            "dx", "mix32", "mix_hi", "mix_lo", "out", "st0", "st1", "st2", "st3", "ready", "pad"]


def mix_project(core, tag, rkv, lora):
    nc, ins = core.nc, core.ins
    wide = [ins["rw_w_rkv"][0, c].rearrange("(k p) e -> p k e", p=P) for c in range(3)]
    narrow = {"lw": ins["rw_w_lora_a"][0], "la": ins["rw_a_lora_a"][0], "lg": ins["rw_g_lora_a"][0]}
    widths = {"lw": [narrow["lw"].shape[1]], "la": [narrow["la"].shape[1]], "lg": [P, narrow["lg"].shape[1] - P]}
    first, n = {}, 0
    for name, _, units in PASSES:
        first[name] = n
        n += units
    buf = {"r": 0, "lw": 1, "k": 2, "la": 1, "v": 0, "lg": 1}
    beside = {"r": ["lw", "k"], "k": ["la", "v"], "v": ["lg"]}
    began = {"r": ND, "k": 3 * ND, "v": 5 * ND}
    complete = {"lw": 3 * ND - 1, "k": 3 * ND, "la": 5 * ND - 1, "v": 5 * ND, "lg": 6 * ND}
    mu_row = {name: c for name, c, _ in PASSES}

    with ExitStack() as ctx:
        s, sb, ps = open_stage(core, ctx, tag, MIX_SEMS)
        open_ring(core, sb)
        h = sb("h", [P, ND, T + 1])
        dx = sb("dx", [P, 2, T])
        mix32 = sb("mix32", [P, 4, T])
        sq, ms, rstd = mix32[:, 0:2], dx[:, 0], dx[:, 1]
        mhi = sb("mhi", [P, 3, ND, T], F32R)
        mlo = sb("mlo", [P, 3, ND, T], F32R)
        staged = sb("staged", [P, 2, T])
        p_ms = ps("p_ms", [P, T])
        p_out = ps("p_out", [P, 4, T])
        block = ctx.enter_context(nc.Block())

        def units_of(eng, name, body):
            base, n = first[name], dict((a, c) for a, _, c in PASSES)[name]
            if name in MAIN:
                with eng.Fori(0, n // 4) as i:
                    for j in range(4):
                        body(4 * i + (base + j), (base + j) % 4, i + (base + j) // 4, 4 * i + j, j)
            else:
                for j in range(n):
                    body(base + j, (base + j) % 4, (base + j) // 4, j, j)

        @block.sync
        def _(sp):
            for name, _, n in PASSES:
                def load(unit, slot, rounds, e, j):
                    if name in MAIN:
                        src = wide[MAIN.index(name)][:, :, bass.ds(e * P, P)]
                    else:
                        m = widths[name][j]
                        src = narrow[name].rearrange("(k p) e -> p k e", p=P)[:, :, j * P:j * P + m]
                    load_unit(sp, s, core, slot, unit, src)
                units_of(sp, name, load)

        @block.vector
        def _(dve):
            dve.sem_inc(s["w_ready"], SLOTS)
            dve.sem_inc(s["ready"], 1)
            nc.vector.memset(h[:, :, 0:1], 0.0).then_inc(s["pad"], 1)
            dve.wait_ge(s["ms"], 1)
            nc.vector.reciprocal(rstd[:], ms[:]).then_inc(s["rstd"], 1)
            dve.wait_ge(s["rstd"], 1)
            gain = core.vec("norm_mix", 0)
            for d in range(ND):
                nc.vector.scalar_tensor_tensor(out=h[:, d, 1:T + 1], in0=core.x[:, d], scalar=gain[:, d:d + 1],
                                               in1=rstd[:], op0=ALU.mult, op1=ALU.mult).then_inc(s["h"], 1)
            dve.wait_ge(s["h"], ND)
            dve.wait_ge(s["pad"], 1)

            def mix_tile(name, m, slot, d):
                mu = core.vec("rw_mu", mu_row[name])
                mu = mu[:, d:d + 1] if isinstance(d, int) else mu[:, one(d)]
                hd = h[:, d:d + 1] if isinstance(d, int) else h[:, one(d)]
                dve.wait_ge(s["mix_hi"], m + 1)
                nc.vector.tensor_tensor(dx[:, slot % 2], flat(hd[:, :, 0:T]), flat(hd[:, :, 1:T + 1]),
                                        ALU.subtract).then_inc(s["dx"], 1)
                dve.wait_ge(s["dx"], m + 1)
                dve.wait_ge(s["mix_lo"], m + 1)
                nc.vector.scalar_tensor_tensor(out=mix32[:, slot], in0=dx[:, slot % 2], scalar=mu,
                                               in1=flat(hd[:, :, 1:T + 1]), op0=ALU.mult, op1=ALU.add).then_inc(s["mix32"], 1)

            for d in range(ND):
                mix_tile("r", d, d % 4, d)
            for name, _, n in PASSES:
                def step(unit, slot, rounds, e, j):
                    m = P if name in MAIN else widths[name][j]
                    split_unit(dve, s, core, slot, rounds, unit, ND, m)
                    for b, other in enumerate(beside.get(name, [])):
                        made = len(beside[name])
                        mix_tile(other, e * made + (began[name] + b), (made * j + b) % 4, e)
                units_of(dve, name, step)

        @block.scalar
        def _(act):
            act.sem_inc(s["mix_hi"], 4)
            act.sem_inc(s["out"], 4)
            for d in range(ND):
                if d >= 2:
                    act.wait_ge(s["sq_used"], d - 1)
                nc.scalar.activation(sq[:, d % 2], core.x[:, d], ACT.Square).then_inc(s["sq"], 1)
            act.wait_ge(s["sq_used"], ND)
            nc.scalar.activation(ms[:], p_ms[:], ACT.Sqrt, scale=1.0 / D, bias=core.eps[:, 0:1]).then_inc(s["ms"], 1)

            def round_tile(name, m, slot, d):
                act.wait_ge(s["mix32"], m + 1)
                act.wait_ge(s["ready"], 1)
                dst = mhi[:, buf[name], d] if isinstance(d, int) else flat(mhi[:, buf[name], one(d)])
                nc.scalar.activation(dst, mix32[:, slot], ACT.Copy).then_inc(s["mix_hi"], 1)

            for d in range(ND):
                round_tile("r", d, d % 4, d)
            for name, _, n in PASSES:
                def step(unit, slot, rounds, e, j):
                    for b, other in enumerate(beside.get(name, [])):
                        made = len(beside[name])
                        round_tile(other, e * made + (began[name] + b), (made * j + b) % 4, e)
                    act.wait_ge(s["w_free"], done(unit))
                    if name in MAIN:
                        before = MAIN.index(name) * ND
                        turn = j % 2
                        act.wait_ge(s[f"st{turn}"], 8 * e + (8 * before - 8 * turn + 16))
                        nc.scalar.activation(staged[:, turn], p_out[:, slot], ACT.Copy).then_inc(s["out"], 1)
                        act.wait_ge(s["out"], unit + 5)
                        dst = rkv[MAIN.index(name)].rearrange("(e p) t -> e p t", p=P)[one(e)].rearrange("a p t -> p (a t)")
                        act.dma_start(dst, staged[:, turn]).then_inc(s[f"st{turn}"], 16)
                    else:
                        m = widths[name][j]
                        func = {"lw": ACT.Tanh, "la": ACT.Copy, "lg": ACT.Sigmoid}[name]
                        nc.scalar.activation(lora[name][0:m, j], p_out[0:m, slot], func).then_inc(s["out"], 1)
                units_of(act, name, step)
            for turn in range(2):
                act.wait_ge(s[f"st{turn}"], 16 * (3 * ND // 2 + 1))

        @block.gpsimd
        def _(pool):
            pool.sem_inc(s["mix_lo"], 4)
            pool.sem_inc(s["st0"], 16)
            pool.sem_inc(s["st1"], 16)

            def low_tile(name, m, slot, d):
                pool.wait_ge(s["mix_hi"], m + 5)
                pool.wait_ge(s["ready"], 1)
                if isinstance(d, int):
                    dst, hi = mlo[:, buf[name], d], fp(mhi[:, buf[name], d])
                else:
                    dst, hi = flat(mlo[:, buf[name], one(d)]), flat(fp(mhi[:, buf[name], one(d)]))
                nc.gpsimd.tensor_tensor(dst, mix32[:, slot], hi, ALU.subtract).then_inc(s["mix_lo"], 1)

            for d in range(ND):
                low_tile("r", d, d % 4, d)
            for name in MAIN:
                def step(unit, slot, rounds, e, j):
                    for b, other in enumerate(beside[name]):
                        made = len(beside[name])
                        low_tile(other, e * made + (began[name] + b), (made * j + b) % 4, e)
                units_of(pool, name, step)

        @block.tensor
        def _(pe):
            pe.sem_inc(s["w_free"], SLOTS)
            for d in range(ND):
                pe.wait_ge(s["sq"], d + 1)
                nc.tensor.matmul(p_ms[:], core.ones[:], sq[:, d % 2], start=(d == 0), stop=(d == ND - 1)).then_inc(s["sq_used"], 1)
            for name, _, n in PASSES:
                if name in complete:
                    pe.wait_ge(s["mix_lo"], complete[name] + 4)
                def step(unit, slot, rounds, e, j):
                    pe.wait_ge(s["w_ready"], done(unit))
                    pe.wait_ge(s["out"], unit + 1)
                    for k in range(ND):
                        if name == "r" and j == 0:
                            pe.wait_ge(s["mix_lo"], k + 5)
                        mm = three_passes(core, p_out[:, slot], slot, k, mhi[:, buf[name], k], mlo[:, buf[name], k],
                                          k == 0, k == ND - 1)
                    mm.then_inc(s["w_free"], 1)
                units_of(pe, name, step)
    close_stage(core, s)


PAIR_EVENTS = {
    "loaded": 16 * 3, "lora_w": 16 * 4, "cur": 1, "zp": 1, "ap": 1, "tw": 1, "ta": 1, "sqk": 1, "ssk": 1, "clip": 1, "lnk": 1,
    "inv": 1, "sg": 1, "cum": 1, "ctr": 1, "qsum": 1, "cc": 1, "ce": 1, "eex": 1, "ep": 1, "em": 1, "q": 1, "pk": 6,
    "tilde": 4, "rk": 1, "bsum": 1, "bon": 1, "gp": 1, "gsb": 1, "vturn": 1, "vtok": 1, "turn": 3, "tok": 3,
    "score": 6, "bl": 4, "kl": 4, "nm": 2, "x_init": 6, "lakv": 1, "aw": 1, "g_mm": 10, "g": 10,
    "x_mm": 10, "x": 10, "au_mm": 2, "au": 2, "rp_mm": 1, "rp": 1, "f_mm": 1, "f": 2, "z_mm": 1, "z": 2,
    "chain": 6, "state": 6, "y_mm": 1, "ysb": 1, "mean": 1, "dev": 1, "sqy": 1, "var": 1, "lny": 1, "rs": 1,
    "yn": 3, "yhi": 1, "pair": 1, "pad": 4,
}
PARTS, FINISH_PARTS = 6, 3
C = 64
NC_ = T // C
NT = T // P
KAPPA = float(np.exp(-0.5))
LEVELS = (2, 4, 8, 16, 32)
LN_SCALE = 2.0 ** 16
W0H, A0H, KK, HKA, OKA, RK, GNW, GNB = range(8)


def recurrence(core, tag, rkv, lora, yhi, ylo):
    nc, ins = core.nc, core.ins
    with ExitStack() as ctx:
        s, sb, ps = open_stage(core, ctx, tag, list(PAIR_EVENTS) + ["ready", "consts", "pv"])

        def at(eng, p, name, k):
            eng.wait_ge(s[name], p * PAIR_EVENTS[name] + k)

        def plain(eng):
            eng.sem_inc(s["ready"], 1)

        def steps(eng, prepare, step, finish):
            for part in range(PARTS):
                prepare(0, 0, part)
            step(0, 0, True, False)
            with eng.Fori(0, ND // 2 - 1) as i:
                step(2 * i + 1, 1, False, False)
                step(2 * i + 2, 0, False, False)
            step(ND - 1, 1, False, True)
            for part in range(FINISH_PARTS):
                finish(ND - 1, 1, part)

        row = lambda name: sb(name, [P, T])
        slots = lambda name, shape: [sb(f"{name}{n}", shape) for n in range(2)]
        masks = sb("masks", [P, 2, P])
        merge = sb("merge", [P, 5, P])
        first_level = sb("first", [P, 2, P])
        i64 = sb("i64", [P, C])
        resets = row("resets")
        half_log = sb("half_log", [P, 1])
        pv = sb("pv", [P, ND, 8])
        cur = slots("cur", [P, 8])
        r, k, v = row("r"), row("k"), row("v")
        wb, ab, gb = sb("wb", [C, P]), sb("ab", [C, P]), sb("gb", [P, 2, P])
        sg, cum, cc, ce = row("sg"), row("cum"), row("cc"), row("ce")
        ta = row("ta")
        tw = sg
        ctr, qs, q = sb("ctr", [P, NC_]), sb("qs", [P, NC_]), slots("q", [P, NC_])
        eex, ep, em = row("eex"), row("ep"), row("em")
        sqk, kk0, kf, kp, a1 = (row(n) for n in ("sqk", "kk0", "kf", "kp", "a1"))
        inv = sqk
        kk, beta = kk0, a1
        rk, bon, gsb = row("rk"), slots("bon", [P, T]), slots("gsb", [P, T])
        ar = slots("ar", [P, NT, 2, P])
        bt, kt = row("bt"), row("kt")
        bz = [sb(f"bz{h}", [P, T]) for h in range(2)]
        kz = [sb(f"kz{h}", [P, T]) for h in range(2)]
        vtok, btok, ktok = (slots(n, [P, NT, P]) for n in ("vtok", "btok", "ktok"))
        aw = slots("aw", [P, NT, 2, P])
        bl = [sb(f"bl{h}", [P, NT, 2, P]) for h in range(2)]
        kl = [sb(f"kl{h}", [P, NT, 2, P]) for h in range(2)]
        x = [sb(f"x{h}", [P, NT, P]) for h in range(2)]
        xt = [sb(f"xt{h}", [P, NT, P]) for h in range(2)]
        g = [sb(f"g{h}", [P, NT, P]) for h in range(2)]
        au = g
        rp, ft, zq, st = row("rp"), sb("ft", [P, NC_, C]), sb("zq", [P, NC_, C]), sb("st", [P, NC_, C])
        ysb, rs = row("ysb"), row("rs")
        dev, sqy, yn = ysb, rs, ysb
        bank = ps("bank", [P, 8, T])
        block = ctx.enter_context(nc.Block())

        def tiles(view):
            return view.rearrange("p (t c) -> p t c", t=NT)

        @block.sync
        def _(sp):
            for dst, name in ((masks, "c_masks"), (merge, "c_merge"), (first_level, "c_first")):
                sp.dma_start(dst[:], core.consts[name]).then_inc(s["consts"], 16)
            sp.dma_start(i64[:], core.consts["c_i64"]).then_inc(s["consts"], 16)

            def load(p, first):
                if not first:
                    at(sp, p - 1, "bon", 1)
                    at(sp, p - 1, "tilde", 4)
                    at(sp, p - 1, "pk", 4)
                    at(sp, p - 1, "sqk", 1)
                for c, dst in enumerate((r, k, v)):
                    src = rkv[c].rearrange("(e p) t -> e p t", p=P)[one(p)].rearrange("a p t -> p (a t)")
                    sp.dma_start(dst[:], src).then_inc(s["loaded"], 16)
                if not first:
                    at(sp, p - 1, "gsb", 1)
                cols = bass.ds(p * P, P)
                for dst, src in ((wb[:], ins["rw_w_lora_b"][0][:, cols]), (ab[:], ins["rw_a_lora_b"][0][:, cols]),
                                 (gb[:, 0], ins["rw_g_lora_b"][0][0:P, cols]),
                                 (gb[0:32, 1], ins["rw_g_lora_b"][0][P:P + 32, cols])):
                    sp.dma_start(dst, src).then_inc(s["lora_w"], 16)

            load(0, True)
            with sp.Fori(0, ND - 1) as i:
                load(i + 1, False)

        @block.tensor
        def _(pe):
            pe.wait_ge(s["consts"], 64)

            def prepare(p, slot, part):
                if part == 0:
                    at(pe, p, "lora_w", 64)
                    if not (isinstance(p, int) and p == 0):
                        at(pe, p - 1, "nm", 2)
                        at(pe, p - 1, "aw", 1)
                    nc.tensor.matmul(bank[:, 4], wb[:], lora["lw"][0:C, 0], start=True, stop=True).then_inc(s["zp"], 1)
                    nc.tensor.matmul(bank[:, 5], ab[:], lora["la"][0:C, 0], start=True, stop=True).then_inc(s["ap"], 1)
                if part == 1:
                    at(pe, p, "sqk", 1)
                    at(pe, p, "tw", 1)
                    nc.tensor.matmul(bank[:, 4], core.head_ones[:], sqk[:], start=True, stop=True).then_inc(s["ssk"], 1)
                    at(pe, p, "ta", 1)
                    nc.tensor.matmul(bank[:, 5], gb[:, 0], lora["lg"][:, 0], start=True, stop=False)
                    nc.tensor.matmul(bank[:, 5], gb[0:32, 1], lora["lg"][0:32, 1], start=False, stop=True).then_inc(s["gp"], 1)
                if part == 2:
                    at(pe, p, "loaded", 48)
                    at(pe, p, "clip", 1)
                    for t in range(NT):
                        mm = nc.tensor.transpose(bank[:, 4, t * P:(t + 1) * P], v[:, t * P:(t + 1) * P], core.ident[:])
                    mm.then_inc(s["vturn"], 1)
                if part == 3:
                    at(pe, p, "rk", 1)
                    at(pe, p, "gsb", 1)
                    nc.tensor.matmul(bank[:, 5], core.head_ones[:], rk[:], start=True, stop=True).then_inc(s["bsum"], 1)
                if part >= 4:
                    for n, src in ((0, ar[slot][:, :, 0]), (1, tiles(bt[:])), (2, tiles(kt[:]))):
                        if (n == 2) != (part == 5):
                            continue
                        at(pe, p, "tilde", 4)
                        at(pe, p, *(("vtok", 1), ("bon", 1), ("tok", 1))[n])
                        for t in range(NT):
                            mm = nc.tensor.transpose(bank[:, 4 + n % 2, t * P:(t + 1) * P], src[:, t], core.ident[:])
                        mm.then_inc(s["turn"], 1)

            def finish(p, slot, part):
                if part == 0:
                    at(pe, p, "ysb", 1)
                    nc.tensor.matmul(bank[:, 6], core.head_ones[:], ysb[:], start=True, stop=True).then_inc(s["mean"], 1)
                if part == 1:
                    at(pe, p, "sqy", 1)
                    nc.tensor.matmul(bank[:, 6], core.head_ones[:], sqy[:], start=True, stop=True).then_inc(s["var"], 1)

            def step(p, slot, first, last):
                A, V_, B_, K_ = ar[slot], vtok[slot], btok[slot], ktok[slot]
                at(pe, p, "tilde", 4)
                at(pe, p, "pad", 4)
                at(pe, p, "tok", 3)
                for h in range(2):
                    for n, rhs in enumerate((bz, kz)):
                        if h == 1:
                            at(pe, p, "bl" if n == 0 else "kl", 2)
                        for t in range(NT):
                            out = bank[:, 2 * n + t // 2, (t % 2) * 2 * P:(t % 2 + 1) * 2 * P]
                            mm = nc.tensor.matmul(out, rhs[h][:, t * P:(t + 1) * P], A[:, t].rearrange("p a c -> p (a c)"),
                                                  start=True, stop=True)
                        mm.then_inc(s["score"], 1)
                        if n == 0 and not first:
                            finish(p - 1, 1 - slot, h)
                    for t in range(NT):
                        mm = nc.tensor.matmul(bank[:, 4 if h == 0 else 7, t * P:(t + 1) * P], A[:, t, 0],
                                              bz[h][:, t * P:(t + 1) * P], start=True, stop=True)
                    mm.then_inc(s["score"], 1)
                at(pe, p, "kl", 4)
                for h in range(2):
                    for t in range(NT):
                        mm = nc.tensor.matmul(bank[:, 5, (t * 2 + h) * C:(t * 2 + h + 1) * C], kl[h][:, t, 0],
                                              V_[:, t, C * h:C * h + C], start=True, stop=True)
                mm.then_inc(s["lakv"], 1)
                for level in range(len(LEVELS)):
                    over = level == len(LEVELS) - 1
                    for h in range(2):
                        if level == 0:
                            at(pe, p, "x_init", 3 * h + 3)
                            at(pe, p, "nm", h + 1)
                            at(pe, p, "bl", 4)
                            if h == 0 and not first:
                                at(pe, p - 1, "lny", 1)
                        else:
                            at(pe, p, "x", 2 * (level - 1) + h + 1)
                        for t in range(NT):
                            mm = nc.tensor.matmul(bank[:, 6 + h, t * P:(t + 1) * P], bl[h][:, t, 0], x[h][:, t], start=True, stop=True)
                        mm.then_inc(s["g_mm"], 1)
                    if not last:
                        prepare(p + 1, 1 - slot, level)
                    for h in range(2):
                        at(pe, p, "g", 2 * level + h + 1)
                        for t in range(NT):
                            cs = slice(t * P, (t + 1) * P)
                            mm = nc.tensor.matmul(bank[:, 2 * h + 1, cs], g[h][:, t], xt[h][:, t], start=True, stop=True)
                            if not over:
                                mm = nc.tensor.matmul(bank[:, 2 * h, cs], xt[h][:, t], g[h][:, t], start=True, stop=True)
                        mm.then_inc(s["x_mm"], 1)
                if not last:
                    prepare(p + 1, 1 - slot, PARTS - 1)
                at(pe, p, "aw", 1)
                for h in range(2):
                    at(pe, p, "x", 8 + h + 1)
                    for t in range(NT):
                        mm = nc.tensor.matmul(bank[:, 6 + h, t * P:(t + 1) * P], xt[h][:, t], aw[slot][:, t, h], start=True, stop=True)
                    mm.then_inc(s["au_mm"], 1)
                for h in range(2):
                    at(pe, p, "au", h + 1)
                    for t in range(NT):
                        mm = nc.tensor.matmul(bank[C * h:C * h + C, 0, t * P:(t + 1) * P], au[h][:, t, 0:C], bl[h][:, t, 1],
                                              start=True, stop=True)
                mm.then_inc(s["rp_mm"], 1)
                for h in range(2):
                    for c in range(NC_):
                        cp = slice(C * (c % 2), C * (c % 2) + C)
                        mm = nc.tensor.matmul(bank[C * h:C * h + C, 1 + 2 * (c % 2), c * C:(c + 1) * C], au[h][cp, c // 2, 0:C],
                                              B_[cp, c // 2, C * h:C * h + C], start=True, stop=True)
                mm.then_inc(s["f_mm"], 1)
                if not last:
                    at(pe, p + 1, "tok", 3)
                    plain(pe)
                for h in range(2):
                    hc = slice(C * h, C * h + C)
                    for c in range(NC_):
                        cp = slice(C * (c % 2), C * (c % 2) + C)
                        out = bank[hc, 2 + 2 * (c % 2), c * C:(c + 1) * C]
                        nc.tensor.matmul(out, B_[cp, c // 2, hc], au[h][cp, c // 2, C:P], start=True, stop=False)
                        mm = nc.tensor.matmul(out, K_[cp, c // 2, hc], V_[cp, c // 2, hc], start=False, stop=True)
                mm.then_inc(s["z_mm"], 1)

                def chain(c):
                    at(pe, p, "f", 2)
                    if c == 1:
                        at(pe, p, "z", 2)
                    else:
                        at(pe, p, "state", c - 1)
                    plain(pe)
                    for h in range(2):
                        hp = slice(C * h, C * h + C)
                        state = zq[hp, 0] if c == 1 else st[hp, c]
                        mm = nc.tensor.matmul(bank[hp, 4, c * C:(c + 1) * C], ft[hp, c], state, start=True, stop=True)
                    mm.then_inc(s["chain"], 1)

                def outputs(t):
                    at(pe, p, "rp", 1)
                    if t:
                        at(pe, p, "state", 2 * t)
                    for h in range(2):
                        hp = slice(C * h, C * h + C)
                        out = bank[hp, 5, t * P:(t + 1) * P]
                        nc.tensor.matmul(out, V_[:, t, hp], kl[h][:, t, 1], start=True, stop=False)
                        nc.tensor.matmul(out, au[h][:, t, C:P], bl[h][:, t, 1], start=False, stop=False)
                        for c in (2 * t, 2 * t + 1):
                            if c:
                                state = zq[hp, 0] if c == 1 else st[hp, c]
                                mm = nc.tensor.matmul(bank[hp, 5, c * C:(c + 1) * C], state, rp[hp, c * C:(c + 1) * C],
                                                      start=False, stop=(c % 2 == 1))
                    return mm

                chain(1)
                outputs(0)
                for c in (2, 3, 4, 5, 6):
                    chain(c)
                    if c in (3, 5):
                        outputs(c // 2)
                outputs(3).then_inc(s["y_mm"], 1)

            steps(pe, prepare, step, finish)

        @block.scalar
        def _(act):
            A = nc.scalar.activation

            def prepare(p, slot, part):
                c = cur[slot]
                if part == 0:
                    at(act, p, "cur", 1)
                    at(act, p, "loaded", 48)
                    A(sqk[:], k[:], ACT.Square, scale=c[:, KK:KK + 1]).then_inc(s["sqk"], 1)
                    at(act, p, "zp", 1)
                    A(tw[:], bank[:, 4], ACT.Tanh, scale=0.5, bias=c[:, W0H:W0H + 1]).then_inc(s["tw"], 1)
                    at(act, p, "ap", 1)
                    A(ta[:], bank[:, 5], ACT.Tanh, scale=0.5, bias=c[:, A0H:A0H + 1]).then_inc(s["ta"], 1)
                if part == 1:
                    at(act, p, "gp", 1)
                    A(gsb[slot][:], bank[:, 5], ACT.Copy).then_inc(s["gsb"], 1)
                    at(act, p, "clip", 1)
                    A(inv[:], sqk[:], ACT.Ln, scale=LN_SCALE).then_inc(s["lnk"], 1)
                    at(act, p, "lnk", 1)
                    A(inv[:], inv[:], ACT.Exp, scale=-0.5, bias=half_log[:, 0:1]).then_inc(s["inv"], 1)
                if part == 2:
                    at(act, p, "ce", 1)
                    A(eex[:], ce[:], ACT.Exp, scale=-KAPPA).then_inc(s["eex"], 1)
                    A(ep[:], cc[:], ACT.Exp, scale=-KAPPA).then_inc(s["ep"], 1)
                    A(em[:], cc[:], ACT.Exp, scale=KAPPA).then_inc(s["em"], 1)
                    at(act, p, "qsum", 1)
                    A(q[slot][:], qs[:], ACT.Exp, scale=-KAPPA).then_inc(s["q"], 1)
                    at(act, p, "vturn", 1)
                    A(vtok[slot][:].rearrange("p t c -> p (t c)"), bank[:, 4], ACT.Copy).then_inc(s["vtok"], 1)
                if part == 4:
                    at(act, p, "turn", 1)
                    A(aw[slot][:, :, :, 0:C], bank[:, 4].rearrange("p (t h c) -> p t h c", t=NT, h=2), ACT.Copy).then_inc(s["tok"], 1)
                    at(act, p, "turn", 2)
                    A(btok[slot][:].rearrange("p t c -> p (t c)"), bank[:, 5], ACT.Copy).then_inc(s["tok"], 1)
                if part == 5:
                    at(act, p, "turn", 3)
                    A(ktok[slot][:].rearrange("p t c -> p (t c)"), bank[:, 4], ACT.Copy).then_inc(s["tok"], 1)

            def finish(p, slot, part):
                if part == 0:
                    at(act, p, "y_mm", 1)
                    at(act, p, "pair", 1)
                    A(ysb[:], bank[:, 5], ACT.Copy).then_inc(s["ysb"], 1)
                    at(act, p, "dev", 1)
                    A(sqy[:], dev[:], ACT.Square).then_inc(s["sqy"], 1)
                if part == 1:
                    at(act, p, "var", 1)
                    A(rs[:], bank[:, 6], ACT.Ln, scale=1.0 / C, bias=core.eps[:, 1:2]).then_inc(s["lny"], 1)
                    at(act, p, "lny", 1)
                    A(rs[:], rs[:], ACT.Exp, scale=-0.5).then_inc(s["rs"], 1)
                if part == 2:
                    at(act, p, "yn", 3)
                    plain(act)
                    A(flat(yhi[:, one(p)]), yn[:], ACT.Copy).then_inc(s["yhi"], 1)

            def step(p, slot, first, last):
                if not first:
                    finish(p - 1, 1 - slot, 0)
                    finish(p - 1, 1 - slot, 1)
                at(act, p, "lakv", 1)
                A(aw[slot][:, :, :, C:P], bank[:, 5].rearrange("p (t h c) -> p t h c", t=NT, h=2), ACT.Copy).then_inc(s["aw"], 1)
                for part in range(PARTS):
                    if part == 1 and not first:
                        finish(p - 1, 1 - slot, 2)
                    if not last:
                        prepare(p + 1, 1 - slot, part)
                for h in range(2):
                    at(act, p, "au_mm", h + 1)
                    A(au[h][:].rearrange("p t c -> p (t c)"), bank[:, 6 + h], ACT.Copy).then_inc(s["au"], 1)

            steps(act, prepare, step, finish)

        @block.gpsimd
        def _(pool):
            G = nc.gpsimd
            pool.sem_inc(s["pair"], 1)
            eye = core.ident[:].rearrange("p (a c) -> p a c", a=1).to_broadcast([P, NT, P])

            def prepare(p, slot, part):
                c = cur[slot]
                if part == 0:
                    at(pool, p, "cur", 1)
                    at(pool, p, "loaded", 48)
                    plain(pool)
                    G.tensor_scalar(kk0[:], k[:], c[:, KK:KK + 1], None, ALU.mult).then_inc(s["pk"], 1)
                    at(pool, p, "ta", 1)
                    plain(pool)
                    G.tensor_scalar(kf[:], ta[:], c[:, HKA:HKA + 1], c[:, OKA:OKA + 1], ALU.mult, ALU.add).then_inc(s["pk"], 1)
                    G.tensor_scalar(a1[:], ta[:], 0.5, 0.5, ALU.mult, ALU.add).then_inc(s["pk"], 1)
                    at(pool, p, "pk", 2)
                    G.tensor_tensor(kp[:], k[:], kf[:], ALU.mult).then_inc(s["pk"], 1)
                if part == 1:
                    at(pool, p, "pk", 3)
                    at(pool, p, "inv", 1)
                    G.tensor_tensor(kk[:], kk0[:], inv[:], ALU.mult).then_inc(s["pk"], 1)
                    at(pool, p, "pk", 5)
                    G.tensor_tensor(beta[:], kk[:], a1[:], ALU.mult).then_inc(s["pk"], 1)
                if part == 3:
                    at(pool, p, "tilde", 4)
                    plain(pool)
                    for src, dst in ((bt, bz), (kt, kz)):
                        for h in range(2):
                            G.tensor_scalar(dst[h][:], src[:], core.head_ones[:, C * h:C * h + 1], None, ALU.mult).then_inc(s["pad"], 1)

            def finish(p, slot, part):
                if part == 2:
                    at(pool, p, "yhi", 1)
                    plain(pool)
                    G.tensor_tensor(flat(ylo[:, one(p)]), yn[:], flat(fp(yhi[:, one(p)])), ALU.subtract).then_inc(s["pair"], 1)

            def step(p, slot, first, last):
                for h in range(2):
                    m = first_level[:, 1:2].to_broadcast([P, NT, P])
                    at(pool, p, "bl", 2 * h + 2)
                    G.tensor_tensor(xt[h][:], bl[h][:, :, 0], m, ALU.mult).then_inc(s["x_init"], 1)
                    at(pool, p, "x_init", 3 * h + 1)
                    G.tensor_tensor(xt[h][:], xt[h][:], eye, ALU.add).then_inc(s["x_init"], 1)
                    at(pool, p, "nm", h + 1)
                    G.tensor_tensor(x[h][:], x[h][:], eye, ALU.add).then_inc(s["x_init"], 1)
                for part in range(PARTS):
                    if not last:
                        prepare(p + 1, 1 - slot, part)
                    if part == 0 and not first:
                        finish(p - 1, 1 - slot, 2)

            steps(pool, prepare, step, finish)
            pool.wait_ge(s["pair"], ND + 1)

        @block.vector
        def _(dve):
            V = nc.vector
            TT = V.tensor_tensor
            V.memset(half_log[:], 0.5 * float(np.log(LN_SCALE)))
            V.memset(resets[:], 1.0).then_inc(s["pv"], 1)
            dve.wait_ge(s["pv"], 1)
            V.memset(resets[:].rearrange("p (c t) -> p c t", t=C)[:, :, 0:1], 0.0)
            for c, name, a in ((W0H, "rw_w0", 0.5), (A0H, "rw_a0", 0.5), (KK, "rw_k_k", 1.0), (HKA, "rw_k_a", 0.5),
                               (RK, "rw_r_k", 1.0), (GNW, "rw_gn_w", 1.0), (GNB, "rw_gn_b", 1.0)):
                V.tensor_scalar(pv[:, :, c], core.vec(name), a, None, ALU.mult)
            V.tensor_scalar(pv[:, :, OKA], core.vec("rw_k_a"), -0.5, 1.0, ALU.mult, ALU.add).then_inc(s["pv"], 1)
            dve.wait_ge(s["pv"], 2)
            dve.wait_ge(s["consts"], 64)
            by_chunk = lambda view: view.rearrange("p (c t) -> p c t", t=C)
            spread = lambda view: view.rearrange("p (c a) -> p c a", a=1).to_broadcast([P, NC_, C])
            two_masks = masks[:].rearrange("p a c -> p (a c)").rearrange("p (o n) -> p o n", o=1).to_broadcast([P, 2, 2 * P])

            def prepare(p, slot, part):
                c = cur[slot]
                if part == 0:
                    plain(dve)
                    V.tensor_copy(c[:], pv[:, one(p)].rearrange("p a c -> p (a c)")).then_inc(s["cur"], 1)
                if part == 1:
                    at(dve, p, "tw", 1)
                    V.tensor_scalar(sg[:], tw[:], 0.5, 0.5, ALU.mult, ALU.add).then_inc(s["sg"], 1)
                    at(dve, p, "ssk", 1)
                    V.tensor_scalar(sqk[:], bank[:, 4], 1e-24, None, ALU.max).then_inc(s["clip"], 1)
                    at(dve, p, "sg", 1)
                    V.tensor_tensor_scan(cum[:], resets[:], sg[:], 0.0, ALU.mult, ALU.add).then_inc(s["cum"], 1)
                    at(dve, p, "cum", 1)
                    V.tensor_scalar(ctr[:], by_chunk(cum[:])[:, :, C - 1], 0.5, None, ALU.mult).then_inc(s["ctr"], 1)
                if part == 2:
                    at(dve, p, "ctr", 1)
                    TT(by_chunk(cc[:]), by_chunk(cum[:]), spread(ctr[:]), ALU.subtract).then_inc(s["cc"], 1)
                    at(dve, p, "cc", 1)
                    TT(ce[:], cc[:], sg[:], ALU.subtract).then_inc(s["ce"], 1)
                    V.memset(qs[:, NC_ - 1:NC_], 0.0)
                    TT(qs[:, 0:NC_ - 1], ctr[:, 0:NC_ - 1], ctr[:, 1:NC_], ALU.add).then_inc(s["qsum"], 1)
                    at(dve, p, "loaded", 48)
                    at(dve, p, "pk", 4)
                    V.scalar_tensor_tensor(out=rk[:], in0=r[:], scalar=c[:, RK:RK + 1], in1=kp[:], op0=ALU.mult,
                                           op1=ALU.mult).then_inc(s["rk"], 1)
                if part == 3:
                    at(dve, p, "ep", 1)
                    at(dve, p, "eex", 1)
                    at(dve, p, "pk", 6)
                    V.scalar_tensor_tensor(out=ar[slot][:, :, 0], in0=tiles(kk[:]), scalar=-1.0, in1=tiles(eex[:]), op0=ALU.mult,
                                           op1=ALU.mult).then_inc(s["tilde"], 1)
                    TT(ar[slot][:, :, 1], tiles(r[:]), tiles(ep[:]), ALU.mult).then_inc(s["tilde"], 1)
                    at(dve, p, "em", 1)
                    TT(kt[:], kp[:], em[:], ALU.mult).then_inc(s["tilde"], 1)
                    TT(bt[:], beta[:], em[:], ALU.mult).then_inc(s["tilde"], 1)
                if part == 4:
                    at(dve, p, "bsum", 1)
                    TT(bon[slot][:], bank[:, 5], v[:], ALU.mult).then_inc(s["bon"], 1)

            def finish(p, slot, part):
                c = cur[slot]
                if part == 0:
                    at(dve, p, "mean", 1)
                    V.scalar_tensor_tensor(out=dev[:], in0=bank[:, 6], scalar=-1.0 / C, in1=ysb[:], op0=ALU.mult,
                                           op1=ALU.add).then_inc(s["dev"], 1)
                if part == 2:
                    at(dve, p, "rs", 1)
                    V.scalar_tensor_tensor(out=yn[:], in0=dev[:], scalar=c[:, GNW:GNW + 1], in1=rs[:], op0=ALU.mult,
                                           op1=ALU.mult).then_inc(s["yn"], 1)
                    at(dve, p, "yn", 1)
                    V.scalar_tensor_tensor(out=yn[:], in0=yn[:], scalar=c[:, GNB:GNB + 1], in1=bon[slot][:], op0=ALU.add,
                                           op1=ALU.add).then_inc(s["yn"], 1)
                    at(dve, p, "yn", 2)
                    TT(yn[:], yn[:], gsb[slot][:], ALU.mult).then_inc(s["yn"], 1)

            def step(p, slot, first, last):
                for h in range(2):
                    for n, dst, name in ((0, bl[h], "bl"), (1, kl[h], "kl")):
                        at(dve, p, "score", 3 * h + n + 1)
                        for half in range(2):
                            TT(dst[:, 2 * half:2 * half + 2].rearrange("p t a c -> p t (a c)"),
                               bank[:, 2 * n + half].rearrange("p (t n) -> p t n", t=2), two_masks, ALU.mult).then_inc(s[name], 1)
                        if h == 0 and n == 0 and not first:
                            finish(p - 1, 1 - slot, 0)
                    at(dve, p, "score", 3 * h + 3)
                    TT(x[h][:], tiles(bank[:, 4 if h == 0 else 7]), first_level[:, 0:1].to_broadcast([P, NT, P]), ALU.mult).then_inc(s["nm"], 1)
                for level in range(len(LEVELS)):
                    over = level == len(LEVELS) - 1
                    for h in range(2):
                        at(dve, p, "g_mm", 2 * level + h + 1)
                        TT(g[h][:], tiles(bank[:, 6 + h]), merge[:, level:level + 1].to_broadcast([P, NT, P]), ALU.mult).then_inc(s["g"], 1)
                    if level == 0 and not first:
                        finish(p - 1, 1 - slot, 2)
                    if not last:
                        prepare(p + 1, 1 - slot, level)
                    for h in range(2):
                        at(dve, p, "x_mm", 2 * level + h + 1)
                        if not over:
                            TT(x[h][:], tiles(bank[:, 2 * h]), x[h][:], ALU.add)
                        TT(xt[h][:], tiles(bank[:, 2 * h + 1]), xt[h][:], ALU.add).then_inc(s["x"], 1)
                at(dve, p, "rp_mm", 1)
                TT(tiles(rp[:]), tiles(bank[:, 0]), ar[slot][:, :, 1], ALU.add).then_inc(s["rp"], 1)
                at(dve, p, "f_mm", 1)
                for odd in range(2):
                    TT(ft[:, odd::2], by_chunk(bank[:, 1 + 2 * odd])[:, odd::2],
                       i64[:].rearrange("p (o c) -> p o c", o=1).to_broadcast([P, NC_ // 2, C]), ALU.add).then_inc(s["f"], 1)
                at(dve, p, "z_mm", 1)
                at(dve, p, "q", 1)
                for odd in range(2):
                    TT(zq[:, odd::2], by_chunk(bank[:, 2 + 2 * odd])[:, odd::2], spread(q[slot][:])[:, odd::2], ALU.mult).then_inc(s["z"], 1)
                at(dve, p, "z", 2)
                for c in range(1, NC_ - 1):
                    at(dve, p, "chain", c)
                    V.scalar_tensor_tensor(out=st[:, c + 1], in0=bank[:, 4, c * C:(c + 1) * C], scalar=q[slot][:, c:c + 1],
                                           in1=zq[:, c], op0=ALU.mult, op1=ALU.add).then_inc(s["state"], 1)

            steps(dve, prepare, step, finish)
    close_stage(core, s)


PROJECT_SEMS = ["raw0", "raw1", "raw2", "raw3", "w_free", "w_hi", "w_ready", "rstd", "h_lo", "h_hi", "h32", "sq",
                "sq_used", "ms", "out", "st0", "st1", "ready"]


def project(core, tag, gain, weights, dst):
    nc = core.nc
    cols = weights.shape[1]
    full, rest = cols // P, cols % P
    assert full % 4 == 0
    w = weights.rearrange("(k p) e -> p k e", p=P)
    with ExitStack() as ctx:
        s, sb, ps = open_stage(core, ctx, tag, PROJECT_SEMS)
        open_ring(core, sb)
        sq = sb("sq", [P, 2, T])
        ms = sb("ms", [P, T])
        rstd = sb("rstd", [P, T])
        h32 = sb("h32", [P, 2, T])
        hhi = sb("hhi", [P, ND, T], F32R)
        hlo = sb("hlo", [P, ND, T], F32R)
        staged = sb("staged", [P, 2, T])
        p_ms = ps("p_ms", [P, T])
        p_out = ps("p_out", [P, 4, T])
        block = ctx.enter_context(nc.Block())

        def units(eng, body):
            with eng.Fori(0, full // 4) as i:
                for j in range(4):
                    body(4 * i + j, j, i, P)
            if rest:
                body(full, 0, full // 4, rest)

        @block.sync
        def _(sp):
            def load(unit, slot, rounds, m):
                src = w[:, :, full * P:] if isinstance(unit, int) else w[:, :, bass.ds(unit * P, P)]
                load_unit(sp, s, core, slot, unit, src)
            units(sp, load)

        @block.vector
        def _(dve):
            dve.sem_inc(s["w_ready"], SLOTS)
            norm_vector(core, dve, s, gain, ms, rstd, h32, hhi, hlo)
            units(dve, lambda unit, slot, rounds, m: split_unit(dve, s, core, slot, rounds, unit, ND, m))

        @block.tensor
        def _(pe):
            pe.sem_inc(s["w_free"], SLOTS)
            norm_tensor(core, pe, s, sq, p_ms)
            pe.wait_ge(s["h_lo"], ND)

            def step(unit, slot, rounds, m):
                pe.wait_ge(s["w_ready"], done(unit))
                pe.wait_ge(s["out"], unit + 1)
                for k in range(ND):
                    mm = three_passes(core, p_out[:, slot], slot, k, hhi[:, k], hlo[:, k], k == 0, k == ND - 1)
                mm.then_inc(s["w_free"], 1)
            units(pe, step)

        @block.scalar
        def _(act):
            act.sem_inc(s["out"], 4)
            act.sem_inc(s["st0"], 16)
            act.sem_inc(s["st1"], 16)
            norm_scalar(core, act, s, sq, p_ms, ms, h32, hhi)
            rows = dst[0:full * P].rearrange("(e p) t -> e p t", p=P)

            def step(unit, slot, rounds, m):
                turn = slot % 2
                act.wait_ge(s["w_free"], done(unit))
                act.wait_ge(s[f"st{turn}"], 32 * rounds + (8 * (slot - turn) + 16))
                nc.scalar.activation(staged[0:m, turn], p_out[0:m, slot], ACT.Copy).then_inc(s["out"], 1)
                act.wait_ge(s["out"], unit + 5)
                to = dst[full * P:cols] if isinstance(unit, int) else rows[one(unit)].rearrange("a p t -> p (a t)")
                act.dma_start(to, staged[0:m, turn]).then_inc(s[f"st{turn}"], 16)
            units(act, step)
            act.wait_ge(s["st0"], 16 * (full // 2 + (1 if rest else 0) + 1))
            act.wait_ge(s["st1"], 16 * (full // 2 + 1))
    close_stage(core, s)


def norm_scalar(core, act, s, sq, p_ms, ms, h32, hhi):
    nc = core.nc
    for d in range(ND):
        if d >= 2:
            act.wait_ge(s["sq_used"], d - 1)
        nc.scalar.activation(sq[:, d % 2], core.x[:, d], ACT.Square).then_inc(s["sq"], 1)
    act.wait_ge(s["sq_used"], ND)
    nc.scalar.activation(ms[:], p_ms[:], ACT.Sqrt, scale=1.0 / D, bias=core.eps[:, 0:1]).then_inc(s["ms"], 1)
    for d in range(ND):
        act.wait_ge(s["h32"], d + 1)
        nc.scalar.activation(hhi[:, d], h32[:, d % 2], ACT.Copy).then_inc(s["h_hi"], 1)


def norm_tensor(core, pe, s, sq, p_ms):
    nc = core.nc
    for d in range(ND):
        pe.wait_ge(s["sq"], d + 1)
        nc.tensor.matmul(p_ms[:], core.ones[:], sq[:, d % 2], start=(d == 0), stop=(d == ND - 1)).then_inc(s["sq_used"], 1)


def norm_vector(core, dve, s, gain, ms, rstd, h32, hhi, hlo):
    nc = core.nc
    dve.wait_ge(s["ms"], 1)
    nc.vector.reciprocal(rstd[:], ms[:]).then_inc(s["rstd"], 1)
    dve.wait_ge(s["rstd"], 1)
    for d in range(ND):
        if d >= 2:
            dve.wait_ge(s["h_lo"], d - 1)
        nc.vector.scalar_tensor_tensor(out=h32[:, d % 2], in0=core.x[:, d], scalar=gain[:, d:d + 1],
                                       in1=rstd[:], op0=ALU.mult, op1=ALU.mult).then_inc(s["h32"], 1)
        dve.wait_ge(s["h_hi"], d + 1)
        nc.vector.tensor_tensor(hlo[:, d], h32[:, d % 2], fp(hhi[:, d]), ALU.subtract).then_inc(s["h_lo"], 1)


ADD_SEMS = ["raw0", "raw1", "raw2", "raw3", "w_free", "w_hi", "w_ready", "out", "added", "ready"]


def project_add(core, tag, yhi, ylo, weights):
    nc = core.nc
    w = weights.rearrange("(k p) e -> p k e", p=P)
    with ExitStack() as ctx:
        s, sb, ps = open_stage(core, ctx, tag, ADD_SEMS)
        open_ring(core, sb)
        part = sb("part", [P, 2, T])
        p_out = ps("p_out", [P, 2, T])
        block = ctx.enter_context(nc.Block())

        @block.sync
        def _(sp):
            with sp.Fori(0, ND // 4) as i:
                for j in range(4):
                    load_unit(sp, s, core, j, 4 * i + j, w[:, :, bass.ds(4 * P * i + j * P, P)])

        @block.vector
        def _(dve):
            dve.sem_inc(s["w_ready"], SLOTS)
            with dve.Fori(0, ND // 4) as i:
                for j in range(4):
                    split_unit(dve, s, core, j, i, 4 * i + j, ND)

        @block.tensor
        def _(pe):
            pe.sem_inc(s["w_free"], SLOTS)
            with pe.Fori(0, ND // 4) as i:
                for j in range(4):
                    pe.wait_ge(s["w_ready"], done(4 * i + j))
                    pe.wait_ge(s["out"], 4 * i + (j + 1))
                    for k in range(ND):
                        mm = three_passes(core, p_out[:, j % 2], j, k, yhi[:, k], ylo[:, k], k == 0, k == ND - 1)
                    mm.then_inc(s["w_free"], 1)

        @block.scalar
        def _(act):
            act.sem_inc(s["out"], 2)
            with act.Fori(0, ND // 4) as i:
                for j in range(4):
                    act.wait_ge(s["w_free"], done(4 * i + j))
                    act.wait_ge(s["added"], 4 * i + (j + 1))
                    nc.scalar.activation(part[:, j % 2], p_out[:, j % 2], ACT.Copy).then_inc(s["out"], 1)

        @block.gpsimd
        def _(pool):
            pool.sem_inc(s["added"], 2)
            with pool.Fori(0, ND // 4) as i:
                for j in range(4):
                    pool.wait_ge(s["out"], 4 * i + (j + 3))
                    pool.sem_inc(s["ready"], 1)
                    xs = flat(core.x[:, one(4 * i + j)])
                    nc.gpsimd.tensor_tensor(xs, xs, part[:, j % 2], ALU.add).then_inc(s["added"], 1)
            pool.wait_ge(s["added"], ND + 2)
    close_stage(core, s)


G = 4
KIND = G * C
N_CMP = (T - 32) // 16 + 1
CMP_LEN, CMP_STRIDE, CMP_HIDDEN = 32, 16, 256
NL = CMP_LEN // 2
NH = CMP_HIDDEN // P

ROTATE_EVENTS = {"sqx": 1, "ss": 1, "ln": 1, "rs": 1, "n": 1, "perm": 1, "t1": 1, "t2": 1, "rot": 1}


def rotate(core, tag, source, tiles, gain_of, plain_out, rot_out, scale=1.0):
    nc = core.nc
    per = tiles // len(gain_of)
    with ExitStack() as ctx:
        s, sb, ps = open_stage(core, ctx, tag, list(ROTATE_EVENTS) + ["loaded", "ready", "consts", "gains", "scaled", "out0", "out1"])

        def at(eng, m, name, k=1):
            eng.wait_ge(s[name], m * ROTATE_EVENTS[name] + k * ROTATE_EVENTS[name])

        def wait_plain(eng):
            eng.sem_inc(s["ready"], 1)

        cos, sin = sb("cos", [P, T]), sb("sin", [P, T])
        swap = sb("swap", [P, P])
        gain = sb("gain", [P, len(gain_of)])
        xt = sb("xt", [P, tiles, T])
        rs = sb("rs", [P, tiles, T])
        sq = sb("sq", [P, 2, T])
        n = sb("n", [P, 2, T])
        t1, t2 = sb("t1", [P, 2, T]), sb("t2", [P, 2, T])
        rot = sb("rot", [P, 2, T])
        p_ss = ps("p_ss", [P, 2, T])
        p_swap = ps("p_swap", [P, 2, T])
        block = ctx.enter_context(nc.Block())
        outs = 2 if plain_out else 1
        loop = lambda eng: eng.Fori(0, tiles // 2)

        @block.sync
        def _(sp):
            for c, g in enumerate(gain_of):
                for h in range(2):
                    sp.dma_start(gain[C * h:C * h + C, c:c + 1], g.rearrange("(d a) -> d a", a=1)).then_inc(s["gains"], 16)
            with loop(sp) as i:
                for j in range(2):
                    sp.dma_start(flat(xt[:, one(2 * i + j)]), source(i, j)).then_inc(s["loaded"], 16)
            for dst, name in ((cos[:], "c_cos"), (sin[:], "c_sin"), (swap[:], "c_swap")):
                sp.dma_start(dst, core.consts[name]).then_inc(s["consts"], 16)
            with loop(sp) as i:
                for j in range(2):
                    m = 2 * i + j
                    at(sp, m, "rot")
                    if plain_out:
                        sp.dma_start(plain_out(i, j), n[:, j]).then_inc(s[f"out{j}"], 16)
                    sp.dma_start(rot_out(i, j), rot[:, j]).then_inc(s[f"out{j}"], 16)
            for j in range(2):
                sp.wait_ge(s[f"out{j}"], 16 * outs * (tiles // 2 + 1))

        @block.scalar
        def _(act):
            act.sem_inc(s["ss"], 2)
            with loop(act) as i:
                for j in range(2):
                    m = 2 * i + j
                    act.wait_ge(s["loaded"], 16 * tiles)
                    at(act, m, "ss")
                    wait_plain(act)
                    nc.scalar.activation(sq[:, j], flat(xt[:, one(m)]), ACT.Square).then_inc(s["sqx"], 1)
                    at(act, m, "ss", 3)
                    wait_plain(act)
                    nc.scalar.activation(flat(rs[:, one(m)]), p_ss[:, j], ACT.Ln, scale=1.0 / C,
                                         bias=core.eps[:, 0:1]).then_inc(s["ln"], 1)
            with loop(act) as i:
                for j in range(2):
                    m = 2 * i + j
                    at(act, m, "ln", 3)
                    wait_plain(act)
                    nc.scalar.activation(flat(rs[:, one(m)]), flat(rs[:, one(m)]), ACT.Exp, scale=-0.5).then_inc(s["rs"], 1)

        @block.tensor
        def _(pe):
            with loop(pe) as i:
                for j in range(2):
                    m = 2 * i + j
                    at(pe, m, "sqx")
                    at(pe, m, "ln")
                    nc.tensor.matmul(p_ss[:, j], core.head_ones[:], sq[:, j], start=True, stop=True).then_inc(s["ss"], 1)
            pe.wait_ge(s["consts"], 48)
            with loop(pe) as i:
                for j in range(2):
                    m = 2 * i + j
                    at(pe, m, "n")
                    nc.tensor.matmul(p_swap[:, j], swap[:], n[:, j], start=True, stop=True).then_inc(s["perm"], 1)

        @block.vector
        def _(dve):
            dve.wait_ge(s["gains"], 32 * len(gain_of))
            nc.vector.tensor_scalar(gain[:], gain[:], scale, None, ALU.mult).then_inc(s["scaled"], 1)
            dve.wait_ge(s["scaled"], 1)
            dve.wait_ge(s["consts"], 48)
            for j in range(2):
                dve.sem_inc(s[f"out{j}"], 16 * outs)
            with loop(dve) as i:
                for j in range(2):
                    m = 2 * i + j
                    at(dve, m, "rs")
                    dve.wait_ge(s[f"out{j}"], 16 * outs * (i + 1))
                    at(dve, m, "t1")
                    g = gain[:, 0:1] if len(gain_of) == 1 else gain[:, one(i)]
                    nc.vector.scalar_tensor_tensor(out=n[:, j], in0=flat(xt[:, one(m)]), scalar=g,
                                                   in1=flat(rs[:, one(m)]), op0=ALU.mult, op1=ALU.mult).then_inc(s["n"], 1)
                    at(dve, m, "perm")
                    nc.vector.tensor_tensor(t2[:, j], p_swap[:, j], sin[:], ALU.mult).then_inc(s["t2"], 1)
                    at(dve, m, "t2")
                    at(dve, m, "t1", 3)
                    nc.vector.tensor_tensor(rot[:, j], t1[:, j], t2[:, j], ALU.add).then_inc(s["rot"], 1)

        @block.gpsimd
        def _(pool):
            pool.wait_ge(s["consts"], 48)
            pool.sem_inc(s["t1"], 2)
            pool.sem_inc(s["ln"], 2)
            with loop(pool) as i:
                for j in range(2):
                    m = 2 * i + j
                    at(pool, m, "n")
                    wait_plain(pool)
                    nc.gpsimd.tensor_tensor(t1[:, j], n[:, j], cos[:], ALU.mult).then_inc(s["t1"], 1)
    close_stage(core, s)


def values(core, tag, kv, v_tok, k_cmp, v_cmp):
    nc, ins = core.nc, core.ins
    with ExitStack() as ctx:
        s, sb, ps = open_stage(core, ctx, tag, ["vt", "turned", "read", "vout", "tok", "pos", "w1", "w2", "blk", "h1",
                                               "gelu", "c2", "sqc", "ss", "pos_turned", "pos_copied", "ln", "rsc", "kc", "vc", "cout", "gain"])
        vt = sb("vt", [P, 4, T])
        vsb = sb("vsb", [P, 4, T])
        tok = sb("tok", [P, 2, G, T])
        pos_rows, pos = sb("pos_rows", [NL, 2, P]), sb("pos", [P, 2, NL])
        w1 = sb("w1", [P, 2, NL, CMP_HIDDEN])
        w2 = sb("w2", [P, 2, NH, C])
        gain = sb("gain", [C, 1])
        NB = G * N_CMP
        blk = sb("blk", [P, 4, NB])
        hid = sb("hid", [P, 2, NH, NB])
        kc, sqc, rsc, vc = sb("kc", [C, NB]), sb("sqc", [C, NB]), sb("rsc", [C, NB]), sb("vc", [NB, C])
        turn = ps("turn", [P, 2, T])
        p_h = ps("p_h", [P, 4, T])
        p_o = ps("p_o", [P, 2, T])
        block = ctx.enter_context(nc.Block())
        v_rows = kv[2 * KIND:6 * KIND].rearrange("(b x e p) t -> x b e p t", b=2, x=2, p=P)[1]
        steps = [(which, lp) for which in range(2) for lp in range(NL)]

        @block.sync
        def _(sp):
            for which in range(2):
                src = kv[which * KIND:(which + 1) * KIND].rearrange("(g d) t -> d g t", d=C)
                sp.dma_start(tok[0:C, which], src).then_inc(s["tok"], 16)
                sp.dma_start(tok[C:P, which, :, 0:T - 1], src[:, :, 1:T]).then_inc(s["tok"], 16)
                p_src = ins["cmp_pos_k" if which == 0 else "cmp_pos_v"].rearrange("(l a) d -> l (a d)", a=2)
                sp.dma_start(pos_rows[:, which], p_src).then_inc(s["pos"], 16)
                w = ins["cmp_k_w1" if which == 0 else "cmp_v_w1"].rearrange("(l p) h -> p l h", p=P)
                sp.dma_start(w1[:, which], w).then_inc(s["w1"], 16)
                sp.dma_start(w2[:, which], ins["cmp_k_w2" if which == 0 else "cmp_v_w2"].rearrange("(l p) h -> p l h", p=P)).then_inc(s["w2"], 16)
            sp.dma_start(gain[:], ins["kv_k_norm"][0].rearrange("(d a) -> d a", a=1)).then_inc(s["gain"], 16)
            sp.wait_ge(s["vc"], 1)
            sp.dma_start(v_cmp, vc[:]).then_inc(s["cout"], 16)
            sp.wait_ge(s["kc"], 1)
            sp.dma_start(k_cmp, kc[:]).then_inc(s["cout"], 16)
            sp.wait_ge(s["cout"], 32)

        @block.scalar
        def _(act):
            for n in range(4):
                act.dma_start(vt[:, n], v_rows[n // 2, n % 2]).then_inc(s["vt"], 16)
            for n in range(4):
                act.wait_ge(s["turned"], n + 1)
                nc.scalar.activation(vsb[:, n], turn[:, n % 2], ACT.Copy).then_inc(s["read"], 1)
                act.wait_ge(s["read"], n + 1)
                act.dma_start(v_tok[n], vsb[:, n]).then_inc(s["vout"], 16)
            for which in range(2):
                for t in range(NH):
                    act.wait_ge(s["h1"], NL * which + NL)
                    nc.scalar.activation(hid[:, which, t], p_h[:, 2 * which + t, 0:NB], ACT.Gelu_apprx_tanh).then_inc(s["gelu"], 1)
            act.wait_ge(s["c2"], 1)
            nc.scalar.activation(sqc[:], p_o[0:C, 0, 0:NB], ACT.Square).then_inc(s["sqc"], 1)
            act.wait_ge(s["c2"], 2)
            nc.scalar.activation(vc[:], p_o[0:NB, 1, 0:C], ACT.Copy).then_inc(s["vc"], 1)
            act.wait_ge(s["ss"], 1)
            nc.scalar.activation(rsc[:], p_h[0:C, 0, 0:NB], ACT.Ln, scale=1.0 / C, bias=core.eps[0:C, 0:1]).then_inc(s["ln"], 1)
            act.wait_ge(s["ln"], 1)
            nc.scalar.activation(rsc[:], rsc[:], ACT.Exp, scale=-0.5).then_inc(s["rsc"], 1)
            act.wait_ge(s["vout"], 64)

        @block.tensor
        def _(pe):
            pe.wait_ge(s["pos"], 32)
            for which in range(2):
                mm = nc.tensor.transpose(p_o[:, 1, which * NL:(which + 1) * NL], pos_rows[:, which], core.ident[0:NL, 0:NL])
            mm.then_inc(s["pos_turned"], 1)
            for n in range(4):
                pe.wait_ge(s["vt"], 64)
                if n >= 2:
                    pe.wait_ge(s["read"], n - 1)
                for t in range(NT):
                    mm = nc.tensor.transpose(turn[:, n % 2, t * P:(t + 1) * P], vt[:, n, t * P:(t + 1) * P], core.ident[:])
                mm.then_inc(s["turned"], 1)
            for n, (which, lp) in enumerate(steps):
                pe.wait_ge(s["blk"], n + 1)
                if lp == 0:
                    pe.wait_ge(s["w1"], 32)
                for t in range(NH):
                    mm = nc.tensor.matmul(p_h[:, 2 * which + t, 0:NB], w1[:, which, lp, t * P:(t + 1) * P],
                                          blk[:, n % 4], start=(lp == 0), stop=(lp == NL - 1))
                mm.then_inc(s["h1"], 1)
            pe.wait_ge(s["w2"], 32)
            pe.wait_ge(s["gelu"], 2)
            for t in range(NH):
                mm = nc.tensor.matmul(p_o[0:C, 0, 0:NB], w2[:, 0, t], hid[:, 0, t], start=(t == 0), stop=(t == NH - 1))
            mm.then_inc(s["c2"], 1)
            pe.wait_ge(s["gelu"], 4)
            for t in range(NH):
                mm = nc.tensor.matmul(p_o[0:NB, 1, 0:C], hid[:, 1, t], w2[:, 1, t], start=(t == 0), stop=(t == NH - 1))
            mm.then_inc(s["c2"], 1)
            pe.wait_ge(s["sqc"], 1)
            nc.tensor.matmul(p_h[0:C, 0, 0:NB], core.ones[0:C, 0:C], sqc[:], start=True, stop=True).then_inc(s["ss"], 1)

        @block.vector
        def _(dve):
            dve.wait_ge(s["tok"], 64)
            dve.wait_ge(s["pos_turned"], 1)
            nc.vector.tensor_copy(pos[:], p_o[:, 1, 0:2 * NL].rearrange("p (a l) -> p a l", a=2)).then_inc(s["pos_copied"], 1)
            dve.wait_ge(s["pos_copied"], 1)
            for n, (which, lp) in enumerate(steps):
                if n >= 4:
                    dve.wait_ge(s["h1"], n - 3)
                src = tok[:, which, :, 2 * lp:2 * lp + CMP_STRIDE * (N_CMP - 1) + 1:CMP_STRIDE]
                nc.vector.tensor_scalar(blk[:, n % 4].rearrange("p (g n) -> p g n", g=G), src,
                                        pos[:, which, lp:lp + 1], None, ALU.add).then_inc(s["blk"], 1)
            dve.wait_ge(s["gain"], 16)
            dve.wait_ge(s["rsc"], 1)
            nc.vector.scalar_tensor_tensor(out=kc[:], in0=p_o[0:C, 0, 0:NB], scalar=gain[:, 0:1], in1=rsc[:],
                                           op0=ALU.mult, op1=ALU.mult).then_inc(s["kc"], 1)
    close_stage(core, s)




def attention_steps():
    steps, turn = [], None
    for group in range(2):
        for pair in range(2):
            for head in range(2):
                steps.append(("cmp", group, pair, head, 0))
                steps += [("main", group, pair, head, t) for t in range(NT)][0:1]
                if turn and head == 0:
                    steps.append(turn)
                steps += [("main", group, pair, head, t) for t in range(1, NT)]
            turn = ("turn", group, pair, 0, 0)
    return steps + [turn]


STEPS = attention_steps()
ATTENTION_EVENTS = {
    "scores": ("cmp", "main"), "masked": ("cmp",), "nmax": ("cmp", "main"), "probs": ("cmp", "main"),
    "turned": ("cmp", "main", "turn"), "copied_v": ("main", "turn"), "copied_a": ("cmp", "main", "turn"),
    "o_mm": ("cmp", "main"), "recip": ("cmp", "main"), "coef": ("cmp", "main"), "o_sel": ("main",), "o": ("cmp", "main"),
}
N_LOADS = 10


def attention(core, tag, q_plain, q_rot, gate_logits, k_rot, v_tok, k_cmp, v_cmp, yhi, ylo):
    nc, ins = core.nc, core.ins
    U = len(STEPS)
    assert U % 4 == 0
    per_body = {e: sum(st[0] in kinds for st in STEPS) for e, kinds in ATTENTION_EVENTS.items()}

    with ExitStack() as ctx:
        s, sb, ps = open_stage(core, ctx, tag, list(ATTENTION_EVENTS) + ["in0", "in1", "gl", "consts", "sig", "gt", "gates", "ready",
                                               "split", "rounded"])

        def at(eng, i, name, u):
            kinds = ATTENTION_EVENTS[name]
            whole, u = divmod(u, U)
            count = sum(st[0] in kinds for st in STEPS[:u + 1]) + whole * per_body[name]
            eng.wait_ge(s[name], i * per_body[name] + (per_body[name] + count))

        def credit(eng, *names):
            for name in names:
                eng.sem_inc(s[name], per_body[name])

        kk = [sb(f"kk{g}", [P, 2, T]) for g in range(2)]
        kc = [sb(f"kc{g}", [P, N_CMP]) for g in range(2)]
        vv = [sb(f"vv{g}", [P, 2, NT, C]) for g in range(2)]
        vc = [sb(f"vc{g}", [N_CMP, C]) for g in range(2)]
        qp = [sb(f"qp{g}", [P, 2, T]) for g in range(2)]
        qr = [sb(f"qr{g}", [P, 4, T]) for g in range(2)]
        q2 = [sb(f"q2{g}", [P, 4, T], F32R) for g in range(2)]
        khi = [sb(f"khi{g}", [P, 2, T], F32R) for g in range(2)]
        klo = [sb(f"klo{g}", [P, 2, T], F32R) for g in range(2)]
        glog = sb("glog", [48, T])
        gates = sb("gates", [P, NT, 48])
        causal = sb("causal", [P, P])
        cmp_neg = sb("cmp_neg", [P, NT, N_CMP])
        has_block = sb("has_block", [P, 1])
        ident16, causal16 = sb("ident16", [P, P], mybir.dt.bfloat16), sb("causal16", [P, P], mybir.dt.bfloat16)
        masked = sb("masked", [P, 2, NT, N_CMP])
        nmax, sums = sb("nmax", [P, 2, NT]), sb("sums", [P, 4, NT])
        probs = sb("probs", [P, 2, 2, T])
        pt = sb("pt", [P, 2, 2, T])
        rcp, coef = sb("rcp", [P, NT]), sb("coef", [P, NT])
        osb = sb("osb", [P, 2, NT, P])
        bank = ps("bank", [P, 8, T])
        block = ctx.enter_context(nc.Block())

        @block.sync
        def _(sp):
            sp.dma_start(glog[:], gate_logits).then_inc(s["gl"], 16)
            for dst, name in ((causal, "c_causal"), (cmp_neg, "c_cmp_neg"), (has_block, "c_has_block")):
                sp.dma_start(dst[:], core.consts[name]).then_inc(s["consts"], 16)
            with sp.Fori(0, 2) as i:
                for g in range(2):
                    last = max(u for u, st in enumerate(STEPS) if st[0] != "turn" and st[1] == g)
                    at(sp, i, "o_mm", last - U)
                    it = lambda view: view[one(i)].rearrange
                    keys = k_rot.rearrange("(b e x d) t -> x e d b t", b=2, x=2, d=C)[g][one(i)].rearrange("o d b t -> (o d) b t")
                    keys_c = k_cmp.rearrange("d (e x n) -> x e d n", x=2, n=N_CMP)[g][one(i)].rearrange("o d n -> (o d) n")
                    for h in range(2):
                        sp.dma_start(kk[g][C * h:C * h + C], keys).then_inc(s[f"in{g}"], 16)
                        sp.dma_start(kc[g][C * h:C * h + C], keys_c).then_inc(s[f"in{g}"], 16)
                    for h in range(2):
                        src = q_rot.rearrange("(e x j d) t -> x e d j t", x=2, j=4, d=C)[g][one(i)].rearrange("o d j t -> (o d) j t")
                        sp.dma_start(qr[g][C * h:C * h + C], src).then_inc(s[f"in{g}"], 16)
                    src = q_plain.rearrange("(e x j p) t -> x e p j t", x=2, j=2, p=P)[g][one(i)].rearrange("o p j t -> (o p) j t")
                    sp.dma_start(qp[g][:], src).then_inc(s[f"in{g}"], 16)
                    for b in range(2):
                        src = v_tok.rearrange("(b e) p (t x d) -> b x e p t d", b=2, x=2, d=C)[b][g][one(i)].rearrange("o p t d -> (o p) t d")
                        sp.dma_start(vv[g][:, b], src).then_inc(s[f"in{g}"], 16)
                    src = v_cmp.rearrange("(e x n) d -> x e n d", x=2, n=N_CMP)[g][one(i)].rearrange("o n d -> (o n) d")
                    sp.dma_start(vc[g][:], src).then_inc(s[f"in{g}"], 16)

        @block.tensor
        def _(pe):
            pe.wait_ge(s["sig"], 1)
            for t in range(NT):
                mm = nc.tensor.transpose(bank[:, 6, t * 48:(t + 1) * 48], glog[:, t * P:(t + 1) * P], core.ident[0:48, 0:48])
            mm.then_inc(s["gt"], 1)
            pe.wait_ge(s["gates"], 2)
            credit(pe, "scores", "turned", "o_mm")

            def scores(i, u):
                kind, g, pair, head, t = STEPS[u]
                if kind == "turn":
                    return
                hp, slot = slice(C * head, C * head + C), u % 2
                if u == 0 or STEPS[u - 1][1] != g and kind == "cmp":
                    pe.wait_ge(s[f"in{g}"], 16 * N_LOADS * (i + 1))
                at(pe, i, "probs", u - 2)
                if kind == "cmp":
                    for t in range(NT):
                        mm = nc.tensor.matmul(bank[:, 2 * slot, t * N_CMP:(t + 1) * N_CMP], qp[g][hp, pair, t * P:(t + 1) * P],
                                              kc[g][hp], start=True, stop=True)
                    mm.then_inc(s["scores"], 1)
                    return
                n = (t + 1) * P
                if t == 0:
                    pe.wait_ge(s["split"], 10 * i + (5 * g + 2 * pair + head + 3))
                for b in range(2):
                    q = q2[g][:, 2 * pair + head, t * P:n]
                    nc.tensor.matmul(bank[:, 2 * slot + b, 0:n], q, khi[g][:, b, 0:n], start=True, stop=False)
                    nc.tensor.matmul(bank[:, 2 * slot + b, 0:n], q, klo[g][:, b, 0:n], start=False, stop=False)
                    mm = nc.tensor.matmul(bank[:, 2 * slot + b, t * P:n], ident16[:], causal16[:], start=False, stop=True)
                mm.then_inc(s["scores"], 1)

            def turn(i, u):
                kind, g, pair, head, t = STEPS[u]
                at(pe, i, "copied_v", u - 1)
                at(pe, i, "copied_a", u - 1)
                if kind == "turn":
                    last = max(w for w in range(U) if STEPS[w] == ("main", g, pair, 1, NT - 1))
                    at(pe, i, "o", last)
                    for t in range(NT):
                        mm = nc.tensor.transpose(bank[:, 4, t * P:(t + 1) * P], osb[:, pair, t], core.ident[:])
                elif kind == "cmp":
                    at(pe, i, "probs", u)
                    for t in range(NT):
                        mm = nc.tensor.transpose(bank[0:N_CMP, 4, t * P:(t + 1) * P], probs[:, u % 2, 0, t * N_CMP:(t + 1) * N_CMP],
                                                 core.ident[:])
                else:
                    at(pe, i, "probs", u)
                    for b in range(2):
                        for j in range(t + 1):
                            mm = nc.tensor.transpose(bank[:, 4 + b, j * P:(j + 1) * P], probs[:, u % 2, b, j * P:(j + 1) * P],
                                                     core.ident[:])
                mm.then_inc(s["turned"], 1)

            def weigh(i, u):
                kind, g, pair, head, t = STEPS[u]
                if kind == "turn":
                    return
                at(pe, i, "copied_a", u)
                at(pe, i, "o", u - 2)
                if kind == "cmp":
                    for t in range(NT):
                        mm = nc.tensor.matmul(bank[:, 6 + u % 2, t * C:(t + 1) * C], pt[0:N_CMP, u % 2, 0, t * P:(t + 1) * P], vc[g][:],
                                              start=True, stop=True)
                else:
                    at(pe, i, "copied_v", u)
                    for b in range(2):
                        out = bank[:, 6 + u % 2, b * C:(b + 1) * C]
                        for j in range(t + 1):
                            mm = nc.tensor.matmul(out, pt[:, u % 2, b, j * P:(j + 1) * P], vv[g][:, b, j], start=(j == 0), stop=(j == t))
                mm.then_inc(s["o_mm"], 1)

            with pe.Fori(0, 2) as i:
                scores(i, 0)
                for u in range(U):
                    if u + 1 < U:
                        scores(i, u + 1)
                    if STEPS[u][0] == "turn":
                        weigh(i, u - 1)
                        turn(i, u)
                    else:
                        turn(i, u)
                        if u:
                            weigh(i, u - 1)

        @block.scalar
        def _(act):
            A = nc.scalar.activation
            credit(act, "probs", "copied_a")
            act.wait_ge(s["gl"], 16)
            A(glog[:], glog[:], ACT.Sigmoid).then_inc(s["sig"], 1)

            def exps(i, u):
                kind, g, pair, head, t = STEPS[u]
                if kind == "turn":
                    return
                slot = u % 2
                at(act, i, "nmax", u)
                at(act, i, "turned", u - 2)
                if kind == "cmp":
                    for t in range(NT):
                        a = A(probs[:, slot, 0, t * N_CMP:(t + 1) * N_CMP], masked[:, slot, t], ACT.Exp,
                              bias=nmax[:, slot, t:t + 1], accum_out=sums[:, u % 4, t:t + 1])
                else:
                    n = (t + 1) * P
                    for b in range(2):
                        a = A(probs[:, slot, b, 0:n], bank[:, 2 * slot + b, 0:n], ACT.Exp, bias=nmax[:, slot, b:b + 1],
                              accum_out=sums[:, u % 4, b:b + 1])
                a.then_inc(s["probs"], 1)

            def copy(i, u):
                kind, g, pair, head, t = STEPS[u]
                at(act, i, "turned", u)
                at(act, i, "o_mm", u - 2)
                if kind == "turn":
                    act.sem_inc(s["ready"], 1)
                    A(flat(yhi[:, one(4 * i + (2 * g + pair))]), bank[:, 4], ACT.Copy).then_inc(s["copied_a"], 1)
                elif kind == "cmp":
                    A(pt[0:N_CMP, u % 2, 0], bank[0:N_CMP, 4], ACT.Copy).then_inc(s["copied_a"], 1)
                else:
                    n = (t + 1) * P
                    A(pt[:, u % 2, 1, 0:n], bank[:, 5, 0:n], ACT.Copy).then_inc(s["copied_a"], 1)

            with act.Fori(0, 2) as i:
                for u in range(U + 1):
                    if u < U:
                        exps(i, u)
                    if u:
                        copy(i, u - 1)

        @block.gpsimd
        def _(pool):
            pool.sem_inc(s["split"], 1)
            with pool.Fori(0, 2) as i:
                for g in range(2):
                    pool.wait_ge(s[f"in{g}"], 16 * N_LOADS * (i + 1))
                    pool.wait_ge(s["split"], 10 * i + (5 * g + 1))
                    pool.sem_inc(s["ready"], 1)
                    nc.gpsimd.tensor_copy(khi[g][:], kk[g][:]).then_inc(s["rounded"], 1)
                    pool.wait_ge(s["rounded"], 10 * i + (5 * g + 1))
                    nc.gpsimd.tensor_tensor(klo[g][:], kk[g][:], fp(khi[g][:]), ALU.subtract).then_inc(s["split"], 1)
                    for h in range(4):
                        pool.wait_ge(s["split"], 10 * i + (5 * g + h + 2))
                        pool.sem_inc(s["ready"], 1)
                        nc.gpsimd.tensor_copy(q2[g][:, h], qr[g][:, h]).then_inc(s["rounded"], 1)
                        pool.wait_ge(s["rounded"], 10 * i + (5 * g + h + 2))
                        nc.gpsimd.tensor_tensor(q2[g][C:P, h], qr[g][C:P, h], fp(q2[g][C:P, h]), ALU.subtract).then_inc(s["split"], 1)

        @block.vector
        def _(dve):
            V = nc.vector
            dve.wait_ge(s["consts"], 48)
            V.tensor_copy(ident16[:], core.ident[:])
            V.tensor_copy(causal16[:], causal[:])
            dve.wait_ge(s["gt"], 1)
            V.tensor_copy(gates[:], bank[:, 6, 0:NT * 48].rearrange("p (t g) -> p t g", t=NT)).then_inc(s["gates"], 1)
            dve.wait_ge(s["gates"], 1)
            V.tensor_scalar(gates[:, 0, 0::3], gates[:, 0, 0::3], has_block[:, 0:1], None, ALU.mult).then_inc(s["gates"], 1)
            dve.wait_ge(s["gates"], 2)
            credit(dve, "masked", "nmax", "copied_v", "recip", "coef", "o_sel", "o")

            def maxima(i, u):
                kind, g, pair, head, t = STEPS[u]
                if kind == "turn":
                    return
                slot = u % 2
                at(dve, i, "scores", u)
                if kind == "cmp":
                    V.tensor_tensor(masked[:, slot], bank[:, 2 * slot, 0:NT * N_CMP].rearrange("p (t n) -> p t n", t=NT),
                                    cmp_neg[:], ALU.add).then_inc(s["masked"], 1)
                    at(dve, i, "masked", u)
                    V.reduce_max(nmax[:, slot], masked[:, slot], axis=AX.X, negate=True).then_inc(s["nmax"], 1)
                else:
                    V.reduce_max(nmax[:, slot, 0:2], bank[:, 2 * slot:2 * slot + 2, 0:(t + 1) * P], axis=AX.X,
                                 negate=True).then_inc(s["nmax"], 1)

            def copy(i, u):
                kind, g, pair, head, t = STEPS[u]
                if kind == "turn":
                    at(dve, i, "copied_a", u)
                    pi = one(4 * i + (2 * g + pair))
                    V.tensor_tensor(flat(ylo[:, pi]), bank[:, 4], flat(fp(yhi[:, pi])), ALU.subtract).then_inc(s["copied_v"], 1)
                elif kind == "main":
                    at(dve, i, "turned", u)
                    at(dve, i, "o_mm", u - 2)
                    n = (t + 1) * P
                    V.tensor_copy(pt[:, u % 2, 0, 0:n], bank[:, 4, 0:n]).then_inc(s["copied_v"], 1)

            def combine(i, u):
                kind, g, pair, head, t = STEPS[u]
                if kind == "turn":
                    return
                m = NT if kind == "cmp" else 2
                h3 = 24 * i + (12 * g + 6 * pair + 3 * head)
                at(dve, i, "o_mm", u)
                at(dve, i, "o", u - 1)
                V.reciprocal(rcp[:, 0:m], sums[:, u % 4, 0:m]).then_inc(s["recip"], 1)
                at(dve, i, "recip", u)
                if kind == "cmp":
                    gate = gates[:, :, one(h3)].rearrange("p t a -> p (t a)")
                else:
                    gate = gates[:, t, bass.ds(h3 + 1, 2)]
                V.tensor_tensor(coef[:, 0:m], rcp[:, 0:m], gate, ALU.mult).then_inc(s["coef"], 1)
                at(dve, i, "coef", u)
                if kind == "cmp":
                    V.tensor_tensor(osb[:, pair, :, C * head:C * head + C], bank[:, 6 + u % 2, 0:NT * C].rearrange("p (t d) -> p t d", t=NT),
                                    coef[:].rearrange("p (t a) -> p t a", a=1).to_broadcast([P, NT, C]), ALU.mult).then_inc(s["o"], 1)
                    return
                o = osb[:, pair, t, C * head:C * head + C]
                V.scalar_tensor_tensor(out=o, in0=bank[:, 6 + u % 2, 0:C], scalar=coef[:, 0:1], in1=o,
                                       op0=ALU.mult, op1=ALU.add).then_inc(s["o_sel"], 1)
                at(dve, i, "o_sel", u)
                V.scalar_tensor_tensor(out=o, in0=bank[:, 6 + u % 2, C:2 * C], scalar=coef[:, 1:2], in1=o,
                                       op0=ALU.mult, op1=ALU.add).then_inc(s["o"], 1)

            with dve.Fori(0, 2) as i:
                for u in range(U + 2):
                    if u < U:
                        maxima(i, u)
                    late = 1 <= u <= U and STEPS[u - 1][0] == "turn"
                    if 1 <= u <= U and not late:
                        copy(i, u - 1)
                    if u >= 2:
                        combine(i, u - 2)
                    if late:
                        copy(i, u - 1)
    close_stage(core, s)


def tile_pairs(view):
    return lambda i, j: view[j][one(i)].rearrange("a p t -> p (a t)")


def setup(core):
    nc, ins = core.nc, core.ins
    with ExitStack() as ctx:
        s, sb, ps = open_stage(core, ctx, "setup", ["const", "rows", "x", "turned", "copied", "filled"])
        nt = T // P
        tok = sb("tok", [P, nt, D])
        rows = sb("rows", [P, 2, P])
        turn = ps("turn", [P, 4, T])
        rest = core.rows - P
        block = ctx.enter_context(nc.Block())

        @block.sync
        def _(sp):
            sp.dma_start(core.ident[:], core.consts["c_ident"]).then_inc(s["const"], 16)
            sp.dma_start(core.head_ones[:], core.consts["c_head_ones"]).then_inc(s["const"], 16)
            for name in VECTORS:
                n = int(np.prod(ins[name].shape)) // P
                r = core.row[name]
                shape = ins[name].shape
                src = ins[name]
                axes = " ".join("abcd"[:len(shape)])
                src = src.rearrange(f"{axes} -> ({axes})") if len(shape) > 1 else src
                src = src.rearrange("(r p) -> r p", p=P)
                for tile in range(2):
                    lo, hi = max(r, tile * P), min(r + n, tile * P + P)
                    if lo < hi:
                        sp.dma_start(rows[lo - tile * P:hi - tile * P, tile], src[lo - r:hi - r]).then_inc(s["rows"], 16)
            core.row_loads = sum(1 + (core.row[v] < P < core.row[v] + int(np.prod(ins[v].shape)) // P) for v in VECTORS)

        @block.scalar
        def _(act):
            for t in range(nt):
                act.dma_start(tok[:, t], ins["x"].rearrange("b (t p) d -> t p (b d)", p=P)[t]).then_inc(s["x"], 16)
            for d in range(ND):
                act.wait_ge(s["turned"], d + 1)
                nc.scalar.activation(core.x[:, d], turn[:, d % 4], ACT.Copy).then_inc(s["copied"], 1)
            for tile, n in enumerate((P, rest)):
                act.wait_ge(s["turned"], ND + tile + 1)
                nc.scalar.activation(core.vecs[:, tile * P:tile * P + n], turn[:, tile, 0:n], ACT.Copy).then_inc(s["copied"], 1)

        @block.vector
        def _(dve):
            nc.vector.memset(core.ones[:], 1.0)
            nc.vector.memset(core.eps[:, 0:1], EPS)
            nc.vector.memset(core.eps[:, 1:2], GN_EPS)
            nc.vector.memset(core.zero[:], 0.0).then_inc(s["filled"], 1)

        @block.tensor
        def _(pe):
            pe.wait_ge(s["const"], 32)
            pe.wait_ge(s["x"], 16 * nt)
            for d in range(ND):
                if d >= 4:
                    pe.wait_ge(s["copied"], d - 3)
                for t in range(nt):
                    mm = nc.tensor.transpose(turn[:, d % 4, t * P:(t + 1) * P], tok[:, t, d * P:(d + 1) * P], core.ident[:])
                mm.then_inc(s["turned"], 1)
            pe.wait_ge(s["rows"], 16 * core.row_loads)
            for tile, n in enumerate((P, rest)):
                pe.wait_ge(s["copied"], ND - 3 + tile)
                nc.tensor.transpose(turn[:, tile, 0:n], rows[0:n, tile], core.ident[0:n, 0:n]).then_inc(s["turned"], 1)
    close_stage(core, s)


def finish(core, out):
    nc = core.nc
    with ExitStack() as ctx:
        s, sb, ps = open_stage(core, ctx, "finish", ["turned", "copied", "out"])
        nt = T // P
        tok = sb("tok", [P, nt, D])
        turn = ps("turn", [P, 4, T])
        block = ctx.enter_context(nc.Block())
        steps = [(t, q) for t in range(nt) for q in range(2)]

        @block.tensor
        def _(pe):
            for n, (t, q) in enumerate(steps):
                if n >= 4:
                    pe.wait_ge(s["copied"], n - 3)
                for j in range(4):
                    mm = nc.tensor.transpose(turn[:, n % 4, j * P:(j + 1) * P],
                                             core.x[:, 4 * q + j, t * P:(t + 1) * P], core.ident[:])
                mm.then_inc(s["turned"], 1)

        @block.scalar
        def _(act):
            for n, (t, q) in enumerate(steps):
                act.wait_ge(s["turned"], n + 1)
                nc.scalar.activation(tok[:, t, q * T:(q + 1) * T], turn[:, n % 4], ACT.Copy).then_inc(s["copied"], 1)

        @block.sync
        def _(sp):
            dst = out.rearrange("b (t p) d -> t p (b d)", p=P)
            for t in range(nt):
                sp.wait_ge(s["copied"], 2 * t + 2)
                sp.dma_start(dst[t], tok[:, t]).then_inc(s["out"], 16)
            sp.wait_ge(s["out"], 16 * nt)


def shared_kv(core, kv, k_rot, v_tok, k_cmp, v_cmp):
    ins = core.ins
    project(core, "kv", core.vec("kv_norm"), ins["kv_w"], kv)
    keys = kv[2 * KIND:].rearrange("(b x e p) t -> x e b p t", b=2, x=2, p=P)[0]
    rows = k_rot.rearrange("(b e p) t -> e b p t", b=2, p=P)
    rotate(core, "krot", tile_pairs(keys), 4, [ins["kv_k_norm"][1], ins["kv_k_norm"][2]], None, tile_pairs(rows))
    values(core, "val", kv, v_tok, k_cmp, v_cmp)


def queries_attend(core, shared, yhi, ylo):
    nc, ins = core.nc, core.ins
    scratch = lambda name, rows: nc.dram_tensor(name, (rows, T), F32).ap()
    qg, q_plain, q_rot = scratch("qg_scratch", D + 48), scratch("q_plain_scratch", D), scratch("q_rot_scratch", D)
    project(core, "q", core.vec("norm_mix", 1), ins["nsa_w_q"][0], qg)
    tiles = lambda view: tile_pairs(view.rearrange("(b e p) t -> e b p t", e=2, p=P))
    rotate(core, "qrot", tiles(qg[0:D]), ND, [ins["nsa_q_norm"][0]], tiles(q_plain), tiles(q_rot), scale=C ** -0.5)
    attention(core, "att", q_plain, q_rot, qg[D:], shared["k_rot"], shared["v_tok"], shared["k_cmp"], shared["v_cmp"], yhi, ylo)


def program(nc, ins, consts, out):
    with ExitStack() as ctx:
        core = Core(nc, ctx, ins, consts)
        scratch = lambda name, *shape: nc.dram_tensor(name, shape, F32).ap()
        half_ffn = lambda n, layer: ffn(core, f"ffn{n}_{layer}", core.vec(f"norm_ffn{n}", layer), ins[f"ffn{n}_w_gate"][layer],
                                        ins[f"ffn{n}_w_up"][layer], ins[f"ffn{n}_w_down"][layer])
        setup(core)
        half_ffn(1, 0)
        rkv = scratch("rkv_scratch", 3, D, T)
        with ExitStack() as mixing:
            hold = lambda name, shape, dt=F32: mixing.enter_context(nc.sbuf_tensor(name, shape, dt))
            lora = {n: hold(f"lora_{n}", [P, c, T]) for n, c in (("lw", 1), ("la", 1), ("lg", 2))}
            mix_project(core, "mix", rkv, lora)
            yhi, ylo = hold("y_hi", [P, ND, T], F32R), hold("y_lo", [P, ND, T], F32R)
            recurrence(core, "rec", rkv, lora, yhi, ylo)
            project_add(core, "rwo", yhi, ylo, ins["rw_w_o"][0])
        half_ffn(2, 0)
        shared = {"kv": scratch("kv_scratch", 6 * KIND, T), "k_rot": scratch("k_rot_scratch", 2 * KIND, T),
                  "v_tok": scratch("v_tok_scratch", 4, P, T), "k_cmp": scratch("k_cmp_scratch", C, G * N_CMP),
                  "v_cmp": scratch("v_cmp_scratch", G * N_CMP, C)}
        shared_kv(core, **shared)
        half_ffn(1, 1)
        with ExitStack() as mixing:
            hold = lambda name, shape, dt=F32: mixing.enter_context(nc.sbuf_tensor(name, shape, dt))
            yhi, ylo = hold("o_hi", [P, ND, T], F32R), hold("o_lo", [P, ND, T], F32R)
            queries_attend(core, shared, yhi, ylo)
            project_add(core, "nwo", yhi, ylo, ins["nsa_w_o"][0])
        half_ffn(2, 1)
        finish(core, out)


def constants():
    head = np.kron(np.eye(2), np.ones((64, 64)))
    a, b = np.arange(P)[:, None], np.arange(P)[None, :]
    same = a // C == b // C
    between = lambda n: (a // (2 * n) == b // (2 * n)) & ((a // n) % 2 == 1) & ((b // n) % 2 == 0)
    tables = {
        "c_ident": np.eye(P), "c_head_ones": head,
        "c_masks": np.stack([same & (a < b), same & (a <= b)], 1),
        "c_merge": np.stack([between(n) for n in LEVELS], 1),
        "c_first": np.stack([between(1), between(1).T], 1),
        "c_i64": a % C == np.arange(C)[None, :],
    }
    half = C // 2
    rate = (10000.0 ** (-np.arange(half) / half)).astype(np.float32)
    angle = (np.arange(T, dtype=np.float32)[None, :] * rate[:, None]).astype(np.float64)
    t, n = np.arange(T).reshape(NT, P).T[:, :, None], np.arange(N_CMP)[None, None, :]
    tables["c_causal"] = np.where(b > a, -1e30, 0.0)
    tables["c_cmp_neg"] = np.where(CMP_STRIDE * n + CMP_LEN - 1 > t, -1e30, 0.0)
    tables["c_has_block"] = (np.arange(P)[:, None] >= CMP_LEN - 1)
    tables["c_cos"] = np.tile(np.cos(angle), (4, 1))
    tables["c_sin"] = np.tile(np.concatenate([-np.sin(angle), np.sin(angle)]), (2, 1))
    tables["c_swap"] = (a // C == b // C) & ((a - b) % C == half)
    return {n: np.ascontiguousarray(t).astype(np.float32) for n, t in tables.items()}


_INS = ['x', 'norm_ffn1', 'ffn1_w_gate', 'ffn1_w_up', 'ffn1_w_down', 'norm_mix', 'norm_ffn2', 'ffn2_w_gate',
        'ffn2_w_up', 'ffn2_w_down', 'rw_mu', 'rw_w_rkv', 'rw_w0', 'rw_w_lora_a', 'rw_w_lora_b', 'rw_a0',
        'rw_a_lora_a', 'rw_a_lora_b', 'rw_g_lora_a', 'rw_g_lora_b', 'rw_k_k', 'rw_k_a', 'rw_r_k', 'rw_gn_w',
        'rw_gn_b', 'rw_w_o', 'kv_norm', 'kv_w', 'kv_k_norm', 'cmp_pos_k', 'cmp_k_w1', 'cmp_k_w2', 'cmp_pos_v',
        'cmp_v_w1', 'cmp_v_w2', 'nsa_w_q', 'nsa_q_norm', 'nsa_w_o']


def kernel(**inputs):
    import concourse.bacc as _bacc
    from concourse.bass_utils import run_bass_kernel_spmd as _run

    nc = _bacc.Bacc("TRN2", target_bir_lowering=False, num_devices=1)
    arrays = {f"in_{n}_dram": np.ascontiguousarray(inputs[n]) for n in _INS}
    arrays.update({f"in_{n}_dram": a for n, a in constants().items()})
    aps = {n[3:-5]: nc.dram_tensor(n, a.shape, mybir.dt.from_np(a.dtype), kind="ExternalInput").ap()
           for n, a in arrays.items()}
    out = nc.dram_tensor("out_0_dram", (1, T, D), F32, kind="ExternalOutput").ap()
    program(nc, {n: aps[n] for n in _INS}, {n: aps[n] for n in constants()}, out)
    r = _run(nc, [arrays], core_ids=[0])
    return r.results[0]["out_0_dram"]
```

```python
from contextlib import ExitStack

import numpy as np

import concourse.bass as bass
from concourse import mybir

ALU = mybir.AluOpType
ACT = mybir.ActivationFunctionType
AX = mybir.AxisListType
F32 = mybir.dt.float32
F32R = mybir.dt.float32r

P = 128
T = 512
D = 1024
ND = D // P
F = 2816
NF = F // P
KMAX = 8
SLOTS = 4
EPS = 1e-6
GN_EPS = 64e-5


def fp(view):
    return view.bitcast(F32)


VECTORS = ["norm_ffn1", "norm_mix", "norm_ffn2", "kv_norm", "rw_mu", "rw_w0", "rw_a0", "rw_k_k", "rw_k_a",
           "rw_r_k", "rw_gn_w", "rw_gn_b"]


class Core:

    def __init__(self, nc, ctx, ins, consts):
        self.nc, self.ins, self.consts = nc, ins, consts
        sb = lambda name, shape, dt=F32: ctx.enter_context(nc.sbuf_tensor(name, shape, dt))
        self.x = sb("x_res", [P, ND, T])
        self.ones = sb("ones", [P, P])
        self.head_ones = sb("head_ones", [P, P])
        self.ident = sb("ident", [P, P])
        self.eps = sb("eps", [P, 2])
        self.row, n = {}, 0
        for name in VECTORS:
            self.row[name] = n
            n += int(np.prod(ins[name].shape)) // P
        self.rows = n
        self.vecs = sb("vecs", [P, n])
        self.zero = sb("zero", [P, 1])
        self.sq = sb("sq", [P, 2, T])
        self.sq_sum = sb("sq_sum", [P, T])
        self.raw = sb("w_raw", [P, SLOTS, KMAX, P])
        self.early = [nc.alloc_semaphore(f"early{j}") for j in range(SLOTS)]
        self.stages = 0

    def vec(self, name, index=0):
        r = self.row[name] + ND * index
        return self.vecs[:, r:r + ND]


def open_ring(core, sb):
    core.stages += 1
    core.whi = sb("w_hi", [P, SLOTS, KMAX, P], F32R)
    core.wlo = sb("w_lo", [P, SLOTS, KMAX, P], F32R)


def open_stage(core, ctx, tag, names):
    nc = core.nc
    s = {n: nc.alloc_semaphore(f"{n}_{tag}") for n in names}
    sb = lambda name, shape, dt=F32: ctx.enter_context(nc.sbuf_tensor(f"{name}_{tag}", shape, dt))
    ps = lambda name, shape: ctx.enter_context(nc.psum_tensor(f"{name}_{tag}", shape, F32))
    return s, sb, ps


def close_stage(core, s):
    nc = core.nc
    with nc.Block() as block:
        @block.sync
        def _(sp):
            for sem in s.values():
                sp.sem_clear(sem)
    for sem in s.values():
        nc.release_semaphore(sem)


def one(i):
    return bass.ds(i, 1)


def flat(view):
    return view.rearrange("p a t -> p (a t)")


def done(unit):
    return unit + (SLOTS + 1)


def first_units(weights):
    w = weights.rearrange("(k p) e -> p k e", p=P)
    return [w[:, :, j * P:(j + 1) * P] for j in range(SLOTS)]


def load_ahead(sp, core, sources):
    for j, source in enumerate(sources):
        sp.dma_start(core.raw[:, j, 0:source.shape[1], 0:source.shape[2]], source).then_inc(core.early[j], 16)


def load_unit(sp, s, core, slot, count, source):
    sp.wait_ge(s["w_ready"], count + 1)
    k = source.shape[1]
    sp.dma_start(core.raw[:, slot, 0:k, 0:source.shape[2]], source).then_inc(s[f"raw{slot}"], 16)


def split_unit(dve, s, core, slot, rounds, count, k, m=P):
    nc = core.nc
    if isinstance(count, int) and count < SLOTS:
        dve.wait_ge(core.early[slot], 16 * core.stages)
    else:
        dve.wait_ge(s[f"raw{slot}"], 16 * rounds)
    dve.wait_ge(s["w_free"], count + 1)
    raw, hi, lo = (t[:, slot, 0:k, 0:m] for t in (core.raw, core.whi, core.wlo))
    nc.vector.tensor_copy(hi, raw).then_inc(s["w_hi"], 1)
    dve.wait_ge(s["w_hi"], count + 1)
    nc.vector.tensor_tensor(lo, raw, fp(hi), ALU.subtract).then_inc(s["w_ready"], 1)


def three_passes(core, out, slot, k, hi, lo, first, last):
    nc = core.nc
    whi, wlo = core.whi[:, slot, k], core.wlo[:, slot, k]
    nc.tensor.matmul(out, whi, hi, start=first, stop=False)
    nc.tensor.matmul(out, whi, lo, start=False, stop=False)
    return nc.tensor.matmul(out, wlo, hi, start=False, stop=last)


NORM_SEMS = ["h_hi", "h_lo", "ms_mm", "ms", "rstd", "sq_0", "sq_sum_0"]


def square_tiles(core, act, s, x_done=None, sq="sq", sq_sum="sq_sum"):
    for d in range(ND):
        if x_done:
            act.wait_ge(s[x_done[0]], x_done[1] + d)
        if d >= 2:
            act.wait_ge(s[sq_sum], d - 1)
        core.nc.scalar.activation(core.sq[:, d % 2], core.x[:, d], ACT.Square).then_inc(s[sq], 1)


def sum_squares(core, pool, s, sq="sq", sq_sum="sq_sum"):
    for d in range(ND):
        pool.wait_ge(s[sq], d + 1)
        if d:
            pool.wait_ge(s[sq_sum], d)
        before = core.sq_sum[:] if d else core.zero[:, 0:1].to_broadcast([P, T])
        core.nc.gpsimd.tensor_tensor(core.sq_sum[:], core.sq[:, d % 2], before, ALU.add).then_inc(s[sq_sum], 1)
    pool.wait_ge(s[sq_sum], ND)


class Norm:

    def __init__(self, core, s, sb, p_ms, gain, first=False):
        self.first = first
        self.core, self.s, self.gain, self.p_ms = core, s, gain, p_ms
        self.hi = sb("hhi", [P, ND, T], F32R)
        self.lo = sb("hlo", [P, ND, T], F32R)
        self.ms = sb("ms", [P, T])
        self.rstd = sb("rstd", [P, T])

    def scalar(self, act):
        core, s = self.core, self.s
        A = core.nc.scalar.activation
        for d in range(ND):
            A(self.hi[:, d], core.x[:, d], ACT.Copy, scale=self.gain[:, d:d + 1]).then_inc(s["h_hi"], 1)
        if self.first:
            square_tiles(core, act, s, None, "sq_0", "sq_sum_0")
        act.wait_ge(s["ms_mm"], 1)
        A(self.ms[:], self.p_ms[:], ACT.Sqrt, scale=1.0 / D, bias=core.eps[:, 0:1]).then_inc(s["ms"], 1)

    def vector_low(self, dve, tiles):
        for d in tiles:
            dve.wait_ge(self.s["h_hi"], d + 1)
            self.core.nc.vector.scalar_tensor_tensor(out=self.lo[:, d], in0=self.core.x[:, d], scalar=self.gain[:, d:d + 1],
                                                     in1=fp(self.hi[:, d]), op0=ALU.mult, op1=ALU.subtract).then_inc(self.s["h_lo"], 1)

    def vector_rstd(self, dve):
        dve.wait_ge(self.s["ms"], 1)
        self.core.nc.vector.reciprocal(self.rstd[:], self.ms[:]).then_inc(self.s["rstd"], 1)
        dve.wait_ge(self.s["rstd"], 1)

    def gpsimd(self, pool):
        if self.first:
            sum_squares(self.core, pool, self.s, "sq_0", "sq_sum_0")

    def tensor(self, pe):
        if self.first:
            pe.wait_ge(self.s["sq_sum_0"], ND)
        self.core.nc.tensor.matmul(self.p_ms[:], self.core.ones[:], self.core.sq_sum[:], start=True, stop=True).then_inc(self.s["ms_mm"], 1)


FFN_SEMS = ["raw0", "raw1", "raw2", "raw3", "w_free", "w_hi", "w_ready", "gate", "gu_free", "x_done", "a_lo", "a_hi",
            "act32", "silu", "sq", "sq_sum", "ready"] + NORM_SEMS


def ffn_first_units(w_gate, w_up):
    return [first_units(w)[j // 2] for j, w in enumerate((w_gate, w_up, w_gate, w_up))]


def ffn(core, tag, x_gain, w_gate, w_up, w_down, ahead):
    nc = core.nc
    groups = [(f0, min(KMAX, NF - f0)) for f0 in range(0, NF, KMAX)]
    gate = w_gate.rearrange("(k p) f -> p k f", p=P)
    up = w_up.rearrange("(k p) f -> p k f", p=P)
    down = w_down.rearrange("(k p) d -> p k d", p=P)
    with ExitStack() as ctx:
        s, sb, ps = open_stage(core, ctx, tag, FFN_SEMS)
        open_ring(core, sb)
        gated = sb("gated", [P, T])
        gsc, usc = sb("gsc", [P, 2, T]), sb("usc", [P, 2, T])
        act32 = sb("act32", [P, T])
        ahi = sb("ahi", [P, KMAX, T], F32R)
        alo = sb("alo", [P, KMAX, T], F32R)
        p_gate = ps("p_gate", [P, 2, T])
        p_up = ps("p_up", [P, 2, T])
        p_down = ps("p_down", [P, 2, T])
        norm = Norm(core, s, sb, ps("p_ms", [P, T]), x_gain, first=(core.stages == 1))
        block = ctx.enter_context(nc.Block())

        @block.sync
        def _(sp):
            unit = 0
            for f0, nf in groups:
                skip = 1 if f0 == 0 else 0
                with sp.Fori(0, nf // 2 - skip) as i:
                    for j in range(4):
                        w = gate if j % 2 == 0 else up
                        src = w[:, :, bass.ds(2 * P * i + (f0 + 2 * skip + j // 2) * P, P)]
                        load_unit(sp, s, core, j, 4 * i + (unit + 4 * skip + j), src)
                unit += 2 * nf
                with sp.Fori(0, ND // 4) as i:
                    for j in range(4):
                        src = down[:, f0:f0 + nf, bass.ds(4 * P * i + j * P, P)]
                        load_unit(sp, s, core, j, 4 * i + (unit + j), src)
                unit += ND
            sp.wait_ge(s["w_ready"], done(unit - 1))
            load_ahead(sp, core, ahead)

        @block.vector
        def _(dve):
            dve.sem_inc(s["w_ready"], SLOTS)
            dve.sem_inc(s["gu_free"], 2)
            dve.sem_inc(s["x_done"], 2)
            split = lambda i, unit, j: split_unit(dve, s, core, j, i + unit // 4, 4 * i + (unit + j), KMAX)
            split(0, 0, 0)
            norm.vector_low(dve, range(ND))
            for j in range(1, 4):
                split(0, 0, j)
            norm.vector_rstd(dve)
            unit, ftile = 0, 0
            for f0, nf in groups:
                with dve.Fori(0, nf // 2) as i:
                    for j in range(2):
                        f = 2 * i + (ftile + j)
                        dve.wait_ge(s["w_free"], done(4 * i + (unit + 2 * j + 1)))
                        dve.wait_ge(s["silu"], f + 1)
                        nc.vector.tensor_tensor(gsc[:, j], p_gate[:, j], norm.rstd[:], ALU.mult).then_inc(s["gate"], 1)
                        dve.wait_ge(s["act32"], f + 1)
                        nc.vector.tensor_tensor(usc[:, j], p_up[:, j], norm.rstd[:], ALU.mult).then_inc(s["gu_free"], 1)
                        split(i, unit + 4, 2 * j)
                        split(i, unit + 4, 2 * j + 1)
                unit += 2 * nf
                ftile += nf
                for d in range(ND):
                    dve.wait_ge(s["w_free"], done(unit + d))
                    if f0 == 0:
                        dve.wait_ge(s["h_lo"], ND)
                    nc.vector.scalar_tensor_tensor(out=core.x[:, d], in0=p_down[:, d % 2], scalar=0.5, in1=core.x[:, d],
                                                   op0=ALU.mult, op1=ALU.add).then_inc(s["x_done"], 1)
                    if f0 + nf < NF or d < ND - 4:
                        split(d // 4, unit + 4, d % 4)
                unit += ND

        @block.tensor
        def _(pe):
            pe.sem_inc(s["w_free"], SLOTS)
            if not norm.first:
                norm.tensor(pe)
            unit, ftile, dtile = 0, 0, 0
            for f0, nf in groups:
                def gate_up(i, first):
                    for j in range(4):
                        out = (p_gate if j % 2 == 0 else p_up)[:, j // 2]
                        pe.wait_ge(s["w_ready"], done(4 * i + (unit + j)))
                        if j % 2 == 0:
                            pe.wait_ge(s["gu_free"], 2 * i + (ftile + j // 2 + 1))
                        for k in range(ND):
                            if first and j == 0:
                                pe.wait_ge(s["h_lo"], k + 1)
                            mm = three_passes(core, out, j, k, norm.hi[:, k], norm.lo[:, k], k == 0, k == ND - 1)
                        mm.then_inc(s["w_free"], 1)
                        if first and norm.first and j == 1:
                            norm.tensor(pe)
                if f0 == 0:
                    gate_up(0, True)
                    with pe.Fori(0, nf // 2 - 1) as i:
                        gate_up(i + 1, False)
                else:
                    with pe.Fori(0, nf // 2) as i:
                        gate_up(i, False)
                unit += 2 * nf
                ftile += nf
                with pe.Fori(0, ND // 4) as i:
                    for j in range(4):
                        out = p_down[:, j % 2]
                        pe.wait_ge(s["w_ready"], done(4 * i + (unit + j)))
                        pe.wait_ge(s["x_done"], 4 * i + (dtile + j + 1))
                        for k in range(nf):
                            if j == 0:
                                pe.wait_ge(s["a_lo"], f0 + k + 2)
                            mm = three_passes(core, out, j, k, ahi[:, k], alo[:, k], k == 0, k == nf - 1)
                        mm.then_inc(s["w_free"], 1)
                unit += ND
                dtile += ND

        @block.scalar
        def _(act):
            act.sem_inc(s["silu"], 1)
            norm.scalar(act)
            ftile = 0
            for f0, nf in groups:
                with act.Fori(0, nf // 2) as i:
                    for j in range(2):
                        f = 2 * i + (ftile + j)
                        act.wait_ge(s["gate"], f + 1)
                        act.wait_ge(s["act32"], f + 1)
                        nc.scalar.activation(gated[:], gsc[:, j], ACT.Silu).then_inc(s["silu"], 1)
                        act.wait_ge(s["act32"], f + 2)
                        act.sem_inc(s["ready"], 1)
                        nc.scalar.activation(flat(ahi[:, one(2 * i + j)]), act32[:], ACT.Copy).then_inc(s["a_hi"], 1)
                ftile += nf
            square_tiles(core, act, s, ("x_done", 2 + (len(groups) - 1) * ND + 1))

        @block.gpsimd
        def _(pool):
            pool.sem_inc(s["act32"], 1)
            pool.sem_inc(s["a_lo"], 1)
            norm.gpsimd(pool)
            ftile = 0
            for f0, nf in groups:
                with pool.Fori(0, nf // 2) as i:
                    for j in range(2):
                        f = 2 * i + (ftile + j)
                        pool.wait_ge(s["silu"], f + 2)
                        pool.wait_ge(s["gu_free"], f + 3)
                        pool.wait_ge(s["a_lo"], f + 1)
                        nc.gpsimd.tensor_tensor(act32[:], gated[:], usc[:, j], ALU.mult).then_inc(s["act32"], 1)
                        pool.wait_ge(s["a_hi"], f + 1)
                        pool.sem_inc(s["ready"], 1)
                        nc.gpsimd.tensor_tensor(flat(alo[:, one(2 * i + j)]), act32[:], flat(fp(ahi[:, one(2 * i + j)])),
                                                ALU.subtract).then_inc(s["a_lo"], 1)
                ftile += nf
            sum_squares(core, pool, s)
    close_stage(core, s)


PASSES = [("r", 0, ND), ("lw", 1, 1), ("k", 2, ND), ("la", 4, 1), ("v", 3, ND), ("lg", 5, 2)]
MAIN = ("r", "k", "v")

MIX_SEMS = ["raw0", "raw1", "raw2", "raw3", "w_free", "w_hi", "w_ready", "rstd", "h", "ms_mm", "ms",
            "dx", "mix32", "mix_hi", "mix_lo", "out", "st0", "st1", "st2", "st3", "ready", "pad"]


def mix_project(core, tag, rkv, lora):
    nc, ins = core.nc, core.ins
    wide = [ins["rw_w_rkv"][0, c].rearrange("(k p) e -> p k e", p=P) for c in range(3)]
    narrow = {"lw": ins["rw_w_lora_a"][0], "la": ins["rw_a_lora_a"][0], "lg": ins["rw_g_lora_a"][0]}
    widths = {"lw": [narrow["lw"].shape[1]], "la": [narrow["la"].shape[1]], "lg": [P, narrow["lg"].shape[1] - P]}
    first, n = {}, 0
    for name, _, units in PASSES:
        first[name] = n
        n += units
    buf = {"r": 0, "lw": 1, "k": 2, "la": 1, "v": 0, "lg": 1}
    beside = {"r": ["lw", "k"], "k": ["la", "v"], "v": ["lg"]}
    began = {"r": ND, "k": 3 * ND, "v": 5 * ND}
    complete = {"lw": 3 * ND - 1, "k": 3 * ND, "la": 5 * ND - 1, "v": 5 * ND, "lg": 6 * ND}
    mu_row = {name: c for name, c, _ in PASSES}

    with ExitStack() as ctx:
        s, sb, ps = open_stage(core, ctx, tag, MIX_SEMS)
        open_ring(core, sb)
        h = sb("h", [P, ND, T + 1])
        dx = [core.sq_sum, sb("dx", [P, T])]
        mix32 = sb("mix32", [P, 4, T])
        ms, rstd = core.sq[:, 0], core.sq[:, 1]
        mhi = sb("mhi", [P, 3, ND, T], F32R)
        mlo = sb("mlo", [P, 3, ND, T], F32R)
        staged = sb("staged", [P, 2, T])
        p_ms = ps("p_ms", [P, T])
        p_out = ps("p_out", [P, 4, T])
        block = ctx.enter_context(nc.Block())

        def units_of(eng, name, body, unrolled=False):
            base, n = first[name], dict((a, c) for a, _, c in PASSES)[name]
            if name == "r" and unrolled:
                for u in range(n):
                    body(u, u % 4, u // 4, u, u % 4)
            elif name in MAIN:
                with eng.Fori(0, n // 4) as i:
                    for j in range(4):
                        body(4 * i + (base + j), (base + j) % 4, i + (base + j) // 4, 4 * i + j, j)
            else:
                for j in range(n):
                    body(base + j, (base + j) % 4, (base + j) // 4, j, j)

        @block.sync
        def _(sp):
            for name, _, n in PASSES:
                def load(unit, slot, rounds, e, j):
                    if isinstance(unit, int) and unit < SLOTS:
                        return
                    if name in MAIN:
                        src = wide[MAIN.index(name)][:, :, bass.ds(e * P, P)]
                    else:
                        m = widths[name][j]
                        src = narrow[name].rearrange("(k p) e -> p k e", p=P)[:, :, j * P:j * P + m]
                    load_unit(sp, s, core, slot, unit, src)
                units_of(sp, name, load, unrolled=True)
            sp.wait_ge(s["w_ready"], done(sum(n for _, _, n in PASSES) - 1))
            load_ahead(sp, core, first_units(ins["rw_w_o"][0]))

        @block.vector
        def _(dve):
            dve.sem_inc(s["w_ready"], SLOTS)
            dve.sem_inc(s["ready"], 1)
            for view in (lora["lw"][:, 0], lora["la"][:, 0], lora["lg"][:, 1]):
                nc.vector.memset(view, 0.0)
            nc.vector.memset(h[:, :, 0:1], 0.0).then_inc(s["pad"], 1)

            def mix_tile(name, m, slot, d):
                mu = core.vec("rw_mu", mu_row[name])
                mu = mu[:, d:d + 1] if isinstance(d, int) else mu[:, one(d)]
                hd = h[:, d:d + 1] if isinstance(d, int) else h[:, one(d)]
                dve.wait_ge(s["mix_hi"], m + 1)
                nc.vector.tensor_tensor(dx[slot % 2][:], flat(hd[:, :, 0:T]), flat(hd[:, :, 1:T + 1]),
                                        ALU.subtract).then_inc(s["dx"], 1)
                dve.wait_ge(s["dx"], m + 1)
                dve.wait_ge(s["mix_lo"], m + 1)
                nc.vector.scalar_tensor_tensor(out=mix32[:, slot], in0=dx[slot % 2][:], scalar=mu,
                                               in1=flat(hd[:, :, 1:T + 1]), op0=ALU.mult, op1=ALU.add).then_inc(s["mix32"], 1)

            split_unit(dve, s, core, 0, 0, 0, ND)
            dve.wait_ge(s["ms"], 1)
            nc.vector.reciprocal(rstd[:], ms[:]).then_inc(s["rstd"], 1)
            dve.wait_ge(s["rstd"], 1)
            dve.wait_ge(s["pad"], 1)
            gain = core.vec("norm_mix", 0)
            for d in range(ND):
                nc.vector.scalar_tensor_tensor(out=h[:, d, 1:T + 1], in0=core.x[:, d], scalar=gain[:, d:d + 1],
                                               in1=rstd[:], op0=ALU.mult, op1=ALU.mult).then_inc(s["h"], 1)
                dve.wait_ge(s["h"], d + 1)
                mix_tile("r", d, d % 4, d)
            for name, _, n in PASSES:
                def step(unit, slot, rounds, e, j):
                    m = P if name in MAIN else widths[name][j]
                    if not (isinstance(unit, int) and unit == 0):
                        split_unit(dve, s, core, slot, rounds, unit, ND, m)
                    for b, other in enumerate(beside.get(name, [])):
                        made = len(beside[name])
                        mix_tile(other, e * made + (began[name] + b), (made * j + b) % 4, e)
                units_of(dve, name, step, unrolled=True)

        @block.scalar
        def _(act):
            act.sem_inc(s["mix_hi"], 4)
            act.sem_inc(s["out"], 4)
            act.wait_ge(s["ms_mm"], 1)
            nc.scalar.activation(ms[:], p_ms[:], ACT.Sqrt, scale=1.0 / D, bias=core.eps[:, 0:1]).then_inc(s["ms"], 1)

            def round_tile(name, m, slot, d):
                act.wait_ge(s["mix32"], m + 1)
                act.wait_ge(s["ready"], 1)
                dst = mhi[:, buf[name], d] if isinstance(d, int) else flat(mhi[:, buf[name], one(d)])
                nc.scalar.activation(dst, mix32[:, slot], ACT.Copy).then_inc(s["mix_hi"], 1)

            for d in range(ND):
                round_tile("r", d, d % 4, d)
            for name, _, n in PASSES:
                def step(unit, slot, rounds, e, j):
                    for b, other in enumerate(beside.get(name, [])):
                        made = len(beside[name])
                        round_tile(other, e * made + (began[name] + b), (made * j + b) % 4, e)
                    act.wait_ge(s["w_free"], done(unit))
                    if name in MAIN:
                        before = MAIN.index(name) * ND
                        turn = j % 2
                        act.wait_ge(s[f"st{turn}"], 8 * e + (8 * before - 8 * turn + 16))
                        nc.scalar.activation(staged[:, turn], p_out[:, slot], ACT.Copy).then_inc(s["out"], 1)
                        act.wait_ge(s["out"], unit + 5)
                        dst = rkv[MAIN.index(name)].rearrange("(e p) t -> e p t", p=P)[one(e)].rearrange("a p t -> p (a t)")
                        act.dma_start(dst, staged[:, turn]).then_inc(s[f"st{turn}"], 16)
                    else:
                        m = widths[name][j]
                        act.wait_ge(s["pad"], 1)
                        func = {"lw": ACT.Tanh, "la": ACT.Copy, "lg": ACT.Sigmoid}[name]
                        nc.scalar.activation(lora[name][0:m, j], p_out[0:m, slot], func).then_inc(s["out"], 1)
                units_of(act, name, step)
            for turn in range(2):
                act.wait_ge(s[f"st{turn}"], 16 * (3 * ND // 2 + 1))

        @block.gpsimd
        def _(pool):
            pool.sem_inc(s["mix_lo"], 4)
            pool.sem_inc(s["st0"], 16)
            pool.sem_inc(s["st1"], 16)

            def low_tile(name, m, slot, d):
                pool.wait_ge(s["mix_hi"], m + 5)
                pool.wait_ge(s["ready"], 1)
                if isinstance(d, int):
                    dst, hi = mlo[:, buf[name], d], fp(mhi[:, buf[name], d])
                else:
                    dst, hi = flat(mlo[:, buf[name], one(d)]), flat(fp(mhi[:, buf[name], one(d)]))
                nc.gpsimd.tensor_tensor(dst, mix32[:, slot], hi, ALU.subtract).then_inc(s["mix_lo"], 1)

            for d in range(ND):
                low_tile("r", d, d % 4, d)
            for name in MAIN:
                def step(unit, slot, rounds, e, j):
                    for b, other in enumerate(beside[name]):
                        made = len(beside[name])
                        low_tile(other, e * made + (began[name] + b), (made * j + b) % 4, e)
                units_of(pool, name, step)

        @block.tensor
        def _(pe):
            pe.sem_inc(s["w_free"], SLOTS)
            nc.tensor.matmul(p_ms[:], core.ones[:], core.sq_sum[:], start=True, stop=True).then_inc(s["ms_mm"], 1)
            for name, _, n in PASSES:
                if name in complete:
                    pe.wait_ge(s["mix_lo"], complete[name] + 4)
                def step(unit, slot, rounds, e, j):
                    pe.wait_ge(s["w_ready"], done(unit))
                    pe.wait_ge(s["out"], unit + 1)
                    for k in range(ND):
                        if name == "r" and j == 0:
                            pe.wait_ge(s["mix_lo"], k + 5)
                        mm = three_passes(core, p_out[:, slot], slot, k, mhi[:, buf[name], k], mlo[:, buf[name], k],
                                          k == 0, k == ND - 1)
                    mm.then_inc(s["w_free"], 1)
                units_of(pe, name, step)
    close_stage(core, s)


PAIR_EVENTS = {
    "loaded": 16 * 3, "lora_w": 16 * 4, "cur": 1, "zp": 1, "ap": 1, "tw": 1, "ta": 1, "sqk": 1, "ssk": 1, "clip": 1, "lnk": 1,
    "inv": 1, "sg": 1, "cum": 1, "ctr": 1, "qsum": 1, "cc": 1, "ce": 1, "eex": 1, "ep": 1, "em": 1, "q": 1, "pk": 6,
    "tilde": 4, "rk": 1, "bsum": 1, "bon": 1, "gp": 1, "gsb": 1, "vturn": 1, "vtok": 1, "turn": 3, "tok": 3,
    "score": 6, "bl": 4, "kl": 4, "nm": 2, "x_init": 6, "lakv": 1, "aw": 1, "g_mm": 10, "g": 10,
    "x_mm": 10, "x": 10, "au_mm": 2, "au": 2, "rp_mm": 1, "rp": 1, "f_mm": 1, "f": 1, "z_mm": 1, "z": 1,
    "chain": 6, "state": 6, "y_mm": 1, "ysb": 1, "mean": 1, "dev": 1, "sqy": 1, "var": 1, "lny": 1, "rs": 1,
    "yn": 3, "yhi": 1, "pair": 1, "pad": 4, "xv": 8, "spread": 4, "ublk": 2,
}
PARTS, FINISH_PARTS = 7, 3
C = 64
NC_ = T // C
NT = T // P
KAPPA = float(np.exp(-0.5))
LEVELS = (2, 4, 8, 16, 32)
LN_SCALE = 2.0 ** 16
W0H, A0H, KK, HKA, OKA, RK, GNW, GNB = range(8)


def recurrence(core, tag, rkv, lora, yhi, ylo):
    nc, ins = core.nc, core.ins
    with ExitStack() as ctx:
        s, sb, ps = open_stage(core, ctx, tag, list(PAIR_EVENTS) + ["ready", "consts", "pv", "zeroed"])

        def at(eng, p, name, k):
            eng.wait_ge(s[name], p * PAIR_EVENTS[name] + k)

        def plain(eng):
            eng.sem_inc(s["ready"], 1)

        def steps(eng, prepare, step, finish):
            for part in range(PARTS):
                prepare(0, 0, part)
            step(0, 0, True, False)
            with eng.Fori(0, ND // 2 - 1) as i:
                step(2 * i + 1, 1, False, False)
                step(2 * i + 2, 0, False, False)
            step(ND - 1, 1, False, True)
            for part in range(FINISH_PARTS):
                finish(ND - 1, 1, part)

        row = lambda name: sb(name, [P, T])
        slots = lambda name, shape: [sb(f"{name}{n}", shape) for n in range(2)]
        masks = sb("masks", [P, 2, P])
        merge = sb("merge", [P, 5, P])
        first_level = sb("first", [P, 2, P])
        i64 = sb("i64", [P, C])
        resets = row("resets")
        half_log = sb("half_log", [P, 1])
        pv = sb("pv", [P, ND, 8])
        cur = slots("cur", [P, 8])
        r, k, v = row("r"), row("k"), row("v")
        wb, ab, gb = sb("wb", [P, P]), sb("ab", [P, P]), sb("gb", [P, 2, P])
        sg, cum, ce = row("sg"), row("cum"), row("ce")
        cc = cum
        ta = row("ta")
        tw = sg
        ctr, qs, q = sb("ctr", [P, NC_]), sb("qs", [P, NC_]), slots("q", [P, NC_])
        eex, ep, em = ce, sg, cc
        sqk, kk0, kf, a1 = (row(n) for n in ("sqk", "kk0", "kf", "a1"))
        inv, kp = sqk, kf
        kk, beta = kk0, a1
        rk = core.sq_sum
        bon, gsb = slots("bon", [P, T]), slots("gsb", [P, T])
        ar = slots("ar", [P, NT, 2, P])
        bt, kt = row("bt"), row("kt")
        bz = [sb(f"bz{h}", [P, T]) for h in range(2)]
        kz = [sb(f"kz{h}", [P, T]) for h in range(2)]
        vtok, btok, ktok = (slots(n, [P, NT, P]) for n in ("vtok", "btok", "ktok"))
        aw = slots("aw", [P, NT, 2, P])
        bl = [sb(f"bl{h}", [P, NT, 2, P]) for h in range(2)]
        kl = [sb(f"kl{h}", [P, NT, 2, P]) for h in range(2)]
        x = [sb(f"x{h}", [P, NT, P]) for h in range(2)]
        xt = [sb(f"xt{h}", [P, NT, P]) for h in range(2)]
        g = [sb(f"g{h}", [P, NT, P]) for h in range(2)]
        au = g
        rp, ft, zq, st = row("rp"), sb("ft", [P, NC_, C]), sb("zq", [P, NC_, C]), sb("st", [P, NC_, C])
        bblk, vblk, ublk = (sb(n, [P, NT, 2, 2, C]) for n in ("bblk", "vblk", "ublk"))
        ysb, rs = core.sq[:, 0], core.sq[:, 1]
        dev, sqy, yn = ysb, rs, ysb
        bank = ps("bank", [P, 8, T])
        block = ctx.enter_context(nc.Block())

        def tiles(view):
            return view.rearrange("p (t c) -> p t c", t=NT)

        def by_chunks(view):
            return view.rearrange("p t (a c) -> p t a c", a=1).to_broadcast([P, NT, 2, C])

        chunks = core.head_ones[:].rearrange("p (o a c) -> p o a c", o=1, a=2).to_broadcast([P, NT, 2, C])

        @block.sync
        def _(sp):
            def load(p, first):
                if not first:
                    at(sp, p - 1, "bon", 1)
                    at(sp, p - 1, "tilde", 4)
                    at(sp, p - 1, "pk", 4)
                    at(sp, p - 1, "sqk", 1)
                for c, dst in enumerate((r, k, v)):
                    src = rkv[c].rearrange("(e p) t -> e p t", p=P)[one(p)].rearrange("a p t -> p (a t)")
                    sp.dma_start(dst[:], src).then_inc(s["loaded"], 16)
                if not first:
                    at(sp, p - 1, "gsb", 1)
                else:
                    sp.wait_ge(s["zeroed"], 1)
                cols = bass.ds(p * P, P)
                for dst, src in ((wb[0:C], ins["rw_w_lora_b"][0][:, cols]), (ab[0:C], ins["rw_a_lora_b"][0][:, cols]),
                                 (gb[:, 0], ins["rw_g_lora_b"][0][0:P, cols]),
                                 (gb[0:32, 1], ins["rw_g_lora_b"][0][P:P + 32, cols])):
                    sp.dma_start(dst, src).then_inc(s["lora_w"], 16)

            load(0, True)
            for dst, name in ((masks, "c_masks"), (merge, "c_merge"), (first_level, "c_first")):
                sp.dma_start(dst[:], core.consts[name]).then_inc(s["consts"], 16)
            sp.dma_start(i64[:], core.consts["c_i64"]).then_inc(s["consts"], 16)
            with sp.Fori(0, ND - 1) as i:
                load(i + 1, False)

        @block.tensor
        def _(pe):
            def prepare(p, slot, part):
                if part == 0:
                    at(pe, p, "lora_w", 64)
                    if not (isinstance(p, int) and p == 0):
                        at(pe, p - 1, "nm", 2)
                        at(pe, p - 1, "aw", 1)
                    nc.tensor.matmul(bank[:, 4], wb[:], lora["lw"][:, 0], start=True, stop=True).then_inc(s["zp"], 1)
                    nc.tensor.matmul(bank[:, 5], ab[:], lora["la"][:, 0], start=True, stop=True).then_inc(s["ap"], 1)
                if part == 1:
                    at(pe, p, "sqk", 1)
                    at(pe, p, "tw", 1)
                    nc.tensor.matmul(bank[:, 4], core.head_ones[:], sqk[:], start=True, stop=True).then_inc(s["ssk"], 1)
                    at(pe, p, "ta", 1)
                    nc.tensor.matmul(bank[:, 5], gb[:, 0], lora["lg"][:, 0], start=True, stop=False)
                    nc.tensor.matmul(bank[:, 5], gb[:, 1], lora["lg"][:, 1], start=False, stop=True).then_inc(s["gp"], 1)
                if part == 2:
                    at(pe, p, "loaded", 48)
                    at(pe, p, "clip", 1)
                    for t in range(NT):
                        mm = nc.tensor.transpose(bank[:, 4, t * P:(t + 1) * P], v[:, t * P:(t + 1) * P], core.ident[:])
                    mm.then_inc(s["vturn"], 1)
                if part == 3:
                    at(pe, p, "rk", 1)
                    at(pe, p, "gsb", 1)
                    nc.tensor.matmul(bank[:, 5], core.head_ones[:], rk[:], start=True, stop=True).then_inc(s["bsum"], 1)
                if part >= 4:
                    n = part - 4
                    src = (ar[slot][:, :, 0], tiles(bt[:]), tiles(kt[:]))[n]
                    at(pe, p, "tilde", 4)
                    if n == 2:
                        at(pe, p, "tok", 1)
                    for t in range(NT):
                        mm = nc.tensor.transpose(bank[:, 7 - n % 2, t * P:(t + 1) * P], src[:, t], core.ident[:])
                    mm.then_inc(s["turn"], 1)

            def finish(p, slot, part):
                if part == 0:
                    if not (isinstance(p, int) and p == ND - 1):
                        at(pe, p + 1, "tok", 2)
                    at(pe, p, "ysb", 1)
                    nc.tensor.matmul(bank[:, 6], core.head_ones[:], ysb[:], start=True, stop=True).then_inc(s["mean"], 1)
                if part == 1:
                    at(pe, p, "sqy", 1)
                    nc.tensor.matmul(bank[:, 6], core.head_ones[:], sqy[:], start=True, stop=True).then_inc(s["var"], 1)

            def step(p, slot, first, last):
                A, V_, B_, K_ = ar[slot], vtok[slot], btok[slot], ktok[slot]
                at(pe, p, "tilde", 4)
                at(pe, p, "pad", 4)
                if first:
                    at(pe, p, "vtok", 1)
                    at(pe, p, "bon", 1)
                for h in range(2):
                    for n, rhs in enumerate((bz, kz)):
                        if h == 1:
                            at(pe, p, "bl" if n == 0 else "kl", 2)
                        for t in range(NT):
                            out = bank[:, 2 * n + t // 2, (t % 2) * 2 * P:(t % 2 + 1) * 2 * P]
                            mm = nc.tensor.matmul(out, rhs[h][:, t * P:(t + 1) * P], A[:, t].rearrange("p a c -> p (a c)"),
                                                  start=True, stop=True)
                        mm.then_inc(s["score"], 1)
                        if n == 0 and not first:
                            finish(p - 1, 1 - slot, h)
                    if h == 1:
                        at(pe, p, "tok", 3)
                    for t in range(NT):
                        mm = nc.tensor.matmul(bank[:, 4 if h == 0 else 7, t * P:(t + 1) * P], A[:, t, 0],
                                              bz[h][:, t * P:(t + 1) * P], start=True, stop=True)
                    mm.then_inc(s["score"], 1)
                def lak_v():
                    at(pe, p, "kl", 4)
                    for h in range(2):
                        for t in range(NT):
                            mm = nc.tensor.matmul(bank[:, 5, (t * 2 + h) * C:(t * 2 + h + 1) * C], kl[h][:, t, 0],
                                                  V_[:, t, C * h:C * h + C], start=True, stop=True)
                    mm.then_inc(s["lakv"], 1)

                for level in range(len(LEVELS)):
                    over = level == len(LEVELS) - 1
                    for h in range(2):
                        if level == 0:
                            at(pe, p, "x_init", 3 * h + 3)
                            at(pe, p, "nm", h + 1)
                            at(pe, p, "bl", 4)
                            if h == 0:
                                at(pe, p, "tok", 2)
                            if h == 0 and not first:
                                at(pe, p - 1, "lny", 1)
                        else:
                            at(pe, p, "xv", 2 * (level - 1) + h + 1)
                        for t in range(NT):
                            mm = nc.tensor.matmul(bank[:, 6 + h, t * P:(t + 1) * P], bl[h][:, t, 0], x[h][:, t], start=True, stop=True)
                        mm.then_inc(s["g_mm"], 1)
                        if level == 0 and h == 0:
                            lak_v()
                    if not last and level < 4:
                        prepare(p + 1, 1 - slot, level)
                    for h in range(2):
                        at(pe, p, "g", 2 * level + h + 1)
                        for t in range(NT):
                            cs = slice(t * P, (t + 1) * P)
                            mm = nc.tensor.matmul(bank[:, 2 * h + 1, cs], g[h][:, t], xt[h][:, t], start=True, stop=True)
                            if not over:
                                mm = nc.tensor.matmul(bank[:, 2 * h, cs], xt[h][:, t], g[h][:, t], start=True, stop=True)
                        mm.then_inc(s["x_mm"], 1)
                at(pe, p, "aw", 1)
                for h in range(2):
                    at(pe, p, "x", 8 + h + 1)
                    for t in range(NT):
                        mm = nc.tensor.matmul(bank[:, 6 + h, t * P:(t + 1) * P], xt[h][:, t], aw[slot][:, t, h], start=True, stop=True)
                    mm.then_inc(s["au_mm"], 1)
                for h in range(2):
                    at(pe, p, "au", h + 1)
                    for t in range(NT):
                        mm = nc.tensor.matmul(bank[C * h:C * h + C, 0, t * P:(t + 1) * P], au[h][:, t, 0:C], bl[h][:, t, 1],
                                              start=True, stop=True)
                mm.then_inc(s["rp_mm"], 1)
                at(pe, p, "spread", 4)
                for h in range(2):
                    for t in range(NT):
                        mm = nc.tensor.matmul(bank[C * h:C * h + C, 1, t * P:(t + 1) * P], au[h][:, t, 0:C],
                                              bblk[:, t, h].rearrange("p a c -> p (a c)"), start=True, stop=True)
                mm.then_inc(s["f_mm"], 1)
                for h in range(2):
                    hc = slice(C * h, C * h + C)
                    at(pe, p, "ublk", h + 1)
                    for t in range(NT):
                        out = bank[hc, 2, t * P:(t + 1) * P]
                        nc.tensor.matmul(out, K_[:, t, hc], vblk[:, t, h].rearrange("p a c -> p (a c)"), start=True, stop=False)
                        mm = nc.tensor.matmul(out, B_[:, t, hc], ublk[:, t, h].rearrange("p a c -> p (a c)"), start=False, stop=True)
                mm.then_inc(s["z_mm"], 1)
                if not last:
                    at(pe, p + 1, "vtok", 1)
                    at(pe, p + 1, "bon", 1)

                def chain(c):
                    at(pe, p, "f", 1)
                    if c == 1:
                        at(pe, p, "z", 1)
                    else:
                        at(pe, p, "state", c - 1)
                    plain(pe)
                    for h in range(2):
                        hp = slice(C * h, C * h + C)
                        state = zq[hp, 0] if c == 1 else st[hp, c]
                        mm = nc.tensor.matmul(bank[hp, 4, c * C:(c + 1) * C], ft[hp, c], state, start=True, stop=True)
                    mm.then_inc(s["chain"], 1)

                def within(t):
                    for h in range(2):
                        hp = slice(C * h, C * h + C)
                        out = bank[hp, 5, t * P:(t + 1) * P]
                        nc.tensor.matmul(out, V_[:, t, hp], kl[h][:, t, 1], start=True, stop=False)
                        nc.tensor.matmul(out, au[h][:, t, C:P], bl[h][:, t, 1], start=False, stop=False)

                def before(t):
                    at(pe, p, "rp", 1)
                    if t:
                        at(pe, p, "state", 2 * t)
                    plain(pe)
                    for h in range(2):
                        hp = slice(C * h, C * h + C)
                        for c in (2 * t, 2 * t + 1):
                            if c:
                                state = zq[hp, 0] if c == 1 else st[hp, c]
                                mm = nc.tensor.matmul(bank[hp, 5, c * C:(c + 1) * C], state, rp[hp, c * C:(c + 1) * C],
                                                      start=False, stop=(c % 2 == 1))
                    return mm

                for c in range(1, NC_ - 1):
                    if c % 2 == 1:
                        within(c // 2)
                    chain(c)
                    if c % 2 == 1:
                        before(c // 2)
                        if not last:
                            prepare(p + 1, 1 - slot, 4 + c // 2)
                within(NT - 1)
                before(NT - 1).then_inc(s["y_mm"], 1)

            steps(pe, prepare, step, finish)

        @block.scalar
        def _(act):
            A = nc.scalar.activation

            def prepare(p, slot, part):
                c = cur[slot]
                if part == 0:
                    at(act, p, "cur", 1)
                    at(act, p, "loaded", 48)
                    A(sqk[:], k[:], ACT.Square, scale=c[:, KK:KK + 1]).then_inc(s["sqk"], 1)
                    at(act, p, "zp", 1)
                    A(tw[:], bank[:, 4], ACT.Tanh, scale=0.5, bias=c[:, W0H:W0H + 1]).then_inc(s["tw"], 1)
                    at(act, p, "ap", 1)
                    A(ta[:], bank[:, 5], ACT.Tanh, scale=0.5, bias=c[:, A0H:A0H + 1]).then_inc(s["ta"], 1)
                if part == 1:
                    at(act, p, "gp", 1)
                    A(gsb[slot][:], bank[:, 5], ACT.Copy).then_inc(s["gsb"], 1)
                    at(act, p, "clip", 1)
                    A(inv[:], sqk[:], ACT.Ln, scale=LN_SCALE).then_inc(s["lnk"], 1)
                    at(act, p, "lnk", 1)
                    A(inv[:], inv[:], ACT.Exp, scale=-0.5, bias=half_log[:, 0:1]).then_inc(s["inv"], 1)
                if part == 2:
                    at(act, p, "ce", 1)
                    A(eex[:], ce[:], ACT.Exp, scale=-KAPPA).then_inc(s["eex"], 1)
                    A(ep[:], cc[:], ACT.Exp, scale=-KAPPA).then_inc(s["ep"], 1)
                    A(em[:], cc[:], ACT.Exp, scale=KAPPA).then_inc(s["em"], 1)
                    at(act, p, "qsum", 1)
                    A(q[slot][:], qs[:], ACT.Exp, scale=-KAPPA).then_inc(s["q"], 1)
                    at(act, p, "vturn", 1)
                    A(vtok[slot][:].rearrange("p t c -> p (t c)"), bank[:, 4], ACT.Copy).then_inc(s["vtok"], 1)
                if part == 4:
                    at(act, p, "turn", 1)
                    A(aw[slot][:, :, :, 0:C], bank[:, 7].rearrange("p (t h c) -> p t h c", t=NT, h=2), ACT.Copy).then_inc(s["tok"], 1)
                if part == 5:
                    at(act, p, "turn", 2)
                    A(btok[slot][:].rearrange("p t c -> p (t c)"), bank[:, 6], ACT.Copy).then_inc(s["tok"], 1)
                if part == 6:
                    at(act, p, "turn", 3)
                    A(ktok[slot][:].rearrange("p t c -> p (t c)"), bank[:, 7], ACT.Copy).then_inc(s["tok"], 1)

            def finish(p, slot, part):
                if part == 0:
                    at(act, p, "y_mm", 1)
                    at(act, p, "pair", 1)
                    A(ysb[:], bank[:, 5], ACT.Copy).then_inc(s["ysb"], 1)
                    at(act, p, "dev", 1)
                    A(sqy[:], dev[:], ACT.Square).then_inc(s["sqy"], 1)
                if part == 1:
                    at(act, p, "var", 1)
                    A(rs[:], bank[:, 6], ACT.Ln, scale=1.0 / C, bias=core.eps[:, 1:2]).then_inc(s["lny"], 1)
                    at(act, p, "lny", 1)
                    A(rs[:], rs[:], ACT.Exp, scale=-0.5).then_inc(s["rs"], 1)
                if part == 2:
                    at(act, p, "yn", 3)
                    plain(act)
                    A(flat(yhi[:, one(p)]), yn[:], ACT.Copy).then_inc(s["yhi"], 1)

            def step(p, slot, first, last):
                if not first:
                    finish(p - 1, 1 - slot, 0)
                    finish(p - 1, 1 - slot, 1)
                at(act, p, "lakv", 1)
                A(aw[slot][:, :, :, C:P], bank[:, 5].rearrange("p (t h c) -> p t h c", t=NT, h=2), ACT.Copy).then_inc(s["aw"], 1)
                for part in range(PARTS):
                    if part == 1 and not first:
                        finish(p - 1, 1 - slot, 2)
                    if part == 4:
                        for h in range(2):
                            at(act, p, "au_mm", h + 1)
                            A(au[h][:].rearrange("p t c -> p (t c)"), bank[:, 6 + h], ACT.Copy).then_inc(s["au"], 1)
                    if not last:
                        prepare(p + 1, 1 - slot, part)

            steps(act, prepare, step, finish)

        @block.gpsimd
        def _(pool):
            G = nc.gpsimd
            pool.sem_inc(s["pair"], 1)
            eye = core.ident[:].rearrange("p (a c) -> p a c", a=1).to_broadcast([P, NT, P])

            def prepare(p, slot, part):
                c = cur[slot]
                if part == 0:
                    at(pool, p, "cur", 1)
                    at(pool, p, "loaded", 48)
                    plain(pool)
                    G.tensor_scalar(kk0[:], k[:], c[:, KK:KK + 1], None, ALU.mult).then_inc(s["pk"], 1)
                    at(pool, p, "ta", 1)
                    plain(pool)
                    G.tensor_scalar(kf[:], ta[:], c[:, HKA:HKA + 1], c[:, OKA:OKA + 1], ALU.mult, ALU.add).then_inc(s["pk"], 1)
                    G.tensor_scalar(a1[:], ta[:], 0.5, 0.5, ALU.mult, ALU.add).then_inc(s["pk"], 1)
                    at(pool, p, "pk", 2)
                    G.tensor_tensor(kp[:], k[:], kf[:], ALU.mult).then_inc(s["pk"], 1)
                if part == 1:
                    at(pool, p, "pk", 3)
                    at(pool, p, "inv", 1)
                    G.tensor_tensor(kk[:], kk0[:], inv[:], ALU.mult).then_inc(s["pk"], 1)
                    at(pool, p, "pk", 5)
                    G.tensor_tensor(beta[:], kk[:], a1[:], ALU.mult).then_inc(s["pk"], 1)
                if part == 3:
                    at(pool, p, "tilde", 4)
                    plain(pool)
                    for src, dst in ((bt, bz), (kt, kz)):
                        for h in range(2):
                            G.tensor_scalar(dst[h][:], src[:], core.head_ones[:, C * h:C * h + 1], None, ALU.mult).then_inc(s["pad"], 1)

            def finish(p, slot, part):
                if part == 2:
                    at(pool, p, "yhi", 1)
                    plain(pool)
                    G.tensor_tensor(flat(ylo[:, one(p)]), yn[:], flat(fp(yhi[:, one(p)])), ALU.subtract).then_inc(s["pair"], 1)

            def step(p, slot, first, last):
                for h in range(2):
                    m = first_level[:, 1:2].to_broadcast([P, NT, P])
                    at(pool, p, "bl", 2 * h + 2)
                    G.tensor_tensor(xt[h][:], bl[h][:, :, 0], m, ALU.mult).then_inc(s["x_init"], 1)
                    at(pool, p, "x_init", 3 * h + 1)
                    G.tensor_tensor(xt[h][:], xt[h][:], eye, ALU.add).then_inc(s["x_init"], 1)
                    at(pool, p, "nm", h + 1)
                    G.tensor_tensor(x[h][:], x[h][:], eye, ALU.add).then_inc(s["x_init"], 1)
                at(pool, p, "vtok", 1)
                at(pool, p, "tok", 2)
                plain(pool)
                for src, dst in ((vtok[slot], vblk), (btok[slot], bblk)):
                    for h in range(2):
                        G.tensor_tensor(dst[:, :, h], by_chunks(src[:, :, C * h:C * h + C]), chunks, ALU.mult).then_inc(s["spread"], 1)
                for part in range(PARTS):
                    if not last:
                        prepare(p + 1, 1 - slot, part)
                    if part == 0 and not first:
                        finish(p - 1, 1 - slot, 2)

            steps(pool, prepare, step, finish)
            pool.wait_ge(s["pair"], ND + 1)

        @block.vector
        def _(dve):
            V = nc.vector
            TT = V.tensor_tensor
            V.memset(wb[:], 0.0)
            V.memset(ab[:], 0.0)
            V.memset(gb[:, 1], 0.0).then_inc(s["zeroed"], 1)
            V.memset(half_log[:], 0.5 * float(np.log(LN_SCALE)))
            V.memset(resets[:], 1.0).then_inc(s["pv"], 1)
            dve.wait_ge(s["pv"], 1)
            V.memset(resets[:].rearrange("p (c t) -> p c t", t=C)[:, :, 0:1], 0.0)
            for c, name, a in ((W0H, "rw_w0", 0.5), (A0H, "rw_a0", 0.5), (KK, "rw_k_k", 1.0), (HKA, "rw_k_a", 0.5),
                               (RK, "rw_r_k", 1.0), (GNW, "rw_gn_w", 1.0), (GNB, "rw_gn_b", 1.0)):
                V.tensor_scalar(pv[:, :, c], core.vec(name), a, None, ALU.mult)
            V.tensor_scalar(pv[:, :, OKA], core.vec("rw_k_a"), -0.5, 1.0, ALU.mult, ALU.add).then_inc(s["pv"], 1)
            dve.wait_ge(s["pv"], 2)
            by_chunk = lambda view: view.rearrange("p (c t) -> p c t", t=C)
            spread = lambda view: view.rearrange("p (c a) -> p c a", a=1).to_broadcast([P, NC_, C])
            two_masks = masks[:].rearrange("p a c -> p (a c)").rearrange("p (o n) -> p o n", o=1).to_broadcast([P, 2, 2 * P])

            def prepare(p, slot, part):
                c = cur[slot]
                if part == 0:
                    plain(dve)
                    V.tensor_copy(c[:], pv[:, one(p)].rearrange("p a c -> p (a c)")).then_inc(s["cur"], 1)
                if part == 1:
                    at(dve, p, "tw", 1)
                    V.tensor_scalar(sg[:], tw[:], 0.5, 0.5, ALU.mult, ALU.add).then_inc(s["sg"], 1)
                    at(dve, p, "ssk", 1)
                    V.tensor_scalar(sqk[:], bank[:, 4], 1e-24, None, ALU.max).then_inc(s["clip"], 1)
                    at(dve, p, "sg", 1)
                    V.tensor_tensor_scan(cum[:], resets[:], sg[:], 0.0, ALU.mult, ALU.add).then_inc(s["cum"], 1)
                    at(dve, p, "cum", 1)
                    V.tensor_scalar(ctr[:], by_chunk(cum[:])[:, :, C - 1], 0.5, None, ALU.mult).then_inc(s["ctr"], 1)
                if part == 2:
                    at(dve, p, "ctr", 1)
                    TT(by_chunk(cc[:]), by_chunk(cum[:]), spread(ctr[:]), ALU.subtract).then_inc(s["cc"], 1)
                    at(dve, p, "cc", 1)
                    TT(ce[:], cc[:], sg[:], ALU.subtract).then_inc(s["ce"], 1)
                    V.memset(qs[:, NC_ - 1:NC_], 0.0)
                    TT(qs[:, 0:NC_ - 1], ctr[:, 0:NC_ - 1], ctr[:, 1:NC_], ALU.add).then_inc(s["qsum"], 1)
                    at(dve, p, "loaded", 48)
                    at(dve, p, "pk", 4)
                    V.scalar_tensor_tensor(out=rk[:], in0=r[:], scalar=c[:, RK:RK + 1], in1=kp[:], op0=ALU.mult,
                                           op1=ALU.mult).then_inc(s["rk"], 1)
                if part == 3:
                    at(dve, p, "ep", 1)
                    at(dve, p, "eex", 1)
                    at(dve, p, "pk", 6)
                    V.scalar_tensor_tensor(out=ar[slot][:, :, 0], in0=tiles(kk[:]), scalar=-1.0, in1=tiles(eex[:]), op0=ALU.mult,
                                           op1=ALU.mult).then_inc(s["tilde"], 1)
                    TT(ar[slot][:, :, 1], tiles(r[:]), tiles(ep[:]), ALU.mult).then_inc(s["tilde"], 1)
                    at(dve, p, "em", 1)
                    TT(kt[:], kp[:], em[:], ALU.mult).then_inc(s["tilde"], 1)
                    TT(bt[:], beta[:], em[:], ALU.mult).then_inc(s["tilde"], 1)
                if part == 4:
                    at(dve, p, "bsum", 1)
                    TT(bon[slot][:], bank[:, 5], v[:], ALU.mult).then_inc(s["bon"], 1)

            def finish(p, slot, part):
                c = cur[slot]
                if part == 0:
                    at(dve, p, "mean", 1)
                    V.scalar_tensor_tensor(out=dev[:], in0=bank[:, 6], scalar=-1.0 / C, in1=ysb[:], op0=ALU.mult,
                                           op1=ALU.add).then_inc(s["dev"], 1)
                if part == 2:
                    at(dve, p, "rs", 1)
                    V.scalar_tensor_tensor(out=yn[:], in0=dev[:], scalar=c[:, GNW:GNW + 1], in1=rs[:], op0=ALU.mult,
                                           op1=ALU.mult).then_inc(s["yn"], 1)
                    at(dve, p, "yn", 1)
                    V.scalar_tensor_tensor(out=yn[:], in0=yn[:], scalar=c[:, GNB:GNB + 1], in1=bon[slot][:], op0=ALU.add,
                                           op1=ALU.add).then_inc(s["yn"], 1)
                    at(dve, p, "yn", 2)
                    TT(yn[:], yn[:], gsb[slot][:], ALU.mult).then_inc(s["yn"], 1)

            def step(p, slot, first, last):
                if first:
                    dve.wait_ge(s["consts"], 64)
                for h in range(2):
                    for n, dst, name in ((0, bl[h], "bl"), (1, kl[h], "kl")):
                        at(dve, p, "score", 3 * h + n + 1)
                        for half in range(2):
                            TT(dst[:, 2 * half:2 * half + 2].rearrange("p t a c -> p t (a c)"),
                               bank[:, 2 * n + half].rearrange("p (t n) -> p t n", t=2), two_masks, ALU.mult).then_inc(s[name], 1)
                        if h == 0 and n == 0 and not first:
                            finish(p - 1, 1 - slot, 0)
                    at(dve, p, "score", 3 * h + 3)
                    TT(x[h][:], tiles(bank[:, 4 if h == 0 else 7]), first_level[:, 0:1].to_broadcast([P, NT, P]), ALU.mult).then_inc(s["nm"], 1)
                for level in range(len(LEVELS)):
                    over = level == len(LEVELS) - 1
                    for h in range(2):
                        at(dve, p, "g_mm", 2 * level + h + 1)
                        TT(g[h][:], tiles(bank[:, 6 + h]), merge[:, level:level + 1].to_broadcast([P, NT, P]), ALU.mult).then_inc(s["g"], 1)
                    if level == 0 and not first:
                        finish(p - 1, 1 - slot, 2)
                    if not last:
                        prepare(p + 1, 1 - slot, level)
                    for h in range(2):
                        at(dve, p, "x_mm", 2 * level + h + 1)
                        if not over:
                            TT(x[h][:], tiles(bank[:, 2 * h]), x[h][:], ALU.add).then_inc(s["xv"], 1)
                        TT(xt[h][:], tiles(bank[:, 2 * h + 1]), xt[h][:], ALU.add).then_inc(s["x"], 1)
                for h in range(2):
                    at(dve, p, "au", h + 1)
                    TT(ublk[:, :, h], by_chunks(au[h][:, :, C:P]), chunks, ALU.mult).then_inc(s["ublk"], 1)
                at(dve, p, "rp_mm", 1)
                TT(tiles(rp[:]), tiles(bank[:, 0]), ar[slot][:, :, 1], ALU.add).then_inc(s["rp"], 1)
                at(dve, p, "f_mm", 1)
                TT(ft[:], by_chunk(bank[:, 1]), i64[:].rearrange("p (o c) -> p o c", o=1).to_broadcast([P, NC_, C]),
                   ALU.add).then_inc(s["f"], 1)
                at(dve, p, "z_mm", 1)
                at(dve, p, "q", 1)
                TT(zq[:], by_chunk(bank[:, 2]), spread(q[slot][:]), ALU.mult).then_inc(s["z"], 1)
                at(dve, p, "z", 1)
                for c in range(1, NC_ - 1):
                    at(dve, p, "chain", c)
                    V.scalar_tensor_tensor(out=st[:, c + 1], in0=bank[:, 4, c * C:(c + 1) * C], scalar=q[slot][:, c:c + 1],
                                           in1=zq[:, c], op0=ALU.mult, op1=ALU.add).then_inc(s["state"], 1)

            steps(dve, prepare, step, finish)
    close_stage(core, s)


ADD_SEMS = ["raw0", "raw1", "raw2", "raw3", "w_free", "w_hi", "w_ready", "x_done", "sq", "sq_sum"]


def project_add(core, tag, yhi, ylo, weights, ahead):
    nc = core.nc
    w = weights.rearrange("(k p) e -> p k e", p=P)
    with ExitStack() as ctx:
        s, sb, ps = open_stage(core, ctx, tag, ADD_SEMS)
        open_ring(core, sb)
        p_out = ps("p_out", [P, 2, T])
        block = ctx.enter_context(nc.Block())

        @block.sync
        def _(sp):
            for u in range(SLOTS, ND):
                load_unit(sp, s, core, u % 4, u, w[:, :, u * P:(u + 1) * P])
            sp.wait_ge(s["w_ready"], done(ND - 1))
            load_ahead(sp, core, ahead)

        @block.vector
        def _(dve):
            dve.sem_inc(s["w_ready"], SLOTS)
            dve.sem_inc(s["x_done"], 2)
            for u in range(4):
                split_unit(dve, s, core, u, 0, u, ND)
            for u in range(ND):
                dve.wait_ge(s["w_free"], done(u))
                nc.vector.tensor_tensor(core.x[:, u], core.x[:, u], p_out[:, u % 2], ALU.add).then_inc(s["x_done"], 1)
                if u < ND - 4:
                    split_unit(dve, s, core, u % 4, u // 4 + 1, u + 4, ND)

        @block.tensor
        def _(pe):
            pe.sem_inc(s["w_free"], SLOTS)
            with pe.Fori(0, ND // 4) as i:
                for j in range(4):
                    pe.wait_ge(s["w_ready"], done(4 * i + j))
                    pe.wait_ge(s["x_done"], 4 * i + (j + 1))
                    for k in range(ND):
                        mm = three_passes(core, p_out[:, j % 2], j, k, yhi[:, k], ylo[:, k], k == 0, k == ND - 1)
                    mm.then_inc(s["w_free"], 1)

        @block.scalar
        def _(act):
            square_tiles(core, act, s, ("x_done", 3))

        @block.gpsimd
        def _(pool):
            sum_squares(core, pool, s)
    close_stage(core, s)


G = 4
KIND = G * C
N_CMP = (T - 32) // 16 + 1
CMP_LEN, CMP_STRIDE, CMP_HIDDEN = 32, 16, 256
NL = CMP_LEN // 2
NH = CMP_HIDDEN // P

HEADS_SEMS = ["raw0", "raw1", "raw2", "raw3", "w_free", "w_hi", "w_ready", "xt", "sqx", "ss", "ln", "rs", "n", "swapped",
              "t1", "t2", "rot", "turned", "copied", "stored", "early", "consts", "gains", "scaled"] + NORM_SEMS


class HeadProjection:

    def __init__(self, core, s, sb, ps, x_gain, weights, units, gains, scale):
        nc = core.nc
        self.core, self.s, self.w, self.units, self.gains, self.scale = core, s, weights.rearrange("(k p) e -> p k e", p=P), units, gains, scale
        open_ring(core, sb)
        self.norm = Norm(core, s, sb, ps("p_ms", [P, T]), x_gain)
        self.rotated = [u for u, unit in enumerate(units) if unit[0] == "rotate"]
        self.turned = [u for u, unit in enumerate(units) if unit[0] == "turn"]
        keep = 2 if all(len(units[u][3]) == 1 for u in self.rotated) else len(self.rotated)
        self.cos, self.sin, self.swap = sb("cos", [P, T]), sb("sin", [P, T]), sb("swap", [P, P])
        self.gain = sb("gain", [P, len(gains)])
        self.xt = sb("xt", [P, 4, T])
        self.sqx, self.rs, self.t1, self.t2 = (sb(n, [P, 2, T]) for n in ("sqx", "rs", "t1", "t2"))
        self.keep, self.n = keep, sb("n", [P, keep, T])
        self.rot = sb("rot", [P, len(self.rotated), T])
        self.tok = sb("tok", [P, max(1, len(self.turned)), T])
        self.p_out = ps("p_out", [P, 4, T])
        self.p_ss, self.p_swap = ps("p_ss", [P, T]), ps("p_swap", [P, T])

    def index(self, u):
        return (self.rotated if self.units[u][0] == "rotate" else self.turned).index(u)

    def is_kind(self, u, kind):
        return 0 <= u < len(self.units) and self.units[u][0] == kind

    def stores(self):
        return sum(len(unit[3]) for unit in self.units if unit[0] != "plain")

    def sync(self, sp):
        core, s = self.core, self.s
        for c, g in enumerate(self.gains):
            for h in range(2):
                sp.dma_start(self.gain[C * h:C * h + C, c:c + 1], g.rearrange("(d a) -> d a", a=1)).then_inc(s["gains"], 16)
        at = 0
        for u, (kind, m, _, _) in enumerate(self.units):
            if u >= SLOTS:
                load_unit(sp, s, core, u % 4, u, self.w[:, :, at:at + m])
            at += m
            if u == 3:
                for dst, name in ((self.cos[:], "c_cos"), (self.sin[:], "c_sin"), (self.swap[:], "c_swap")):
                    sp.dma_start(dst, core.consts[name]).then_inc(s["consts"], 16)

    def vector(self, dve):
        core, s, V = self.core, self.s, self.core.nc.vector
        U = len(self.units)
        dve.sem_inc(s["w_ready"], SLOTS)
        split = lambda u: split_unit(dve, s, core, u % 4, u // 4, u, ND, self.units[u][1])
        split(0)
        self.norm.vector_low(dve, range(ND))
        for u in range(1, 4):
            split(u)
        dve.wait_ge(s["gains"], 32 * len(self.gains))
        V.tensor_scalar(self.gain[:], self.gain[:], self.scale, None, ALU.mult).then_inc(s["scaled"], 1)
        self.norm.vector_rstd(dve)
        dve.wait_ge(s["scaled"], 1)
        for u in range(U + 3):
            if self.is_kind(u - 3, "rotate"):
                r = self.index(u - 3)
                dve.wait_ge(s["swapped"], r + 1)
                V.tensor_tensor(self.t2[:, r % 2], self.p_swap[:], self.sin[:], ALU.mult).then_inc(s["t2"], 1)
                dve.wait_ge(s["t2"], r + 1)
                dve.wait_ge(s["t1"], r + 1)
                V.tensor_tensor(self.rot[:, r], self.t1[:, r % 2], self.t2[:, r % 2], ALU.add).then_inc(s["rot"], 1)
            if u < U:
                m = self.units[u][1]
                dve.wait_ge(s["w_free"], done(u))
                if self.is_kind(u - 4, "plain"):
                    assert all(unit[0] == "plain" for unit in self.units[:4])
                    dve.wait_ge(s["early"], 64)
                V.tensor_tensor(self.xt[0:m, u % 4], self.p_out[0:m, u % 4], self.norm.rstd[0:m], ALU.mult).then_inc(s["xt"], 1)
            if u + 4 < U:
                split(u + 4)
            if self.is_kind(u - 1, "rotate"):
                r = self.index(u - 1)
                dve.wait_ge(s["rs"], r + 1)
                if r >= 2:
                    dve.wait_ge(s["t1"], r - 1)
                V.scalar_tensor_tensor(out=self.n[:, r % self.keep], in0=self.xt[:, (u - 1) % 4], scalar=self.gain[:, self.units[u - 1][2]:self.units[u - 1][2] + 1],
                                       in1=self.rs[:, r % 2], op0=ALU.mult, op1=ALU.mult).then_inc(s["n"], 1)

    def tensor(self, pe):
        core, s, T_ = self.core, self.s, self.core.nc.tensor
        U = len(self.units)
        pe.sem_inc(s["w_free"], SLOTS)
        self.norm.tensor(pe)
        for u in range(U + 2):
            if u < U:
                pe.wait_ge(s["w_ready"], done(u))
                if u >= 4:
                    pe.wait_ge(s["xt"], u - 3)
                for k in range(ND):
                    if u == 0:
                        pe.wait_ge(s["h_lo"], k + 1)
                    mm = three_passes(core, self.p_out[:, u % 4], u % 4, k, self.norm.hi[:, k], self.norm.lo[:, k], k == 0, k == ND - 1)
                mm.then_inc(s["w_free"], 1)
            if u == 1:
                pe.wait_ge(s["consts"], 48)
            if self.is_kind(u - 1, "rotate"):
                r = self.index(u - 1)
                pe.wait_ge(s["sqx"], r + 1)
                if r:
                    pe.wait_ge(s["ln"], r)
                T_.matmul(self.p_ss[:], core.head_ones[:], self.sqx[:, r % 2], start=True, stop=True).then_inc(s["ss"], 1)
            if self.is_kind(u - 2, "rotate"):
                r = self.index(u - 2)
                pe.wait_ge(s["n"], r + 1)
                before = sum(v < u - 2 for v in self.turned)
                if before:
                    pe.wait_ge(s["copied"], before)
                if r:
                    pe.wait_ge(s["t2"], r)
                T_.matmul(self.p_swap[:], self.swap[:], self.n[:, r % self.keep], start=True, stop=True).then_inc(s["swapped"], 1)
            if self.is_kind(u - 2, "turn"):
                r = self.index(u - 2)
                pe.wait_ge(s["xt"], u - 1)
                if r:
                    pe.wait_ge(s["copied"], r)
                before = sum(v < u - 2 for v in self.rotated)
                if before:
                    pe.wait_ge(s["t2"], before)
                for t in range(NT):
                    mm = T_.transpose(self.p_swap[:, t * P:(t + 1) * P], self.xt[:, (u - 2) % 4, t * P:(t + 1) * P], core.ident[:])
                mm.then_inc(s["turned"], 1)

    def scalar(self, act):
        core, s, A = self.core, self.s, self.core.nc.scalar.activation
        U = len(self.units)
        self.norm.scalar(act)
        for u in range(U + 4):
            if u < U:
                kind, m, _, to = self.units[u]
                act.wait_ge(s["xt"], u + 1)
                if kind == "plain":
                    act.dma_start(to[0], self.xt[0:m, u % 4]).then_inc(s["early"], 16)
                if kind == "rotate":
                    r = self.index(u)
                    if r >= 2:
                        act.wait_ge(s["ss"], r - 1)
                    A(self.sqx[:, r % 2], self.xt[:, u % 4], ACT.Square).then_inc(s["sqx"], 1)
            if self.is_kind(u - 1, "rotate"):
                r = self.index(u - 1)
                act.wait_ge(s["ss"], r + 1)
                if r >= 2:
                    act.wait_ge(s["n"], r - 1)
                A(self.rs[:, r % 2], self.p_ss[:], ACT.Ln, scale=1.0 / C, bias=core.eps[:, 0:1]).then_inc(s["ln"], 1)
                act.wait_ge(s["ln"], r + 1)
                A(self.rs[:, r % 2], self.rs[:, r % 2], ACT.Exp, scale=-0.5).then_inc(s["rs"], 1)
            if self.is_kind(u - 2, "turn"):
                r = self.index(u - 2)
                act.wait_ge(s["turned"], r + 1)
                A(self.tok[:, r], self.p_swap[:], ACT.Copy).then_inc(s["copied"], 1)
                act.wait_ge(s["copied"], r + 1)
                act.dma_start(self.units[u - 2][3][0], self.tok[:, r]).then_inc(s["stored"], 16)
            if self.is_kind(u - 3, "rotate"):
                r = self.index(u - 3)
                to = self.units[u - 3][3]
                act.wait_ge(s["rot"], r + 1)
                act.dma_start(to[0], self.rot[:, r]).then_inc(s["stored"], 16)
                if len(to) > 1:
                    act.dma_start(to[1], self.n[:, r]).then_inc(s["stored"], 16)

    def finish(self, act):
        act.wait_ge(self.s["early"], 16 * sum(unit[0] == "plain" for unit in self.units))
        act.wait_ge(self.s["stored"], 16 * self.stores())

    def gpsimd(self, pool):
        s = self.s
        pool.wait_ge(s["consts"], 48)
        for r in range(len(self.rotated)):
            pool.wait_ge(s["n"], r + 1)
            if r >= 2:
                pool.wait_ge(s["rot"], r - 1)
            self.core.nc.gpsimd.tensor_tensor(self.t1[:, r % 2], self.n[:, r % self.keep], self.cos[:], ALU.mult).then_inc(s["t1"], 1)


def queries(core, tag, gain, weights, q_gain, q_rot, q_plain, gate_logits, ahead):
    nc = core.nc
    units = [("rotate", P, 0, (q_rot[d * P:(d + 1) * P], q_plain[d * P:(d + 1) * P])) for d in range(ND)]
    units.append(("plain", weights.shape[1] - D, 0, (gate_logits,)))
    with ExitStack() as ctx:
        s, sb, ps = open_stage(core, ctx, tag, HEADS_SEMS)
        heads = HeadProjection(core, s, sb, ps, gain, weights, units, [q_gain], C ** -0.5)
        block = ctx.enter_context(nc.Block())

        @block.sync
        def _(sp):
            heads.sync(sp)
            sp.wait_ge(s["w_ready"], done(len(units) - 1))
            load_ahead(sp, core, ahead)

        @block.vector
        def _(dve):
            heads.vector(dve)

        @block.tensor
        def _(pe):
            heads.tensor(pe)

        @block.scalar
        def _(act):
            heads.scalar(act)
            heads.finish(act)

        @block.gpsimd
        def _(pool):
            heads.gpsimd(pool)
    close_stage(core, s)


def shared_kv(core, kv, k_rot, v_tok, k_cmp, v_cmp, ahead):
    nc, ins = core.nc, core.ins
    kinds = []
    for u in range(6 * KIND // P):
        what, half = u * P // KIND, u % (KIND // P)
        if what < 2:
            kinds.append(("plain", P, 0, (kv[u * P:(u + 1) * P],)))
        elif what % 2 == 0:
            row = (what // 2 - 1) * KIND + half * P
            kinds.append(("rotate", P, what // 2 - 1, (k_rot[row:row + P],)))
        else:
            kinds.append(("turn", P, 0, (v_tok[(what // 2 - 1) * (KIND // P) + half],)))
    with ExitStack() as ctx:
        s, sb, ps = open_stage(core, ctx, "kv", HEADS_SEMS + [
            "tok", "pos", "w1", "w2", "blk", "h1", "gelu", "c2", "sqc", "c_ss", "c_ln", "c_rs", "pos_turned", "pos_copied",
            "kc", "vc", "cout", "c_gain"])
        heads = HeadProjection(core, s, sb, ps, core.vec("kv_norm"), ins["kv_w"], kinds,
                               [ins["kv_k_norm"][1], ins["kv_k_norm"][2]], 1.0)
        NB = G * N_CMP
        tok = [fp(t[:])[:, 0:G] for t in (heads.norm.hi, heads.norm.lo)]
        pos_rows, pos = sb("pos_rows", [NL, 2, P]), sb("pos", [P, 2, NL])
        w1 = sb("w1", [P, 2, NL, CMP_HIDDEN])
        w2 = sb("w2", [P, 2, NH, C])
        c_gain = sb("c_gain", [C, 1])
        blk = sb("blk", [P, 4, NB])
        hid = sb("hid", [P, 2, NH, NB])
        kc, sqc, rsc, vc = sb("kc", [C, NB]), sb("sqc", [C, NB]), sb("rsc", [C, NB]), sb("vc", [NB, C])
        p_h, p_o, p_ss = heads.p_out, heads.p_ss, heads.p_swap
        steps = [(which, lp) for which in range(2) for lp in range(NL)]
        block = ctx.enter_context(nc.Block())

        @block.sync
        def _(sp):
            heads.sync(sp)
            for which in range(2):
                p_src = ins["cmp_pos_k" if which == 0 else "cmp_pos_v"].rearrange("(l a) d -> l (a d)", a=2)
                sp.dma_start(pos_rows[:, which], p_src).then_inc(s["pos"], 16)
                w = ins["cmp_k_w1" if which == 0 else "cmp_v_w1"].rearrange("(l p) h -> p l h", p=P)
                sp.dma_start(w1[:, which], w).then_inc(s["w1"], 16)
                sp.dma_start(w2[:, which], ins["cmp_k_w2" if which == 0 else "cmp_v_w2"].rearrange("(l p) h -> p l h", p=P)).then_inc(s["w2"], 16)
            sp.dma_start(c_gain[:], ins["kv_k_norm"][0].rearrange("(d a) -> d a", a=1)).then_inc(s["c_gain"], 16)
            sp.wait_ge(s["early"], 16 * 2 * (KIND // P))
            sp.wait_ge(s["w_free"], done(len(kinds) - 1))
            for which in range(2):
                src = kv[which * KIND:(which + 1) * KIND].rearrange("(g d) t -> d g t", d=C)
                sp.dma_start(tok[which][0:C], src).then_inc(s["tok"], 16)
                sp.dma_start(tok[which][C:P, :, 0:T - 1], src[:, :, 1:T]).then_inc(s["tok"], 16)
            load_ahead(sp, core, ahead)
            sp.wait_ge(s["vc"], 1)
            sp.dma_start(v_cmp, vc[:]).then_inc(s["cout"], 16)
            sp.wait_ge(s["kc"], 1)
            sp.dma_start(k_cmp, kc[:]).then_inc(s["cout"], 16)
            sp.wait_ge(s["cout"], 32)

        @block.scalar
        def _(act):
            heads.scalar(act)
            for which in range(2):
                act.wait_ge(s["h1"], NL * which + NL)
                for t in range(NH):
                    nc.scalar.activation(hid[:, which, t], p_h[:, 2 * which + t, 0:NB], ACT.Gelu_apprx_tanh).then_inc(s["gelu"], 1)
            act.wait_ge(s["c2"], 1)
            nc.scalar.activation(sqc[:], p_o[0:C, 0:NB], ACT.Square).then_inc(s["sqc"], 1)
            act.wait_ge(s["c2"], 2)
            nc.scalar.activation(vc[:], p_h[0:NB, 2, 0:C], ACT.Copy).then_inc(s["vc"], 1)
            act.wait_ge(s["c_ss"], 1)
            nc.scalar.activation(rsc[:], p_ss[0:C, 0:NB], ACT.Ln, scale=1.0 / C, bias=core.eps[0:C, 0:1]).then_inc(s["c_ln"], 1)
            act.wait_ge(s["c_ln"], 1)
            nc.scalar.activation(rsc[:], rsc[:], ACT.Exp, scale=-0.5).then_inc(s["c_rs"], 1)
            heads.finish(act)

        @block.tensor
        def _(pe):
            heads.tensor(pe)
            pe.wait_ge(s["pos"], 32)
            pe.wait_ge(s["ln"], len(heads.rotated))
            for which in range(2):
                mm = nc.tensor.transpose(p_o[:, which * NL:(which + 1) * NL], pos_rows[:, which], core.ident[0:NL, 0:NL])
            mm.then_inc(s["pos_turned"], 1)
            pe.wait_ge(s["xt"], len(kinds))
            pe.wait_ge(s["w1"], 32)
            for n, (which, lp) in enumerate(steps):
                pe.wait_ge(s["blk"], n + 1)
                for t in range(NH):
                    mm = nc.tensor.matmul(p_h[:, 2 * which + t, 0:NB], w1[:, which, lp, t * P:(t + 1) * P],
                                          blk[:, n % 4], start=(lp == 0), stop=(lp == NL - 1))
                mm.then_inc(s["h1"], 1)
            pe.wait_ge(s["w2"], 32)
            pe.wait_ge(s["gelu"], 2)
            for t in range(NH):
                mm = nc.tensor.matmul(p_o[0:C, 0:NB], w2[:, 0, t], hid[:, 0, t], start=(t == 0), stop=(t == NH - 1))
            mm.then_inc(s["c2"], 1)
            pe.wait_ge(s["gelu"], 4)
            for t in range(NH):
                mm = nc.tensor.matmul(p_h[0:NB, 2, 0:C], hid[:, 1, t], w2[:, 1, t], start=(t == 0), stop=(t == NH - 1))
            mm.then_inc(s["c2"], 1)
            pe.wait_ge(s["sqc"], 1)
            pe.wait_ge(s["copied"], len(heads.turned))
            nc.tensor.matmul(p_ss[0:C, 0:NB], core.ones[0:C, 0:C], sqc[:], start=True, stop=True).then_inc(s["c_ss"], 1)

        @block.vector
        def _(dve):
            heads.vector(dve)
            dve.wait_ge(s["pos_turned"], 1)
            nc.vector.tensor_copy(pos[:], p_o[:, 0:2 * NL].rearrange("p (a l) -> p a l", a=2)).then_inc(s["pos_copied"], 1)
            dve.wait_ge(s["pos_copied"], 1)
            dve.wait_ge(s["tok"], 64)
            for n, (which, lp) in enumerate(steps):
                if n >= 4:
                    dve.wait_ge(s["h1"], n - 3)
                src = tok[which][:, :, 2 * lp:2 * lp + CMP_STRIDE * (N_CMP - 1) + 1:CMP_STRIDE]
                nc.vector.tensor_scalar(blk[:, n % 4].rearrange("p (g n) -> p g n", g=G), src,
                                        pos[:, which, lp:lp + 1], None, ALU.add).then_inc(s["blk"], 1)
            dve.wait_ge(s["c_gain"], 16)
            dve.wait_ge(s["c_rs"], 1)
            nc.vector.scalar_tensor_tensor(out=kc[:], in0=p_o[0:C, 0:NB], scalar=c_gain[:, 0:1], in1=rsc[:],
                                           op0=ALU.mult, op1=ALU.mult).then_inc(s["kc"], 1)

        @block.gpsimd
        def _(pool):
            heads.gpsimd(pool)
    close_stage(core, s)




def attention_steps():
    steps, turn = [], None
    for group in range(2):
        for pair in range(2):
            for head in range(2):
                steps.append(("cmp", group, pair, head, 0))
                steps.append(("main", group, pair, head, 0))
                if turn and head == 0:
                    steps.append(turn)
                steps += [("main", group, pair, head, t) for t in range(1, NT)]
            turn = ("turn", group, pair, 0, 0)
    return steps + [turn]


STEPS = attention_steps()
ATTENTION_EVENTS = {
    "nmax_sel": ("main",), "probs_sel": ("main",),
    "scores": ("cmp", "main"), "masked": ("cmp",), "nmax": ("cmp", "main"), "probs": ("cmp", "main"),
    "turned": ("cmp", "main", "turn"), "copied_v": ("main", "turn"), "copied_a": ("cmp", "main", "turn"),
    "o_mm": ("cmp", "main"), "recip": ("cmp", "main"), "coef": ("cmp", "main"), "o_sel": ("main",), "o": ("cmp", "main"),
}
N_LOADS = 4
N_SMALL_LOADS = 3


def attention(core, tag, q_plain, q_rot, gate_logits, k_rot, v_tok, k_cmp, v_cmp, yhi, ylo):
    nc = core.nc
    U = len(STEPS)
    assert U % 4 == 0
    per_body = {e: sum(st[0] in kinds for st in STEPS) for e, kinds in ATTENTION_EVENTS.items()}

    with ExitStack() as ctx:
        s, sb, ps = open_stage(core, ctx, tag, list(ATTENTION_EVENTS) + ["in0", "in1", "cmp_in0", "cmp_in1", "v_in0", "v_in1", "gl", "consts", "sig", "gt", "gates", "ready",
                                               "split", "rounded"])

        def at(eng, i, name, u):
            kinds = ATTENTION_EVENTS[name]
            whole, u = divmod(u, U)
            count = sum(st[0] in kinds for st in STEPS[:u + 1]) + whole * per_body[name]
            eng.wait_ge(s[name], i * per_body[name] + (per_body[name] + count))

        def credit(eng, *names):
            for name in names:
                eng.sem_inc(s[name], per_body[name])

        kk = [sb(f"kk{g}", [P, 2, T]) for g in range(2)]
        kc = [sb(f"kc{g}", [P, N_CMP]) for g in range(2)]
        vv = [sb(f"vv{g}", [P, 2, NT, C]) for g in range(2)]
        vc = [sb(f"vc{g}", [N_CMP, C]) for g in range(2)]
        qp = [sb(f"qp{g}", [P, 2, T]) for g in range(2)]
        qr = [sb(f"qr{g}", [P, 4, T]) for g in range(2)]
        q2 = [sb(f"q2{g}", [P, 4, T], F32R) for g in range(2)]
        khi = [sb(f"khi{g}", [P, 2, T], F32R) for g in range(2)]
        klo = [sb(f"klo{g}", [P, 2, T], F32R) for g in range(2)]
        glog = sb("glog", [48, T])
        gates = sb("gates", [P, NT, 48])
        causal = sb("causal", [P, P])
        cmp_neg = sb("cmp_neg", [P, NT, N_CMP])
        has_block = sb("has_block", [P, 1])
        ident16, causal16 = sb("ident16", [P, P], mybir.dt.bfloat16), sb("causal16", [P, P], mybir.dt.bfloat16)
        masked = sb("masked", [P, 2, NT, N_CMP])
        nmax, sums = sb("nmax", [P, 2, NT]), sb("sums", [P, 4, NT])
        probs = sb("probs", [P, 2, 2, T])
        pt = sb("pt", [P, 2, 2, T])
        rcp, coef = sb("rcp", [P, 4, NT]), sb("coef", [P, 4, NT])
        osb = sb("osb", [P, 2, NT, P])
        bank = ps("bank", [P, 8, T])
        block = ctx.enter_context(nc.Block())

        @block.sync
        def _(sp):
            sp.dma_start(glog[:], gate_logits).then_inc(s["gl"], 16)
            for dst, name in ((causal, "c_causal"), (cmp_neg, "c_cmp_neg"), (has_block, "c_has_block")):
                sp.dma_start(dst[:], core.consts[name]).then_inc(s["consts"], 16)
            with sp.Fori(0, 2) as i:
                for g in range(2):
                    last = max(u for u, st in enumerate(STEPS) if st[0] != "turn" and st[1] == g)
                    at(sp, i, "o_mm", last - U)
                    keys = k_rot.rearrange("(b e x d) t -> x e d b t", b=2, x=2, d=C)[g][one(i)].rearrange("o d b t -> (o d) b t")
                    keys_c = k_cmp.rearrange("d (e x n) -> x e d n", x=2, n=N_CMP)[g][one(i)].rearrange("o d n -> (o d) n")
                    for h in range(2):
                        sp.dma_start(kc[g][C * h:C * h + C], keys_c).then_inc(s[f"cmp_in{g}"], 16)
                    src = q_plain.rearrange("(e x j p) t -> x e p j t", x=2, j=2, p=P)[g][one(i)].rearrange("o p j t -> (o p) j t")
                    sp.dma_start(qp[g][:], src).then_inc(s[f"cmp_in{g}"], 16)
                    for h in range(2):
                        sp.dma_start(kk[g][C * h:C * h + C], keys).then_inc(s[f"in{g}"], 16)
                    for h in range(2):
                        src = q_rot.rearrange("(e x j d) t -> x e d j t", x=2, j=4, d=C)[g][one(i)].rearrange("o d j t -> (o d) j t")
                        sp.dma_start(qr[g][C * h:C * h + C], src).then_inc(s[f"in{g}"], 16)
                    src = v_cmp.rearrange("(e x n) d -> x e n d", x=2, n=N_CMP)[g][one(i)].rearrange("o n d -> (o n) d")
                    sp.dma_start(vc[g][:], src).then_inc(s[f"v_in{g}"], 16)
                    for b in range(2):
                        src = v_tok.rearrange("(b e) p (t x d) -> b x e p t d", b=2, x=2, d=C)[b][g][one(i)].rearrange("o p t d -> (o p) t d")
                        sp.dma_start(vv[g][:, b], src).then_inc(s[f"v_in{g}"], 16)

        @block.tensor
        def _(pe):
            credit(pe, "scores", "turned", "o_mm")
            pe.wait_ge(s["sig"], 1)
            for t in range(NT):
                mm = nc.tensor.transpose(bank[:, 6, t * 48:(t + 1) * 48], glog[:, t * P:(t + 1) * P], core.ident[0:48, 0:48])
            mm.then_inc(s["gt"], 1)
            pe.wait_ge(s["gates"], 2)

            def scores(i, u):
                kind, g, pair, head, t = STEPS[u]
                if kind == "turn":
                    return
                hp, slot = slice(C * head, C * head + C), u % 2
                if u == 0 or STEPS[u - 1][1] != g and kind == "cmp":
                    pe.wait_ge(s[f"cmp_in{g}"], 16 * N_SMALL_LOADS * (i + 1))
                at(pe, i, "probs", u - 2)
                if kind == "cmp":
                    for t in range(NT):
                        mm = nc.tensor.matmul(bank[:, 2 * slot, t * N_CMP:(t + 1) * N_CMP], qp[g][hp, pair, t * P:(t + 1) * P],
                                              kc[g][hp], start=True, stop=True)
                    mm.then_inc(s["scores"], 1)
                    return
                n = (t + 1) * P
                if t == 0:
                    pe.wait_ge(s["split"], 10 * i + (5 * g + 2 * pair + head + 2))
                for b in range(2):
                    q = q2[g][:, 2 * pair + head, t * P:n]
                    nc.tensor.matmul(bank[:, 2 * slot + b, 0:n], q, khi[g][:, b, 0:n], start=True, stop=False)
                    nc.tensor.matmul(bank[:, 2 * slot + b, 0:n], q, klo[g][:, b, 0:n], start=False, stop=False)
                    mm = nc.tensor.matmul(bank[:, 2 * slot + b, t * P:n], ident16[:], causal16[:], start=False, stop=True)
                mm.then_inc(s["scores"], 1)

            def turn(i, u):
                kind, g, pair, head, t = STEPS[u]
                at(pe, i, "copied_v", u - 1)
                at(pe, i, "copied_a", u - 1)
                if kind == "turn":
                    last = max(w for w in range(U) if STEPS[w] == ("main", g, pair, 1, NT - 1))
                    at(pe, i, "o", last)
                    for t in range(NT):
                        mm = nc.tensor.transpose(bank[:, 4, t * P:(t + 1) * P], osb[:, pair, t], core.ident[:])
                elif kind == "cmp":
                    at(pe, i, "probs", u)
                    for t in range(NT):
                        mm = nc.tensor.transpose(bank[0:N_CMP, 4, t * P:(t + 1) * P], probs[:, u % 2, 0, t * N_CMP:(t + 1) * N_CMP],
                                                 core.ident[:])
                else:
                    for b in range(2):
                        at(pe, i, "probs_sel" if b == 0 else "probs", u)
                        for j in range(t + 1):
                            mm = nc.tensor.transpose(bank[:, 4 + b, j * P:(j + 1) * P], probs[:, u % 2, b, j * P:(j + 1) * P],
                                                     core.ident[:])
                mm.then_inc(s["turned"], 1)

            def weigh(i, u):
                kind, g, pair, head, t = STEPS[u]
                if kind == "turn":
                    return
                if u == 0 or STEPS[u - 1][1] != g and kind == "cmp":
                    pe.wait_ge(s[f"v_in{g}"], 16 * N_SMALL_LOADS * (i + 1))
                at(pe, i, "copied_a", u)
                at(pe, i, "o", u - 2)
                if kind == "cmp":
                    for t in range(NT):
                        mm = nc.tensor.matmul(bank[:, 6 + u % 2, t * C:(t + 1) * C], pt[0:N_CMP, u % 2, 0, t * P:(t + 1) * P], vc[g][:],
                                              start=True, stop=True)
                else:
                    at(pe, i, "copied_v", u)
                    for b in range(2):
                        out = bank[:, 6 + u % 2, b * C:(b + 1) * C]
                        for j in range(t + 1):
                            mm = nc.tensor.matmul(out, pt[:, u % 2, b, j * P:(j + 1) * P], vv[g][:, b, j], start=(j == 0), stop=(j == t))
                mm.then_inc(s["o_mm"], 1)

            with pe.Fori(0, 2) as i:
                scores(i, 0)
                for u in range(U):
                    if u + 1 < U:
                        scores(i, u + 1)
                    if STEPS[u][0] == "turn":
                        weigh(i, u - 1)
                        turn(i, u)
                    else:
                        turn(i, u)
                        if u:
                            weigh(i, u - 1)

        @block.scalar
        def _(act):
            A = nc.scalar.activation
            credit(act, "probs_sel", "probs", "copied_a")
            act.wait_ge(s["gl"], 16)
            A(glog[:], glog[:], ACT.Sigmoid).then_inc(s["sig"], 1)

            def exps(i, u):
                kind, g, pair, head, t = STEPS[u]
                if kind == "turn":
                    return
                slot = u % 2
                at(act, i, "turned", u - 2)
                if kind == "cmp":
                    at(act, i, "nmax", u)
                    for t in range(NT):
                        a = A(probs[:, slot, 0, t * N_CMP:(t + 1) * N_CMP], masked[:, slot, t], ACT.Exp,
                              bias=nmax[:, slot, t:t + 1], accum_out=sums[:, u % 4, t:t + 1])
                else:
                    n = (t + 1) * P
                    for b in range(2):
                        at(act, i, "nmax_sel" if b == 0 else "nmax", u)
                        a = A(probs[:, slot, b, 0:n], bank[:, 2 * slot + b, 0:n], ACT.Exp, bias=nmax[:, slot, b:b + 1],
                              accum_out=sums[:, u % 4, b:b + 1])
                        if b == 0:
                            a.then_inc(s["probs_sel"], 1)
                a.then_inc(s["probs"], 1)

            def copy(i, u):
                kind, g, pair, head, t = STEPS[u]
                at(act, i, "turned", u)
                at(act, i, "o_mm", u - 2)
                if kind == "turn":
                    act.sem_inc(s["ready"], 1)
                    A(flat(yhi[:, one(4 * i + (2 * g + pair))]), bank[:, 4], ACT.Copy).then_inc(s["copied_a"], 1)
                elif kind == "cmp":
                    A(pt[0:N_CMP, u % 2, 0], bank[0:N_CMP, 4], ACT.Copy).then_inc(s["copied_a"], 1)
                else:
                    n = (t + 1) * P
                    A(pt[:, u % 2, 1, 0:n], bank[:, 5, 0:n], ACT.Copy).then_inc(s["copied_a"], 1)

            with act.Fori(0, 2) as i:
                for u in range(U + 1):
                    if u < U:
                        exps(i, u)
                    if u:
                        copy(i, u - 1)

        def split_group(eng, unit, n):
            g = n % 2
            eng.wait_ge(s[f"in{g}"], 16 * N_LOADS * (n // 2 + 1))
            if n:
                eng.wait_ge(s["split"], 5 * n)
            unit.tensor_copy(khi[g][:], kk[g][:]).then_inc(s["rounded"], 1)
            eng.wait_ge(s["rounded"], 5 * n + 1)
            unit.tensor_tensor(klo[g][:], kk[g][:], fp(khi[g][:]), ALU.subtract).then_inc(s["split"], 1)
            for h in range(4):
                eng.wait_ge(s["split"], 5 * n + h + 1)
                unit.tensor_copy(q2[g][:, h], qr[g][:, h]).then_inc(s["rounded"], 1)
                eng.wait_ge(s["rounded"], 5 * n + h + 2)
                unit.tensor_tensor(q2[g][C:P, h], qr[g][C:P, h], fp(q2[g][C:P, h]), ALU.subtract).then_inc(s["split"], 1)

        @block.gpsimd
        def _(pool):
            for n in range(1, 4):
                split_group(pool, nc.gpsimd, n)

        @block.vector
        def _(dve):
            V = nc.vector
            dve.wait_ge(s["consts"], 48)
            V.tensor_copy(ident16[:], core.ident[:])
            V.tensor_copy(causal16[:], causal[:])
            dve.wait_ge(s["gt"], 1)
            V.tensor_copy(gates[:], bank[:, 6, 0:NT * 48].rearrange("p (t g) -> p t g", t=NT)).then_inc(s["gates"], 1)
            dve.wait_ge(s["gates"], 1)
            V.tensor_scalar(gates[:, 0, 0::3], gates[:, 0, 0::3], has_block[:, 0:1], None, ALU.mult).then_inc(s["gates"], 1)
            dve.wait_ge(s["gates"], 2)
            split_group(dve, V, 0)
            credit(dve, "nmax_sel", "masked", "nmax", "copied_v", "recip", "coef", "o_sel", "o")

            def maxima(i, u):
                kind, g, pair, head, t = STEPS[u]
                if kind == "turn":
                    return
                slot = u % 2
                at(dve, i, "scores", u)
                if kind == "cmp":
                    V.tensor_tensor(masked[:, slot], bank[:, 2 * slot, 0:NT * N_CMP].rearrange("p (t n) -> p t n", t=NT),
                                    cmp_neg[:], ALU.add).then_inc(s["masked"], 1)
                    at(dve, i, "masked", u)
                    V.reduce_max(nmax[:, slot], masked[:, slot], axis=AX.X, negate=True).then_inc(s["nmax"], 1)
                else:
                    for b in range(2):
                        V.reduce_max(nmax[:, slot, b:b + 1], bank[:, 2 * slot + b, 0:(t + 1) * P], axis=AX.X,
                                     negate=True).then_inc(s["nmax_sel" if b == 0 else "nmax"], 1)

            def copy(i, u):
                kind, g, pair, head, t = STEPS[u]
                if kind == "turn":
                    at(dve, i, "copied_a", u)
                    pi = one(4 * i + (2 * g + pair))
                    V.tensor_tensor(flat(ylo[:, pi]), bank[:, 4], flat(fp(yhi[:, pi])), ALU.subtract).then_inc(s["copied_v"], 1)
                elif kind == "main":
                    at(dve, i, "turned", u)
                    at(dve, i, "o_mm", u - 2)
                    n = (t + 1) * P
                    V.tensor_copy(pt[:, u % 2, 0, 0:n], bank[:, 4, 0:n]).then_inc(s["copied_v"], 1)

            def reciprocals(i, u):
                kind, g, pair, head, t = STEPS[u]
                if kind != "turn":
                    m = NT if kind == "cmp" else 2
                    at(dve, i, "probs", u)
                    V.reciprocal(rcp[:, u % 4, 0:m], sums[:, u % 4, 0:m]).then_inc(s["recip"], 1)

            def coefficients(i, u):
                kind, g, pair, head, t = STEPS[u]
                if kind != "turn":
                    m = NT if kind == "cmp" else 2
                    h3 = 24 * i + (12 * g + 6 * pair + 3 * head)
                    gate = gates[:, :, one(h3)].rearrange("p t a -> p (t a)") if kind == "cmp" else gates[:, t, bass.ds(h3 + 1, 2)]
                    at(dve, i, "recip", u)
                    V.tensor_tensor(coef[:, u % 4, 0:m], rcp[:, u % 4, 0:m], gate, ALU.mult).then_inc(s["coef"], 1)

            def combine(i, u):
                kind, g, pair, head, t = STEPS[u]
                if kind == "turn":
                    return
                c = coef[:, u % 4]
                at(dve, i, "o_mm", u)
                at(dve, i, "o", u - 1)
                at(dve, i, "coef", u)
                if kind == "cmp":
                    V.tensor_tensor(osb[:, pair, :, C * head:C * head + C], bank[:, 6 + u % 2, 0:NT * C].rearrange("p (t d) -> p t d", t=NT),
                                    c.rearrange("p (t a) -> p t a", a=1).to_broadcast([P, NT, C]), ALU.mult).then_inc(s["o"], 1)
                    return
                o = osb[:, pair, t, C * head:C * head + C]
                V.scalar_tensor_tensor(out=o, in0=bank[:, 6 + u % 2, 0:C], scalar=c[:, 0:1], in1=o,
                                       op0=ALU.mult, op1=ALU.add).then_inc(s["o_sel"], 1)
                at(dve, i, "o_sel", u)
                V.scalar_tensor_tensor(out=o, in0=bank[:, 6 + u % 2, C:2 * C], scalar=c[:, 1:2], in1=o,
                                       op0=ALU.mult, op1=ALU.add).then_inc(s["o"], 1)

            with dve.Fori(0, 2) as i:
                for u in range(U + 2):
                    if u < U:
                        maxima(i, u)
                    late = 1 <= u <= U and STEPS[u - 1][0] == "turn"
                    if 1 <= u <= U:
                        reciprocals(i, u - 1)
                    if 1 <= u <= U and not late:
                        copy(i, u - 1)
                    if 1 <= u <= U:
                        coefficients(i, u - 1)
                    if u >= 2:
                        combine(i, u - 2)
                    if late:
                        copy(i, u - 1)
    close_stage(core, s)


def setup(core, ahead):
    nc, ins = core.nc, core.ins
    with ExitStack() as ctx:
        s, sb, ps = open_stage(core, ctx, "setup", ["const", "rows", "x", "turned", "copied", "filled"])
        nt = T // P
        tok = sb("tok", [P, nt, D])
        rows = sb("rows", [P, 2, P])
        turn = ps("turn", [P, 4, T])
        rest = core.rows - P
        block = ctx.enter_context(nc.Block())

        @block.sync
        def _(sp):
            sp.dma_start(core.ident[:], core.consts["c_ident"]).then_inc(s["const"], 16)
            sp.dma_start(core.head_ones[:], core.consts["c_head_ones"]).then_inc(s["const"], 16)
            for name in VECTORS:
                n = int(np.prod(ins[name].shape)) // P
                r = core.row[name]
                shape = ins[name].shape
                src = ins[name]
                axes = " ".join("abcd"[:len(shape)])
                src = src.rearrange(f"{axes} -> ({axes})") if len(shape) > 1 else src
                src = src.rearrange("(r p) -> r p", p=P)
                for tile in range(2):
                    lo, hi = max(r, tile * P), min(r + n, tile * P + P)
                    if lo < hi:
                        sp.dma_start(rows[lo - tile * P:hi - tile * P, tile], src[lo - r:hi - r]).then_inc(s["rows"], 16)
            load_ahead(sp, core, ahead)
            core.row_loads = sum(1 + (core.row[v] < P < core.row[v] + int(np.prod(ins[v].shape)) // P) for v in VECTORS)

        @block.scalar
        def _(act):
            for t in range(nt):
                act.dma_start(tok[:, t], ins["x"].rearrange("b (t p) d -> t p (b d)", p=P)[t]).then_inc(s["x"], 16)
            for d in range(ND):
                act.wait_ge(s["turned"], d + 1)
                nc.scalar.activation(core.x[:, d], turn[:, d % 4], ACT.Copy).then_inc(s["copied"], 1)
            for tile, n in enumerate((P, rest)):
                act.wait_ge(s["turned"], ND + tile + 1)
                nc.scalar.activation(core.vecs[:, tile * P:tile * P + n], turn[:, tile, 0:n], ACT.Copy).then_inc(s["copied"], 1)

        @block.vector
        def _(dve):
            nc.vector.memset(core.ones[:], 1.0)
            nc.vector.memset(core.eps[:, 0:1], EPS)
            nc.vector.memset(core.eps[:, 1:2], GN_EPS)
            nc.vector.memset(core.zero[:], 0.0).then_inc(s["filled"], 1)

        @block.tensor
        def _(pe):
            pe.wait_ge(s["const"], 32)
            pe.wait_ge(s["x"], 16 * nt)
            for d in range(ND):
                if d >= 4:
                    pe.wait_ge(s["copied"], d - 3)
                for t in range(nt):
                    mm = nc.tensor.transpose(turn[:, d % 4, t * P:(t + 1) * P], tok[:, t, d * P:(d + 1) * P], core.ident[:])
                mm.then_inc(s["turned"], 1)
            pe.wait_ge(s["rows"], 16 * core.row_loads)
            for tile, n in enumerate((P, rest)):
                pe.wait_ge(s["copied"], ND - 3 + tile)
                nc.tensor.transpose(turn[:, tile, 0:n], rows[0:n, tile], core.ident[0:n, 0:n]).then_inc(s["turned"], 1)
    close_stage(core, s)


def finish(core, out):
    nc = core.nc
    with ExitStack() as ctx:
        s, sb, ps = open_stage(core, ctx, "finish", ["turned", "copied", "out"])
        nt = T // P
        tok = sb("tok", [P, nt, D])
        turn = ps("turn", [P, 4, T])
        block = ctx.enter_context(nc.Block())
        steps = [(t, q) for t in range(nt) for q in range(2)]

        @block.tensor
        def _(pe):
            for n, (t, q) in enumerate(steps):
                if n >= 4:
                    pe.wait_ge(s["copied"], n - 3)
                for j in range(4):
                    mm = nc.tensor.transpose(turn[:, n % 4, j * P:(j + 1) * P],
                                             core.x[:, 4 * q + j, t * P:(t + 1) * P], core.ident[:])
                mm.then_inc(s["turned"], 1)

        @block.scalar
        def _(act):
            for n, (t, q) in enumerate(steps):
                act.wait_ge(s["turned"], n + 1)
                nc.scalar.activation(tok[:, t, q * T:(q + 1) * T], turn[:, n % 4], ACT.Copy).then_inc(s["copied"], 1)

        @block.sync
        def _(sp):
            dst = out.rearrange("b (t p) d -> t p (b d)", p=P)
            for t in range(nt):
                sp.wait_ge(s["copied"], 2 * t + 2)
                sp.dma_start(dst[t], tok[:, t]).then_inc(s["out"], 16)
            sp.wait_ge(s["out"], 16 * nt)


def program(nc, ins, consts, out):
    with ExitStack() as ctx:
        core = Core(nc, ctx, ins, consts)
        scratch = lambda name, *shape: nc.dram_tensor(name, shape, F32).ap()
        weights = lambda n, layer: (ins[f"ffn{n}_w_gate"][layer], ins[f"ffn{n}_w_up"][layer])
        half_ffn = lambda n, layer, ahead: ffn(core, f"ffn{n}_{layer}", core.vec(f"norm_ffn{n}", layer), *weights(n, layer),
                                               ins[f"ffn{n}_w_down"][layer], ahead)
        setup(core, ffn_first_units(*weights(1, 0)))
        half_ffn(1, 0, first_units(ins["rw_w_rkv"][0, 0]))
        rkv = scratch("rkv_scratch", 3, D, T)
        with ExitStack() as mixing:
            hold = lambda name, shape, dt=F32: mixing.enter_context(nc.sbuf_tensor(name, shape, dt))
            lora = {n: hold(f"lora_{n}", [P, c, T]) for n, c in (("lw", 1), ("la", 1), ("lg", 2))}
            mix_project(core, "mix", rkv, lora)
            yhi, ylo = hold("y_hi", [P, ND, T], F32R), hold("y_lo", [P, ND, T], F32R)
            recurrence(core, "rec", rkv, lora, yhi, ylo)
            project_add(core, "rwo", yhi, ylo, ins["rw_w_o"][0], ffn_first_units(*weights(2, 0)))
        half_ffn(2, 0, first_units(ins["kv_w"]))
        shared = {"kv": scratch("kv_scratch", 6 * KIND, T), "k_rot": scratch("k_rot_scratch", 2 * KIND, T),
                  "v_tok": scratch("v_tok_scratch", 4, P, T), "k_cmp": scratch("k_cmp_scratch", C, G * N_CMP),
                  "v_cmp": scratch("v_cmp_scratch", G * N_CMP, C)}
        shared_kv(core, **shared, ahead=ffn_first_units(*weights(1, 1)))
        half_ffn(1, 1, first_units(ins["nsa_w_q"][0]))
        with ExitStack() as mixing:
            hold = lambda name, shape, dt=F32: mixing.enter_context(nc.sbuf_tensor(name, shape, dt))
            gate_logits, q_plain, q_rot = scratch("gate_scratch", 48, T), scratch("q_plain_scratch", D, T), scratch("q_rot_scratch", D, T)
            queries(core, "q", core.vec("norm_mix", 1), ins["nsa_w_q"][0], ins["nsa_q_norm"][0], q_rot, q_plain, gate_logits,
                    first_units(ins["nsa_w_o"][0]))
            yhi, ylo = hold("o_hi", [P, ND, T], F32R), hold("o_lo", [P, ND, T], F32R)
            attention(core, "att", q_plain, q_rot, gate_logits, shared["k_rot"], shared["v_tok"], shared["k_cmp"], shared["v_cmp"], yhi, ylo)
            project_add(core, "nwo", yhi, ylo, ins["nsa_w_o"][0], ffn_first_units(*weights(2, 1)))
        half_ffn(2, 1, [])
        finish(core, out)


def constants():
    head = np.kron(np.eye(2), np.ones((64, 64)))
    a, b = np.arange(P)[:, None], np.arange(P)[None, :]
    same = a // C == b // C
    between = lambda n: (a // (2 * n) == b // (2 * n)) & ((a // n) % 2 == 1) & ((b // n) % 2 == 0)
    tables = {
        "c_ident": np.eye(P), "c_head_ones": head,
        "c_masks": np.stack([same & (a < b), same & (a <= b)], 1),
        "c_merge": np.stack([between(n) for n in LEVELS], 1),
        "c_first": np.stack([between(1), between(1).T], 1),
        "c_i64": a % C == np.arange(C)[None, :],
    }
    half = C // 2
    rate = (10000.0 ** (-np.arange(half) / half)).astype(np.float32)
    angle = (np.arange(T, dtype=np.float32)[None, :] * rate[:, None]).astype(np.float64)
    t, n = np.arange(T).reshape(NT, P).T[:, :, None], np.arange(N_CMP)[None, None, :]
    tables["c_causal"] = np.where(b > a, -1e30, 0.0)
    tables["c_cmp_neg"] = np.where(CMP_STRIDE * n + CMP_LEN - 1 > t, -1e30, 0.0)
    tables["c_has_block"] = (np.arange(P)[:, None] >= CMP_LEN - 1)
    tables["c_cos"] = np.tile(np.cos(angle), (4, 1))
    tables["c_sin"] = np.tile(np.concatenate([-np.sin(angle), np.sin(angle)]), (2, 1))
    tables["c_swap"] = (a // C == b // C) & ((a - b) % C == half)
    return {n: np.ascontiguousarray(t).astype(np.float32) for n, t in tables.items()}


_INS = ['x', 'norm_ffn1', 'ffn1_w_gate', 'ffn1_w_up', 'ffn1_w_down', 'norm_mix', 'norm_ffn2', 'ffn2_w_gate',
        'ffn2_w_up', 'ffn2_w_down', 'rw_mu', 'rw_w_rkv', 'rw_w0', 'rw_w_lora_a', 'rw_w_lora_b', 'rw_a0',
        'rw_a_lora_a', 'rw_a_lora_b', 'rw_g_lora_a', 'rw_g_lora_b', 'rw_k_k', 'rw_k_a', 'rw_r_k', 'rw_gn_w',
        'rw_gn_b', 'rw_w_o', 'kv_norm', 'kv_w', 'kv_k_norm', 'cmp_pos_k', 'cmp_k_w1', 'cmp_k_w2', 'cmp_pos_v',
        'cmp_v_w1', 'cmp_v_w2', 'nsa_w_q', 'nsa_q_norm', 'nsa_w_o']


def kernel(**inputs):
    import concourse.bacc as _bacc
    from concourse.bass_utils import run_bass_kernel_spmd as _run

    nc = _bacc.Bacc("TRN2", target_bir_lowering=False, num_devices=1)
    arrays = {f"in_{n}_dram": np.ascontiguousarray(inputs[n]) for n in _INS}
    arrays.update({f"in_{n}_dram": a for n, a in constants().items()})
    aps = {n[3:-5]: nc.dram_tensor(n, a.shape, mybir.dt.from_np(a.dtype), kind="ExternalInput").ap()
           for n, a in arrays.items()}
    out = nc.dram_tensor("out_0_dram", (1, T, D), F32, kind="ExternalOutput").ap()
    program(nc, {n: aps[n] for n in _INS}, {n: aps[n] for n in constants()}, out)
    r = _run(nc, [arrays], core_ids=[0])
    return r.results[0]["out_0_dram"]
```
